# Optimizing a Trainium2 kernel written in Bass

```python
import math
import jax, jax.numpy as jnp
from jax import lax
import numpy as np

D_MODEL = 1024
BATCH = 1
SEQ = 512
DEPTH = 2

CHUNK = 64
N_META = 16
Q_BLOCK = 128
DIFF_HEADS = 4
DIFF_HEAD_DIM = 64
DIFF_V_DIM = 2 * DIFF_HEAD_DIM
FOX_HEADS = 8
FOX_HEAD_DIM = 64
DIFF_QK_W = DIFF_HEADS * 2 * DIFF_HEAD_DIM
DIFF_V_W = DIFF_HEADS * DIFF_V_DIM
FOX_W = FOX_HEADS * FOX_HEAD_DIM
EVEN_IN_W = 2 * DIFF_QK_W + DIFF_V_W + 3 * FOX_W + FOX_HEADS
EVEN_MIX_W = DIFF_V_W + FOX_W
RET_HEADS = 4
RET_QK_DIM = D_MODEL // RET_HEADS
RET_V_DIM = 2 * RET_QK_DIM
RET_QK_W = RET_HEADS * RET_QK_DIM
RET_V_W = RET_HEADS * RET_V_DIM
RET_IN_W = 2 * RET_QK_W + 2 * RET_V_W
D_FF = 4 * D_MODEL
N_EVEN = (DEPTH + 1) // 2
N_ODD = DEPTH // 2
DEEPNORM_ALPHA = (2 * DEPTH) ** 0.25
DEEPNORM_BETA = (8 * DEPTH) ** -0.25
LN_EPS = 1e-5
RMS_EPS = 1e-6


F32 = jnp.float32

def _chunk_id(pos):
    return (pos + CHUNK - N_META) // CHUNK

def _layer_norm(x, g, b):
    xf = x.astype(F32)
    mu = jnp.mean(xf, axis=-1, keepdims=True)
    var = jnp.mean(jnp.square(xf - mu), axis=-1, keepdims=True)
    y = (xf - mu) * lax.rsqrt(var + LN_EPS)
    return (y * g.astype(F32) + b.astype(F32)).astype(x.dtype)

def _rms_norm(x):
    xf = x.astype(F32)
    return xf * lax.rsqrt(jnp.mean(jnp.square(xf), axis=-1, keepdims=True) + RMS_EPS)

def _even_mixer(h, w_in, f_bias, lam_vecs, subln_g, w_out, layer_idx):
    B, L, _ = h.shape
    Lp = -(-L // Q_BLOCK) * Q_BLOCK
    nblk = Lp // Q_BLOCK
    proj = h @ w_in
    offs = [int(o) for o in np.cumsum([DIFF_QK_W, DIFF_QK_W, DIFF_V_W, FOX_W, FOX_W, FOX_W])]
    qa, ka, va, qb, kb, vb, fb = jnp.split(proj, offs, axis=-1)
    pad = ((0, 0), (0, Lp - L), (0, 0))
    qa, ka, va, qb, kb, vb = (jnp.pad(t, pad) for t in (qa, ka, va, qb, kb, vb))
    log_f = jnp.pad(jax.nn.log_sigmoid((fb + f_bias).astype(F32)), pad)
    cum_f = jnp.cumsum(log_f, axis=1).transpose(0, 2, 1)

    qa = qa.reshape(B, nblk, Q_BLOCK, DIFF_HEADS, 2, DIFF_HEAD_DIM).transpose(1, 0, 3, 4, 2, 5)
    ka = ka.reshape(B, Lp, DIFF_HEADS, 2, DIFF_HEAD_DIM).transpose(0, 2, 3, 1, 4)
    va = va.reshape(B, Lp, DIFF_HEADS, DIFF_V_DIM).transpose(0, 2, 1, 3)
    qb = qb.reshape(B, nblk, Q_BLOCK, FOX_HEADS, FOX_HEAD_DIM).transpose(1, 0, 3, 2, 4)
    kb = kb.reshape(B, Lp, FOX_HEADS, FOX_HEAD_DIM).transpose(0, 2, 1, 3)
    vb = vb.reshape(B, Lp, FOX_HEADS, FOX_HEAD_DIM).transpose(0, 2, 1, 3)
    cq = cum_f.reshape(B, FOX_HEADS, nblk, Q_BLOCK).transpose(2, 0, 1, 3)

    lam_init = 0.8 - 0.6 * math.exp(-0.3 * layer_idx)
    lv = lam_vecs.astype(F32)
    lam = jnp.exp(jnp.sum(lv[0] * lv[1])) - jnp.exp(jnp.sum(lv[2] * lv[3])) + lam_init
    slopes = 2.0 ** (-8.0 * jnp.arange(1, DIFF_HEADS + 1, dtype=F32) / DIFF_HEADS)
    scale_a = DIFF_HEAD_DIM ** -0.5
    scale_b = FOX_HEAD_DIM ** -0.5
    k_pos = jnp.arange(Lp)
    k_chunk = _chunk_id(k_pos)
    q_pos_blk = k_pos.reshape(nblk, Q_BLOCK)

    def one_block(args):
        qa_i, qb_i, cq_i, q_pos = args
        dist = jnp.abs(q_pos[:, None] - k_pos[None, :]).astype(F32)
        chunk_vis = k_chunk[None, :] <= _chunk_id(q_pos)[:, None]
        frame_vis = k_pos[None, :] <= q_pos[:, None]
        s_a = jnp.einsum('bhmqd,bhmkd->bhmqk', qa_i, ka).astype(F32) * scale_a \
            - slopes[:, None, None, None] * dist
        p_a = jax.nn.softmax(jnp.where(chunk_vis, s_a, -jnp.inf), axis=-1)
        p_diff = p_a[:, :, 0] - lam * p_a[:, :, 1]
        o_a = jnp.einsum('bhqk,bhkd->bhqd', p_diff.astype(va.dtype), va)
        s_b = jnp.einsum('bhqd,bhkd->bhqk', qb_i, kb).astype(F32) * scale_b \
            + cq_i[..., :, None] - cum_f[:, :, None, :]
        p_b = jax.nn.softmax(jnp.where(frame_vis, s_b, -jnp.inf), axis=-1)
        o_b = jnp.einsum('bhqk,bhkd->bhqd', p_b.astype(vb.dtype), vb)
        return o_a, o_b

    o_a, o_b = lax.map(one_block, (qa, qb, cq, q_pos_blk))
    o_a = o_a.transpose(1, 0, 3, 2, 4).reshape(B, Lp, DIFF_HEADS, DIFF_V_DIM)[:, :L]
    o_a = (_rms_norm(o_a) * subln_g.astype(F32) * (1.0 - lam_init)).astype(h.dtype)
    o_b = o_b.transpose(1, 0, 3, 2, 4).reshape(B, Lp, FOX_W)[:, :L]
    o = jnp.concatenate([o_a.reshape(B, L, DIFF_V_W), o_b.astype(h.dtype)], axis=-1)
    return o @ w_out

def _retention(h, w_in, w_out):
    B, L, _ = h.shape
    proj = h @ w_in
    q, k, v, g = jnp.split(proj, [RET_QK_W, 2 * RET_QK_W, 2 * RET_QK_W + RET_V_W], axis=-1)
    k = k * RET_QK_DIM ** -0.5
    lpad = (-N_META) % CHUNK
    Lr = L + lpad
    nc = Lr // CHUNK

    def to_chunks(t, d):
        t = jnp.pad(t, ((0, 0), (lpad, 0), (0, 0)))
        return t.reshape(B, nc, CHUNK, RET_HEADS, d).transpose(1, 0, 3, 2, 4)

    qc, kc, vc = to_chunks(q, RET_QK_DIM), to_chunks(k, RET_QK_DIM), to_chunks(v, RET_V_DIM)
    log_gamma = jnp.log1p(-(2.0 ** (-5.0 - jnp.arange(RET_HEADS, dtype=F32))))
    idx = jnp.arange(CHUNK, dtype=F32)
    intra = jnp.exp(log_gamma[:, None, None] * jnp.abs(idx[:, None] - idx[None, :]))
    q_dec = jnp.exp(log_gamma[:, None] * (idx + 1.0))[:, :, None]
    k_dec = jnp.exp(log_gamma[:, None] * (CHUNK - 1.0 - idx))[:, :, None]
    c_dec = jnp.exp(log_gamma * CHUNK)[:, None, None]

    def step(state, inp):
        q_i, k_i, v_i = inp
        scores = jnp.einsum('bhid,bhjd->bhij', q_i, k_i) * intra
        o = jnp.einsum('bhij,bhje->bhie', scores, v_i) \
            + jnp.einsum('bhid,bhde->bhie', q_i * q_dec, state)
        state = c_dec * state + jnp.einsum('bhjd,bhje->bhde', k_i * k_dec, v_i)
        return state, o

    s0 = jnp.zeros((B, RET_HEADS, RET_QK_DIM, RET_V_DIM), F32)
    _, o = lax.scan(step, s0, (qc, kc, vc))
    o = o.transpose(1, 0, 3, 2, 4).reshape(B, Lr, RET_HEADS, RET_V_DIM)[:, lpad:]
    o = _rms_norm(o).reshape(B, L, RET_V_W).astype(h.dtype)
    y = jax.nn.silu(g) * o
    return y @ w_out

def _sq_relu_mlp(h, w1, w2):
    return jnp.square(jax.nn.relu(h @ w1)) @ w2

def first_inputs(seed: int = 0) -> dict:
    key = jax.random.key(seed)
    ks = jax.random.split(key, 13)

    def nrm(k, shape, scale):
        return jax.random.normal(k, shape, F32) * scale

    beta = DEEPNORM_BETA
    x = nrm(ks[0], (BATCH, SEQ, D_MODEL), 1.0)
    meta_tokens = nrm(ks[1], (N_META, D_MODEL), 1.0)
    even_col_scale = jnp.concatenate([
        jnp.ones((2 * DIFF_QK_W,), F32), jnp.full((DIFF_V_W,), beta, F32),
        jnp.ones((2 * FOX_W,), F32), jnp.full((FOX_W,), beta, F32),
        jnp.ones((FOX_HEADS,), F32)])
    even_w_in = nrm(ks[2], (N_EVEN, D_MODEL, EVEN_IN_W), D_MODEL ** -0.5) * even_col_scale
    even_f_bias = jnp.linspace(1.0, 6.0, FOX_HEADS, dtype=F32) + nrm(ks[3], (N_EVEN, FOX_HEADS), 0.1)
    diff_lambda = nrm(ks[4], (N_EVEN, 4, DIFF_HEAD_DIM), 0.1)
    diff_subln_g = 1.0 + nrm(ks[5], (N_EVEN, DIFF_V_DIM), 0.02)
    even_w_out = nrm(ks[6], (N_EVEN, EVEN_MIX_W, D_MODEL), EVEN_MIX_W ** -0.5 * beta)
    ret_col_scale = jnp.concatenate([
        jnp.ones((2 * RET_QK_W,), F32), jnp.full((RET_V_W,), beta, F32), jnp.ones((RET_V_W,), F32)])
    ret_w_in = nrm(ks[7], (N_ODD, D_MODEL, RET_IN_W), D_MODEL ** -0.5) * ret_col_scale
    ret_w_out = nrm(ks[8], (N_ODD, RET_V_W, D_MODEL), RET_V_W ** -0.5 * beta)
    ln_g = 1.0 + nrm(ks[9], (DEPTH, 2, D_MODEL), 0.02)
    ln_b = nrm(ks[10], (DEPTH, 2, D_MODEL), 0.02)
    ffn_w1 = nrm(ks[11], (DEPTH, D_MODEL, D_FF), D_MODEL ** -0.5 * beta)
    ffn_w2 = nrm(ks[12], (DEPTH, D_FF, D_MODEL), D_FF ** -0.5 * beta)
    return {"x": x, "meta_tokens": meta_tokens, "even_w_in": even_w_in, "even_f_bias": even_f_bias,
            "diff_lambda": diff_lambda, "diff_subln_g": diff_subln_g, "even_w_out": even_w_out,
            "ret_w_in": ret_w_in, "ret_w_out": ret_w_out, "ln_g": ln_g, "ln_b": ln_b,
            "ffn_w1": ffn_w1, "ffn_w2": ffn_w2}

def first_block(x, meta_tokens, even_w_in, even_f_bias, diff_lambda, diff_subln_g, even_w_out,
              ret_w_in, ret_w_out, ln_g, ln_b, ffn_w1, ffn_w2):
    B = x.shape[0]
    meta = jnp.broadcast_to(meta_tokens[None].astype(x.dtype), (B, N_META, D_MODEL))
    h = jnp.concatenate([meta, x], axis=1)
    for layer in range(DEPTH):
        i = layer // 2
        if layer % 2 == 0:
            mix = _even_mixer(h, even_w_in[i], even_f_bias[i], diff_lambda[i], diff_subln_g[i],
                              even_w_out[i], layer)
        else:
            mix = _retention(h, ret_w_in[i], ret_w_out[i])
        h = _layer_norm(DEEPNORM_ALPHA * h + mix, ln_g[layer, 0], ln_b[layer, 0])
        h = _layer_norm(DEEPNORM_ALPHA * h + _sq_relu_mlp(h, ffn_w1[layer], ffn_w2[layer]),
                        ln_g[layer, 1], ln_b[layer, 1])
    return h[:, N_META:, :]


DEPTH_2 = 1

ATT_HEADS = 16
ATT_HEAD_DIM = 64
KV_LATENT = 128
IDX_HEADS = 8
IDX_DIM = 64
TOPK_MAX = 256
REL_BUCKETS = 32
REL_MAX_DIST = 128
SSM_INNER = 2 * D_MODEL
SSM_HEAD_DIM = 64
SSM_HEADS = SSM_INNER // SSM_HEAD_DIM
SSM_GROUPS = 4
SSM_HEADS_PER_GROUP = SSM_HEADS // SSM_GROUPS
SSM_STATE = 128
SSM_CONV = 4
SSM_CHUNK = 128
SSM_XBC = SSM_INNER + 2 * SSM_GROUPS * SSM_STATE
FFN_DIM = 2816
FFN_CONV = 3
EPS = 1e-6

IN_SPLITS = (
    ATT_HEADS * ATT_HEAD_DIM,
    KV_LATENT,
    IDX_HEADS * IDX_DIM,
    IDX_DIM,
    IDX_HEADS,
    SSM_INNER,
    SSM_XBC,
    SSM_HEADS,
    D_MODEL,
    D_MODEL,
)
IN_COLS = sum(IN_SPLITS)


def split_cols(a, sizes):
    idx, acc = [], 0
    for sz in sizes[:-1]:
        acc += sz
        idx.append(acc)
    return jnp.split(a, idx, axis=-1)

def rmsnorm(x, g):
    x32 = x.astype(jnp.float32)
    y = x32 * lax.rsqrt(jnp.mean(x32 * x32, axis=-1, keepdims=True) + EPS)
    return (y * g.astype(jnp.float32)).astype(x.dtype)

def causal_depthwise_conv(u, w, bias):
    k, ch = w.shape
    out = lax.conv_general_dilated(
        u, w[:, None, :].astype(u.dtype), window_strides=(1,), padding=[(k - 1, 0)],
        dimension_numbers=("NWC", "WIO", "NWC"), feature_group_count=ch)
    return out + bias.astype(u.dtype)

def t5_bucket(dist):
    n = jnp.maximum(dist, 0)
    max_exact = REL_BUCKETS // 2
    large = max_exact + (jnp.log(jnp.maximum(n, 1).astype(jnp.float32) / max_exact)
                         / math.log(REL_MAX_DIST / max_exact)
                         * (REL_BUCKETS - max_exact)).astype(jnp.int32)
    large = jnp.minimum(large, REL_BUCKETS - 1)
    return jnp.where(n < max_exact, n, large)

def dsa_attention(q_lat, c_kv, q_idx, k_idx, w_idx, rel_bias):
    b, s, h, c = q_lat.shape
    n_sel = min(TOPK_MAX, s // 4)
    nblk = s // Q_BLOCK
    scale = ATT_HEAD_DIM ** -0.5
    key_pos = jnp.arange(s)
    gather = jax.vmap(lambda table, idx: table[idx])

    def to_blocks(a):
        return a.reshape(b, nblk, Q_BLOCK, *a.shape[2:]).swapaxes(0, 1)

    def block(args):
        qb, qib, wib, blk = args
        q_pos = blk * Q_BLOCK + jnp.arange(Q_BLOCK)
        causal = key_pos[None, :] <= q_pos[:, None]
        idx_logits = jnp.einsum("bqhd,bsd->bqhs", qib, k_idx,
                                preferred_element_type=jnp.float32)
        score = jnp.einsum("bqhs,bqh->bqs", jax.nn.relu(idx_logits),
                           wib.astype(jnp.float32))
        score = jnp.where(causal[None], score, -jnp.inf)
        _, sel = lax.top_k(score, n_sel)
        c_sel = gather(c_kv, sel)
        logits = jnp.einsum("bqhc,bqkc->bhqk", qb, c_sel,
                            preferred_element_type=jnp.float32) * scale
        dist = q_pos[None, :, None] - sel
        bias = rel_bias[t5_bucket(dist)]
        logits = logits + jnp.moveaxis(bias, -1, 1).astype(jnp.float32)
        logits = jnp.where((dist >= 0)[:, None], logits, -jnp.inf)
        p = jax.nn.softmax(logits, axis=-1).astype(c_sel.dtype)
        return jnp.einsum("bhqk,bqkc->bqhc", p, c_sel)

    out = lax.map(block, (to_blocks(q_lat), to_blocks(q_idx), to_blocks(w_idx),
                          jnp.arange(nblk)))
    return out.swapaxes(0, 1).reshape(b, s, h, c)

def ssd_scan(xh, dt, a, bmat, cmat):
    b, l, g, r, p = xh.shape
    n = bmat.shape[-1]
    q = SSM_CHUNK
    nc = l // q
    f32 = jnp.float32
    x = (xh.astype(f32) * dt[..., None]).reshape(b, nc, q, g, r, p)
    adt = (dt * a).reshape(b, nc, q, g, r)
    bm = bmat.astype(f32).reshape(b, nc, q, g, n)
    cm = cmat.astype(f32).reshape(b, nc, q, g, n)
    a_cum = jnp.cumsum(adt, axis=2)
    tri = jnp.tril(jnp.ones((q, q), dtype=bool))
    seg = a_cum[:, :, :, None] - a_cum[:, :, None, :]
    decay = jnp.exp(jnp.where(tri[None, None, :, :, None, None], seg, -jnp.inf))
    cb = jnp.einsum("bclgn,bcsgn->bclsg", cm, bm)
    y_diag = jnp.einsum("bclsgr,bcsgrp->bclgrp", cb[..., None] * decay, x)
    decay_states = jnp.exp(a_cum[:, :, -1:] - a_cum)
    states = jnp.einsum("bclgn,bclgrp->bcgrpn", bm, x * decay_states[..., None])
    chunk_decay = jnp.exp(a_cum[:, :, -1])

    def step(hstate, inp):
        st, dec = inp
        return hstate * dec[..., None, None] + st, hstate

    h0 = jnp.zeros((b, g, r, p, n), f32)
    _, prev = lax.scan(step, h0, (states.swapaxes(0, 1), chunk_decay.swapaxes(0, 1)))
    prev = prev.swapaxes(0, 1)
    y_off = jnp.einsum("bclgn,bcgrpn->bclgrp", cm, prev) * jnp.exp(a_cum)[..., None]
    return (y_diag + y_off).reshape(b, l, g, r, p)

def gated_group_rmsnorm(y, z, g):
    u = y.astype(jnp.float32) * jax.nn.silu(z.astype(jnp.float32))
    b, l, c = u.shape
    u = u.reshape(b, l, SSM_GROUPS, c // SSM_GROUPS)
    u = u * lax.rsqrt(jnp.mean(u * u, axis=-1, keepdims=True) + EPS)
    return (u.reshape(b, l, c) * g.astype(jnp.float32)).astype(z.dtype)

def second_inputs(seed: int = 0) -> dict:
    key = jax.random.key(seed)
    ks = jax.random.split(key, 24)
    f32 = jnp.float32

    def nrm(k, shape, scale):
        return jax.random.normal(k, shape, f32) * scale

    def gain(k, shape):
        return 1.0 + 0.05 * jax.random.normal(k, shape, f32)

    dt0 = jnp.exp(jax.random.uniform(ks[8], (DEPTH_2, SSM_HEADS), f32,
                                     math.log(1e-3), math.log(1e-1)))
    dt_bias = dt0 + jnp.log(-jnp.expm1(-dt0))
    return {
        "x": nrm(ks[0], (BATCH, SEQ, D_MODEL), 1.0),
        "rel_bias": nrm(ks[1], (REL_BUCKETS, ATT_HEADS), 0.5),
        "norm_mix": gain(ks[2], (DEPTH_2, D_MODEL)),
        "w_in": nrm(ks[3], (DEPTH_2, D_MODEL, IN_COLS), D_MODEL ** -0.5),
        "kv_norm": gain(ks[4], (DEPTH_2, KV_LATENT)),
        "w_uk": nrm(ks[5], (DEPTH_2, ATT_HEADS, ATT_HEAD_DIM, KV_LATENT), ATT_HEAD_DIM ** -0.5),
        "w_uv": nrm(ks[6], (DEPTH_2, ATT_HEADS, ATT_HEAD_DIM, KV_LATENT), KV_LATENT ** -0.5),
        "conv_ssm_w": nrm(ks[7], (DEPTH_2, SSM_CONV, SSM_XBC), SSM_CONV ** -0.5),
        "conv_ssm_b": nrm(ks[9], (DEPTH_2, SSM_XBC), 0.01),
        "dt_bias": dt_bias,
        "a_log": jnp.log(jax.random.uniform(ks[10], (DEPTH_2, SSM_HEADS), f32, 1.0, 16.0)),
        "d_skip": 1.0 + 0.1 * jax.random.normal(ks[11], (DEPTH_2, SSM_HEADS), f32),
        "ssm_norm": gain(ks[12], (DEPTH_2, SSM_INNER)),
        "w_att_out": nrm(ks[13], (DEPTH_2, ATT_HEADS * ATT_HEAD_DIM, D_MODEL),
                         (ATT_HEADS * ATT_HEAD_DIM) ** -0.5),
        "w_ssm_out": nrm(ks[14], (DEPTH_2, SSM_INNER, D_MODEL), SSM_INNER ** -0.5),
        "w_out": nrm(ks[15], (DEPTH_2, D_MODEL, D_MODEL), D_MODEL ** -0.5),
        "norm_ffn": gain(ks[16], (DEPTH_2, D_MODEL)),
        "w_ffn_up": nrm(ks[17], (DEPTH_2, D_MODEL, 2 * FFN_DIM), D_MODEL ** -0.5),
        "conv_ffn_w": nrm(ks[18], (DEPTH_2, FFN_CONV, 2 * FFN_DIM), FFN_CONV ** -0.5),
        "conv_ffn_b": nrm(ks[19], (DEPTH_2, 2 * FFN_DIM), 0.01),
        "w_ffn_down": nrm(ks[20], (DEPTH_2, FFN_DIM, D_MODEL), FFN_DIM ** -0.5),
        "norm_final": gain(ks[21], (D_MODEL,)),
    }

def second_block(x, rel_bias, norm_mix, w_in, kv_norm, w_uk, w_uv, conv_ssm_w, conv_ssm_b,
              dt_bias, a_log, d_skip, ssm_norm, w_att_out, w_ssm_out, w_out, norm_ffn,
              w_ffn_up, conv_ffn_w, conv_ffn_b, w_ffn_down, norm_final):
    b, s, _ = x.shape
    for layer in range(DEPTH_2):
        h = rmsnorm(x, norm_mix[layer])
        proj = h @ w_in[layer]
        (q, c_raw, q_idx, k_idx, w_idx, z, xbc, dt_raw, g_att, g_ssm) = split_cols(proj, IN_SPLITS)

        q = q.reshape(b, s, ATT_HEADS, ATT_HEAD_DIM)
        q_lat = jnp.einsum("bshd,hdc->bshc", q, w_uk[layer])
        c_kv = rmsnorm(c_raw, kv_norm[layer])
        att_lat = dsa_attention(q_lat, c_kv,
                                q_idx.reshape(b, s, IDX_HEADS, IDX_DIM), k_idx, w_idx,
                                rel_bias)
        att = jnp.einsum("bshc,hdc->bshd", att_lat, w_uv[layer])
        y_att = att.reshape(b, s, ATT_HEADS * ATT_HEAD_DIM) @ w_att_out[layer]

        xbc = jax.nn.silu(causal_depthwise_conv(xbc, conv_ssm_w[layer], conv_ssm_b[layer]))
        xs, bm, cm = split_cols(xbc, (SSM_INNER, SSM_GROUPS * SSM_STATE, SSM_GROUPS * SSM_STATE))
        dt = jax.nn.softplus(dt_raw.astype(jnp.float32) + dt_bias[layer].astype(jnp.float32))
        a = -jnp.exp(a_log[layer].astype(jnp.float32))
        xh = xs.reshape(b, s, SSM_GROUPS, SSM_HEADS_PER_GROUP, SSM_HEAD_DIM)
        y = ssd_scan(xh,
                     dt.reshape(b, s, SSM_GROUPS, SSM_HEADS_PER_GROUP),
                     a.reshape(SSM_GROUPS, SSM_HEADS_PER_GROUP),
                     bm.reshape(b, s, SSM_GROUPS, SSM_STATE),
                     cm.reshape(b, s, SSM_GROUPS, SSM_STATE))
        y = y + d_skip[layer].astype(jnp.float32).reshape(
            SSM_GROUPS, SSM_HEADS_PER_GROUP)[..., None] * xh.astype(jnp.float32)
        y = gated_group_rmsnorm(y.reshape(b, s, SSM_INNER), z, ssm_norm[layer])
        y_ssm = y @ w_ssm_out[layer]

        merged = jax.nn.sigmoid(g_att) * y_att + jax.nn.sigmoid(g_ssm) * y_ssm
        x = x + merged @ w_out[layer]

        h = rmsnorm(x, norm_ffn[layer])
        u = causal_depthwise_conv(h @ w_ffn_up[layer], conv_ffn_w[layer], conv_ffn_b[layer])
        gate, val = jnp.split(u, 2, axis=-1)
        x = x + (jax.nn.silu(gate) * val) @ w_ffn_down[layer]
    return rmsnorm(x, norm_final)


def setup_inputs(seed=0):
    out = dict(first_inputs(seed))
    for name, value in second_inputs(seed + 1).items():
        if name != "x":
            out[name + "_2"] = value
    return out


def reference(
    x, meta_tokens, even_w_in, even_f_bias, diff_lambda, diff_subln_g, even_w_out, ret_w_in,
    ret_w_out, ln_g, ln_b, ffn_w1, ffn_w2, rel_bias_2, norm_mix_2, w_in_2, kv_norm_2, w_uk_2,
    w_uv_2, conv_ssm_w_2, conv_ssm_b_2, dt_bias_2, a_log_2, d_skip_2, ssm_norm_2, w_att_out_2,
    w_ssm_out_2, w_out_2, norm_ffn_2, w_ffn_up_2, conv_ffn_w_2, conv_ffn_b_2, w_ffn_down_2,
    norm_final_2,
):
    x = first_block(
        x, meta_tokens, even_w_in, even_f_bias, diff_lambda, diff_subln_g, even_w_out, ret_w_in,
        ret_w_out, ln_g, ln_b, ffn_w1, ffn_w2,
    )
    return second_block(
        x, rel_bias_2, norm_mix_2, w_in_2, kv_norm_2, w_uk_2, w_uv_2, conv_ssm_w_2,
        conv_ssm_b_2, dt_bias_2, a_log_2, d_skip_2, ssm_norm_2, w_att_out_2, w_ssm_out_2,
        w_out_2, norm_ffn_2, w_ffn_up_2, conv_ffn_w_2, conv_ffn_b_2, w_ffn_down_2, norm_final_2,
    )


_drawn_inputs = setup_inputs


def setup_inputs(seed=0):
    import zlib

    import numpy as np

    out = dict(_drawn_inputs(seed))
    spreads = {}
    factors = {'diff_lambda': 8.0,
     'diff_subln_g': 5.836,
     'kv_norm_2': 5.481,
     'conv_ssm_b_2': 20.222,
     'conv_ffn_b_2': 8.0,
     'd_skip_2': 4.689,
     'ssm_norm_2': 5.379,
     'norm_ffn_2': 3.436}
    for name, (base, spread) in spreads.items():
        noise = np.random.default_rng([zlib.crc32(name.encode()), seed]).standard_normal(out[name].shape)
        drawn = base * np.exp(spread * noise) if base else spread * noise
        out[name] = __import__('jax').numpy.asarray(drawn.astype(out[name].dtype))
    for name, factor in factors.items():
        out[name] = (out[name] * factor).astype(out[name].dtype)
    return out
```

```python
import math
from contextlib import ExitStack

import concourse.bass as bass
import numpy as np
from concourse import mybir

ALU = mybir.AluOpType
ACT = mybir.ActivationFunctionType
F32 = mybir.dt.float32
F32R = mybir.dt.float32r

P = 128
D = 1024
KT = D // P
META = 16
SEQ = 512
T = META + SEQ
HALF = T // 2
QT = SEQ // P
NEG = -1.0e30
FILL = -3.0e38
FIRST_MIN = 3.0e38
ALPHA = 4.0 ** 0.25
LN_EPS = 1e-5
RMS_EPS = 1e-6
LAM_INIT = 0.8 - 0.6 * math.exp(-0.3 * 0)

DIFF_HEADS, FOX_HEADS, RET_HEADS = 4, 8, 4
ATT_HEADS, IDX_HEADS = 16, 8
SSM_GROUPS, HEADS_PER_GROUP = 4, 8
FFN2 = 2816 // P

SKEW = 641 * P

RING = 4
AHEAD = RING - 1

STAGES = [("qk", 16), ("forget", 1), ("v", 8), ("even_out", 8),
          ("up0a", 16), ("down0a", 16), ("up0b", 16), ("down0b", 16)]
STAGES += [("ret0", 12), ("ret1", 12), ("ret_out0", 8), ("ret2", 12), ("ret3", 12), ("ret_out1", 8)]
STAGES += [("up1a", 16), ("down1a", 16), ("up1b", 16), ("down1b", 16)]
STAGES += [("latq", 8), ("latc", 1), ("idxq", 4), ("idxk", 1), ("idxw", 1), ("att_out", 8), ("gate_att", 8), ("dt", 1)]
STAGES += [s for g in range(SSM_GROUPS) for s in ((f"xs{g}", 6), (f"z{g}", 4), (f"so{g}", 4))]
STAGES += [("gate_ssm", 8), ("mix_out", 8)]
STAGES += [s for g, n in enumerate((8, 8, 6)) for s in ((f"gv{g}", 2 * n), (f"fd{g}", 8))]
CHUNKS = dict(STAGES)
KGROUPS = {n: 2 for n in ("down0a", "down0b", "down1a", "down1b")}
FIRST_CHUNK, FIRST_TILE = {}, {}
_c = _t = 0
for _n, _k in STAGES:
    FIRST_CHUNK[_n], FIRST_TILE[_n] = _c, _t
    _c += _k
    _t += 2 * _k if _n.startswith("so") else _k // KGROUPS.get(_n, 1)
TOTAL_CHUNKS, TOTAL_TILES = _c, _t

PARAM = {}
_c = 0
for _n, _k in [("ln_g", 32), ("ln_b", 32), ("subln_g", 1), ("f_bias", 1), ("norm_mix", 8), ("norm_ffn", 8),
               ("norm_final", 8), ("kv_norm", 1), ("conv_ssm_w", 96), ("conv_ssm_b", 24), ("ssm_norm", 16),
               ("d_skip", 16), ("dt_bias", 1), ("a_log", 1), ("conv_ffn_w", 132), ("conv_ffn_b", 44),
               ("rel_far", 16)]:
    PARAM[_n] = _c
    _c += _k
PARAMS = _c


class Step:

    def __init__(self, start, i=0, stride=0):
        self.start, self.i, self.stride = start, i, stride

    def plus(self, k):
        return Step(self.start + k, self.i, self.stride)

    def over(self, n):
        assert self.stride % n == 0
        return Step(self.start // n, self.i, self.stride // n)

    def mod(self, n):
        assert self.stride % n == 0
        return self.start % n

    def at(self, factor=1, plus=0):
        fixed = self.start * factor + plus
        return fixed + self.i * (self.stride * factor) if self.stride else fixed


def loop(eng, n, unroll, body, peel=0, tail=0, chains=()):
    done = peel * unroll
    turns = (n - done) // unroll - tail
    for t in range(done):
        body(Step(t))
    if turns >= 2:
        before = [chain.count for chain, _ in chains]
        with eng.Fori(0, turns) as i:
            for chain, per_step in chains:
                chain.turn = i * (per_step * unroll)
            for j in range(unroll):
                body(Step(done + j, i, unroll))
        for (chain, per_step), first in zip(chains, before):
            assert chain.count == first + per_step * unroll
            chain.count, chain.turn = first + per_step * unroll * turns, 0
        done += turns * unroll
    for t in range(done, n):
        body(Step(t))


def wait(eng, sem, value):
    if not isinstance(value, int) or value > 0:
        eng.wait_ge(sem, value)


class Chain:

    def __init__(self, sem):
        self.sem, self.count, self.turn = sem, 0, 0

    def mark(self, ins):
        ins.then_inc(self.sem, 1)
        self.count += 1

    def settle(self, eng):
        eng.wait_ge(self.sem, self.turn + self.count)


def one(step):
    return bass.ds(step.at(), 1) if step.stride else slice(step.start, step.start + 1)


TABLE = {}
_c = 0
for _n, _k in [("ident", P), ("tri", P), ("sel", FOX_HEADS * P), ("causal", T), ("alibi", DIFF_HEADS * T),
               ("decay", RET_HEADS * SEQ), ("decay_meta", RET_HEADS * SEQ), ("bucket", 640)]:
    TABLE[_n] = _c
    _c += _k
TABLES = _c


def program(nc, x_in, weights, params, tables, lam_in, w_uk, w_uv, rel, line, skewed, acum_dram, out, until="end"):
    with ExitStack() as ctx:
        def sb(name, shape, dt=F32):
            return ctx.enter_context(nc.sbuf_tensor(name, shape, dt))

        def sem(name):
            return ctx.enter_context(nc.semaphore(name))

        raw = sb("raw", [P, RING, 8, P])
        w_hi = sb("w_hi", [P, RING, 8, P], F32R)
        w_lo = sb("w_lo", [P, RING, 8, P], F32R)
        x32 = sb("x32", [P, KT, T])
        x_hi = sb("x_hi", [P, KT, T], F32R)
        x_lo = sb("x_lo", [P, KT, T], F32R)
        ident = sb("ident", [P, P])
        ones_d = sb("ones_d", [P, P])
        ones_h = sb("ones_h", [P, P])
        ones_g = sb("ones_g", [P, P])
        par = sb("par", [P, PARAMS])
        small = sb("small", [P, 64])
        shared = nc.sbuf_base
        placed = {}

        def at(name, shape, dt=F32, start=None):
            off = placed["next"] if start is None else start
            off = (off + 31) // 32 * 32
            size = int(np.prod(shape[1:])) * 4
            assert off + size <= nc.sbuf_usable_end, (name, off + size, nc.sbuf_usable_end)
            placed["next"] = off + size
            return nc.alloc_sbuf_tensor_at(name, shape, dt, offset=off)

        ps = ctx.enter_context(nc.psum_tensor("ps", [P, 8, 512], F32))
        flat = ps[:, :, :].rearrange("p b n -> p (b n)")

        def bank(b, n=1024, rows=slice(0, P)):
            return flat[rows, b * 512:b * 512 + n]

        landed = [sem(f"landed{s}") for s in range(RING)]
        hi_ready = sem("hi_ready")
        lo_ready = sem("lo_ready")
        chunk_done = sem("chunk_done")
        evicted = [sem(f"evicted{s}") for s in range(2)]
        dve_own, act_own, pool_own = sem("dve_own"), sem("act_own"), sem("pool_own")
        dve_chain, act_chain, pool_chain = Chain(dve_own), Chain(act_own), Chain(pool_own)
        loaded = sem("loaded")

        def tiles_out(eng, tile):
            for s in range(2):
                wait(eng, evicted[s], (tile - s + 1) // 2)

        def stream_weights(sp):
            def body(g):
                s = g.mod(RING)
                wait(sp, lo_ready, g.at(plus=1 - RING))
                src = weights[one(g), :, :].rearrange("g p n -> p (g n)")
                sp.dma_start(raw[:, s, :, :].rearrange("p k n -> p (k n)"), src).then_inc(landed[s], 16)
            loop(sp, TOTAL_CHUNKS, RING, body, peel=1)

        def split_hi(act, g):
            if not g.stride and g.start >= TOTAL_CHUNKS:
                return
            s = g.mod(RING)
            act.wait_ge(landed[s], g.over(RING).at(16, 16))
            wait(act, chunk_done, g.at(plus=1 - RING))
            nc.scalar.activation(w_hi[:, s], raw[:, s], ACT.Copy).then_inc(hi_ready, 1)

        def split_lo(dve, g):
            if not g.stride and g.start >= TOTAL_CHUNKS:
                return
            s = g.mod(RING)
            dve.wait_ge(hi_ready, g.at(plus=1))
            nc.vector.tensor_tensor(w_lo[:, s], raw[:, s], w_hi[:, s], ALU.subtract).then_inc(lo_ready, 1)

        def tile_out(tile, wide):
            s = tile.mod(2)
            return ps[:, 2 * s:2 * s + 2, 0:HALF] if wide else ps[:, 2 * s:2 * s + 1, 0:SEQ]

        def halves(ap, wide):
            return ap[:, 0:T].rearrange("p (h n) -> p h n", h=2) if wide else ap[:, META:T].rearrange("p (h n) -> p h n", h=1)

        def chunk_products(pe, name, t, act_hi, act_lo, wide, nk=8, k0=0, start=True, stop=True, first_col=0):
            kg = KGROUPS.get(name, 1)
            g = t.plus(FIRST_CHUNK[name])
            tile = t.over(kg).plus(FIRST_TILE[name])
            s = g.mod(RING)
            pe.wait_ge(lo_ready, g.at(plus=1))
            if start:
                wait(pe, evicted[tile.mod(2)], tile.over(2).at())
            o = tile_out(tile, wide)
            parts = [(h, slice(h * HALF, (h + 1) * HALF)) for h in range(2)] if wide else [(0, slice(META, T))]
            for k in range(nk):
                for n, (w, a) in enumerate(((w_hi, act_hi), (w_hi, act_lo), (w_lo, act_hi))):
                    for h, cols in parts:
                        last = nc.tensor.matmul(o[:, h, :], w[:, s, k], a[:, k0 + k, cols],
                                                start=start and k == 0 and n == 0, stop=stop and k == nk - 1 and n == 2)
            last.then_inc(chunk_done, 1)

        def pe_stage(pe, name, act_hi, act_lo, wide, before=None):
            kg = KGROUPS.get(name, 1)

            def body(t):
                c = t.mod(kg) if kg > 1 else 0
                if before:
                    before(t)
                chunk_products(pe, name, t, act_hi, act_lo, wide, k0=8 * c, start=c == 0, stop=c == kg - 1)
            loop(pe, CHUNKS[name], 4, body, peel=1 if before or FIRST_CHUNK[name] == 0 else 0)

        def side_stage(eng, split, name, evict, chains=(), peel=0, unroll=4):
            kg = KGROUPS.get(name, 1)
            last = FIRST_CHUNK[name] + CHUNKS[name] + AHEAD > TOTAL_CHUNKS

            def body(t):
                split(eng, t.plus(FIRST_CHUNK[name] + AHEAD))
                if t.mod(kg) == kg - 1 and evict:
                    evict(t.over(kg), t.plus(FIRST_CHUNK[name]).at(plus=1))
            loop(eng, CHUNKS[name], unroll, body, peel=max(peel, FIRST_CHUNK[name] == 0), tail=1 if last else 0,
                 chains=chains)

        placed["next"] = shared
        qk = at("qk", [P, 16, T])
        vt = at("vt", [P, 5, D])
        diff_o = at("diff_o", [P, DIFF_HEADS, T])
        alibi = at("alibi", [P, DIFF_HEADS, T])
        causal = at("causal", [P, T])
        sel = at("sel", [FOX_HEADS, FOX_HEADS, P])
        cum_f = at("cum_f", [FOX_HEADS, T])
        neg_cum = at("neg_cum", [FOX_HEADS, T])
        work = placed["next"]
        v_slot = at("v_slot", [P, 2, T])
        f_row = at("f_row", [FOX_HEADS, 4, T])
        s_buf = at("s_buf", [P, 4, T], start=work)
        p_norm = at("p_norm", [P, 3, T])
        p_turn = at("p_turn", [P, 2, 5, P])
        stat = at("stat", [P, 4, 64])
        lam_row = at("lam_row", [P, 4, 64])
        even_end = placed["next"]

        products = [("a", h, j) for h in range(DIFF_HEADS) for j in range(5)]
        products += [("b", h, j) for h in range(FOX_HEADS) for j in range(5)]
        maps = {}
        for p, (kind, h, j) in enumerate(products):
            n = sum(len(m) for m in maps.values())
            maps[p] = [n, n + 1] if kind == "a" else [n]
        NPROD = len(products)
        product_of = {u: p for p in maps for u in maps[p]}
        v_turned, v_stored = sem("v_turned"), sem("v_stored")
        scored, masked, expd, normed = sem("scored"), sem("masked"), sem("expd"), sem("normed")
        turned, turn_kept, weighed = sem("turned"), sem("turn_kept"), sem("weighed")
        head_hi, head_lo = sem("head_hi"), sem("head_lo")
        forget_in, forget_ready, lam_ready = sem("forget_in"), sem("forget_ready"), sem("lam_ready")

        def q_rows(j):
            return (0, META) if j == 0 else (META + (j - 1) * P, P)

        def keys_of(j):
            return META if j == 0 else META + j * P

        def even_loads(pool):
            for dst, src in ((x32[:, :, :], x_in), (par[:], params), (ident[:], tables[:, 0:P]),
                             (alibi[:].rearrange("p h n -> p (h n)"), tables[:, TABLE["alibi"]:TABLE["alibi"] + 4 * T]),
                             (causal[:], tables[:, TABLE["causal"]:TABLE["causal"] + T]),
                             (sel[:].rearrange("p h n -> p (h n)"), tables[0:8, TABLE["sel"]:TABLE["sel"] + 8 * P]),
                             (lam_row[:].rearrange("p a n -> p (a n)"), lam_in)):
                pool.dma_start(dst, src).then_inc(loaded, 16)
            nc.gpsimd.memset(ones_d[:], 1.0 / D).then_inc(forget_in, 1)
            nc.gpsimd.memset(ones_h[:], 1.0 / P).then_inc(forget_in, 1)
            nc.gpsimd.memset(ones_g[:], 1.0 / 512).then_inc(forget_in, 1)
            nc.gpsimd.memset(f_row[:, 3, :], 1.0).then_inc(forget_in, 1)

        LOADS = 7 * 16
        x_split_hi, x_split_lo = sem("x_split_hi"), sem("x_split_lo")

        def even_act_start(act):
            act.wait_ge(loaded, LOADS)
            for k in range(KT):
                nc.scalar.activation(x_hi[:, k], x32[:, k], ACT.Copy).then_inc(x_split_hi, 1)
            for g in range(AHEAD):
                split_hi(act, Step(g))

        def even_dve_start(dve):
            dve.wait_ge(loaded, LOADS)
            for k in range(KT):
                dve.wait_ge(x_split_hi, k + 1)
                nc.vector.tensor_tensor(x_lo[:, k], x32[:, k], x_hi[:, k], ALU.subtract).then_inc(x_split_lo, 1)
            for g in range(AHEAD):
                split_lo(dve, Step(g))

        def qk_act(act):
            def keep(tile, done):
                act.wait_ge(chunk_done, done)
                nc.scalar.activation(halves(qk[:, one(tile)].rearrange("p a n -> p (a n)"), True),
                                     tile_out(tile.plus(FIRST_TILE["qk"]), True), ACT.Copy,
                                     scale=0.125 if tile.mod(8) < 4 else 1.0) \
                    .then_inc(evicted[tile.mod(2)], 1)
            side_stage(act, split_hi, "qk", keep, unroll=8, peel=0)

        def forget_act(act):
            tile = Step(FIRST_TILE["forget"])
            split_hi(act, Step(FIRST_CHUNK["forget"] + AHEAD))
            act.wait_ge(chunk_done, FIRST_CHUNK["forget"] + 1)
            bias = par[0:8, PARAM["f_bias"]:PARAM["f_bias"] + 1]
            act_chain.mark(nc.scalar.activation(halves(f_row[:, 0], True), tile_out(tile, True)[0:8], ACT.Identity, bias=bias))
            act_chain.settle(act)
            nc.scalar.activation(f_row[:, 1], f_row[:, 0], ACT.Abs).then_inc(evicted[tile.mod(2)], 1)
            act.wait_ge(evicted[tile.mod(2)], tile.start // 2 + 1)
            act_chain.mark(nc.scalar.activation(f_row[:, 1], f_row[:, 1], ACT.Exp, scale=-1.0))
            act_chain.settle(act)
            nc.scalar.activation(f_row[:, 2], f_row[:, 1], ACT.Ln, bias=1.0).then_inc(forget_in, 1)

        def forget_dve(dve):
            split_lo(dve, Step(FIRST_CHUNK["forget"] + AHEAD))
            dve.wait_ge(forget_in, 5)
            dve_chain.mark(nc.vector.tensor_scalar(f_row[:, 1], f_row[:, 0], 0.0, None, ALU.min))
            dve_chain.settle(dve)
            dve_chain.mark(nc.vector.tensor_tensor(f_row[:, 2], f_row[:, 1], f_row[:, 2], ALU.subtract))
            dve_chain.settle(dve)
            dve_chain.mark(nc.vector.tensor_tensor_scan(cum_f[:], f_row[:, 3], f_row[:, 2], 0.0, ALU.mult, ALU.add))
            dve_chain.settle(dve)
            nc.vector.tensor_scalar(neg_cum[:], cum_f[:], -1.0, None, ALU.mult).then_inc(forget_ready, 1)

        def v_act(act):
            def keep(tile, done):
                act.wait_ge(chunk_done, done)
                wait(act, v_turned, tile.at(plus=-1))
                nc.scalar.activation(halves(v_slot[:, tile.mod(2)], True), tile_out(tile.plus(FIRST_TILE["v"]), True),
                                     ACT.Copy).then_inc(evicted[tile.plus(FIRST_TILE["v"]).mod(2)], 1)
            side_stage(act, split_hi, "v", keep, peel=1)

        def v_pe(pe):
            def turn(t):
                tile = FIRST_TILE["v"] + t
                pe.wait_ge(evicted[tile % 2], tile // 2 + 1)
                wait(pe, v_stored, t)
                for b in range(5):
                    c, n = q_rows(b)
                    o = 2048 + (512 if b == 0 else (b - 1) * P)
                    last = nc.tensor.transpose(flat[0:n, o:o + P], v_slot[:, t % 2, c:c + n], ident[:, :])
                last.then_inc(v_turned, 1)
            pe.wait_ge(loaded, LOADS)
            for t in range(8):
                chunk_products(pe, "v", Step(t), x_hi, x_lo, True)
                if t:
                    turn(t - 1)
            turn(7)

        def v_dve(dve):
            for t in range(8):
                split_lo(dve, Step(FIRST_CHUNK["v"] + t + AHEAD))
                dve.wait_ge(v_turned, t + 1)
                nc.vector.tensor_copy(vt[:, 1:5, t * P:(t + 1) * P], bank(4, 512).rearrange("p (b n) -> p b n", b=4))
                nc.vector.tensor_copy(vt[0:META, 0, t * P:(t + 1) * P], flat[0:META, 2560:2560 + P]).then_inc(v_stored, 1)

        def lam_dve(dve):
            for m in range(2):
                dve_chain.mark(nc.vector.tensor_tensor_reduce(lam_row[:, 2 * m], lam_row[:, 2 * m], lam_row[:, 2 * m + 1], 1.0, 0.0,
                                                              ALU.mult, ALU.add, small[:, m:m + 1]))
            dve_chain.settle(dve)
            nc.vector.tensor_scalar(small[:, 8:10], small[:, 0:2], 1.0, None, ALU.mult).then_inc(lam_ready, 1)
            dve.wait_ge(lam_ready, 2)
            dve_chain.mark(nc.vector.tensor_tensor(small[:, 4:5], small[:, 3:4], small[:, 2:3], ALU.subtract))
            dve_chain.settle(dve)
            dve_chain.mark(nc.vector.tensor_scalar(small[:, 4:5], small[:, 4:5], -LAM_INIT, None, ALU.add))
            g = PARAM["subln_g"]
            dve_chain.mark(nc.vector.tensor_scalar(small[:, 5:6], par[:, g:g + 1], 1.0 - LAM_INIT, None, ALU.mult))
            dve_chain.settle(dve)

        def lam_act(act):
            act.wait_ge(lam_ready, 1)
            nc.scalar.activation(small[:, 2:4], small[:, 8:10], ACT.Exp).then_inc(lam_ready, 1)

        def even_scores(pe, p):
            kind, h, j = products[p]
            (c, n), keys = q_rows(j), keys_of(j)
            for m, u in enumerate(maps[p]):
                if u >= 2:
                    pe.wait_ge(masked, u - 1)
                o = (u % 2) * 1024
                if kind == "a":
                    rows, qt, kt_ = slice(64 * m, 64 * m + 64), h, 4 + h
                else:
                    rows, qt, kt_ = slice(64 * (h % 2), 64 * (h % 2) + 64), 8 + h // 2, 12 + h // 2
                for a in range(0, keys, 512):
                    b = min(keys, a + 512)
                    last = nc.tensor.matmul(flat[0:n, o + a:o + b], qk[rows, qt, c:c + n], qk[rows, kt_, a:b],
                                            start=True, stop=kind == "a")
                    if kind == "b":
                        for e in range(a, b, P):
                            f = min(b, e + P)
                            nc.tensor.matmul(flat[0:n, o + e:o + f], cum_f[:, c:c + n], sel[:, h, 0:f - e],
                                             start=False, stop=False, skip_group_check=True)
                        last = nc.tensor.matmul(flat[0:n, o + a:o + b], sel[:, h, 0:n], neg_cum[:, a:b], start=False, stop=True)
                last.then_inc(scored, 1)

        def even_mask(dve, p):
            kind, h, j = products[p]
            (c, n), keys = q_rows(j), keys_of(j)
            f0 = 400 if j == 0 else 528 - keys
            for u in maps[p]:
                bias = (alibi[0:n, h] if kind == "a" else causal[0:n])[:, f0:f0 + keys]
                dve.wait_ge(scored, u + 1)
                if u >= 4:
                    dve.wait_ge(normed, product_of[u - 4] + 1)
                nc.vector.tensor_tensor_reduce(s_buf[0:n, u % 4, 0:keys], bank((u % 2) * 2, keys, slice(0, n)), bias, -1.0,
                                               FIRST_MIN, ALU.add, ALU.min, stat[0:n, 0, u % 64:u % 64 + 1]).then_inc(masked, 1)

        def even_exp(act, p):
            kind, h, j = products[p]
            n, keys = q_rows(j)[1], keys_of(j)
            for u in maps[p]:
                act.wait_ge(masked, u + 1)
                s = s_buf[0:n, u % 4, 0:keys]
                nc.scalar.activation(s, s, ACT.Exp, scale=-1.0, bias=stat[0:n, 0, u % 64:u % 64 + 1],
                                     accum_out=stat[0:n, 1, u % 64:u % 64 + 1]).then_inc(expd, 1)

        def even_norm(dve, p):
            kind, h, j = products[p]
            n, keys = q_rows(j)[1], keys_of(j)
            dve.wait_ge(expd, maps[p][-1] + 1)
            for u in maps[p]:
                q = u % 64
                dve_chain.mark(nc.vector.reciprocal(stat[0:n, 2, q:q + 1], stat[0:n, 1, q:q + 1]))
            dve_chain.settle(dve)
            if p >= 3:
                dve.wait_ge(turned, p - 2)
            q = maps[p][0] % 64
            o = p_norm[0:n, p % 3, 0:keys]
            ins = nc.vector.tensor_scalar(o, s_buf[0:n, maps[p][0] % 4, 0:keys], stat[0:n, 2, q:q + 1], None, ALU.mult)
            if kind == "a":
                dve_chain.mark(ins)
                dve_chain.mark(nc.vector.tensor_scalar(stat[0:n, 3, q:q + 1], stat[0:n, 2, q + 1:q + 2], small[0:n, 4:5], None, ALU.mult))
                dve_chain.settle(dve)
                ins = nc.vector.scalar_tensor_tensor(o, s_buf[0:n, maps[p][1] % 4, 0:keys], stat[0:n, 3, q:q + 1], o, ALU.mult, ALU.add)
            ins.then_inc(normed, 1)

        def even_turn(pe, p):
            n, j = q_rows(products[p][2])[1], products[p][2]
            pe.wait_ge(normed, p + 1)
            if p:
                pe.wait_ge(turn_kept, p)
            for b in range(j + 1):
                c, k = q_rows(b)
                o = 2048 + (512 if b == 0 else (b - 1) * P)
                last = nc.tensor.transpose(flat[0:k, o:o + n], p_norm[0:n, p % 3, c:c + k], ident[0:n, 0:n])
            last.then_inc(turned, 1)

        def even_keep_turned(act, p):
            n, j = q_rows(products[p][2])[1], products[p][2]
            act.wait_ge(turned, p + 1)
            if p >= 2:
                act.wait_ge(weighed, p - 1)
            if j:
                nc.scalar.activation(p_turn[:, p % 2, 0:j, :], bank(4, j * P).rearrange("p (b n) -> p b n", b=j), ACT.Copy)
            nc.scalar.activation(p_turn[0:META, p % 2, 4, 0:n], flat[0:META, 2560:2560 + n], ACT.Copy).then_inc(turn_kept, 1)

        def groups_before(p):
            return sum(1 for q in range(p) if ends_group(q))

        def ends_group(p):
            kind, h, j = products[p]
            return j == 4 and (kind == "a" or h % 2 == 1)

        def even_values(pe, p):
            kind, h, j = products[p]
            c, n = q_rows(j)
            pe.wait_ge(turn_kept, p + 1)
            done = groups_before(p)
            if done and (p == 0 or ends_group(p - 1)):
                pe.wait_ge(head_hi, done)
                wait(pe, head_lo, done - DIFF_HEADS)
            rows = slice(0, P) if kind == "a" else slice(64 * (h % 2), 64 * (h % 2) + 64)
            col = h * P if kind == "a" else 512 + h * 64
            wide = P if kind == "a" else 64
            o = 3072 + (512 if j == 0 else (j - 1) * P)
            for b in range(j + 1):
                k = q_rows(b)[1]
                last = nc.tensor.matmul(flat[rows, o:o + n], vt[0:k, b, col:col + wide],
                                        p_turn[0:k, p % 2, 4 if b == 0 else b - 1, 0:n], start=b == 0, stop=b == j)
            last.then_inc(weighed, 1)

        def even_keep_head(act, p):
            kind, h, j = products[p]
            if not ends_group(p):
                return
            act.wait_ge(weighed, p + 1)
            dst = diff_o[:, h] if kind == "a" else x_hi[:, 4 + h // 2]
            nc.scalar.activation(dst[:, META:T], bank(6, 512), ACT.Copy)
            nc.scalar.activation(dst[:, 0:META], bank(7, META), ACT.Copy).then_inc(head_hi, 1)

        def even_head_lo(dve, p):
            kind, h, j = products[p]
            if not ends_group(p) or kind == "a":
                return
            k = 4 + h // 2
            dve.wait_ge(head_hi, groups_before(p) + 1)
            nc.vector.tensor_tensor(x_lo[:, k, META:T], bank(6, 512), x_hi[:, k, META:T], ALU.subtract)
            nc.vector.tensor_tensor(x_lo[:, k, 0:META], bank(7, META), x_hi[:, k, 0:META], ALU.subtract).then_inc(head_lo, 1)

        def even_attention_pe(pe):
            pe.wait_ge(forget_ready, 1)
            pe.wait_ge(v_stored, 8)
            tiles_out(pe, FIRST_TILE["even_out"])
            for p in range(NPROD + 3):
                if p < NPROD:
                    even_scores(pe, p)
                if 2 <= p < NPROD + 2:
                    even_turn(pe, p - 2)
                if 3 <= p:
                    even_values(pe, p - 3)
            pe.wait_ge(head_sq, 1)
            pe.wait_ge(head_lo, 4)
            for h in range(DIFF_HEADS):
                nc.tensor.matmul(bank(2 * h, 512), ones_h[:], diff_sq[:, h, META:T], start=True, stop=True)
                nc.tensor.matmul(bank(2 * h + 1, META), ones_h[:], diff_sq[:, h, 0:META], start=True, stop=True).then_inc(head_mean, 1)

        head_sq, head_mean, head_var, head_root, head_t, diff_hi_s, diff_lo_s = (
            sem(n) for n in ("head_sq", "head_mean", "head_var", "head_root", "head_t", "diff_hi", "diff_lo"))
        diff_sq = nc.alloc_sbuf_tensor_at("diff_sq", [P, DIFF_HEADS, T], F32, offset=shared)
        diff_rt = nc.alloc_sbuf_tensor_at("diff_rt", [P, DIFF_HEADS, T], F32, offset=shared + DIFF_HEADS * T * 4)

        def even_attention_act(act):
            lam_act(act)
            for p in range(NPROD + 4):
                if p < NPROD:
                    even_exp(act, p)
                if 2 <= p < NPROD + 2:
                    even_keep_turned(act, p - 2)
                if 4 <= p:
                    even_keep_head(act, p - 4)
            act.wait_ge(weighed, NPROD)
            nc.scalar.activation(diff_sq[:], diff_o[:], ACT.Square).then_inc(head_sq, 1)
            for h in range(DIFF_HEADS):
                act.wait_ge(head_var, h + 1)
                nc.scalar.activation(diff_rt[:, h], diff_rt[:, h], ACT.Sqrt).then_inc(head_root, 1)
            for h in range(DIFF_HEADS):
                act.wait_ge(head_t, h + 1)
                nc.scalar.activation(x_hi[:, h], diff_o[:, h], ACT.Copy).then_inc(diff_hi_s, 1)

        def even_attention_dve(dve):
            lam_dve(dve)
            for p in range(NPROD + 4):
                if p < NPROD:
                    even_mask(dve, p)
                if 1 <= p < NPROD + 1:
                    even_norm(dve, p - 1)
                if 4 <= p:
                    even_head_lo(dve, p - 4)
            for h in range(DIFF_HEADS):
                dve.wait_ge(head_mean, h + 1)
                nc.vector.tensor_scalar(diff_rt[:, h, META:T], bank(2 * h, 512), RMS_EPS, None, ALU.add)
                nc.vector.tensor_scalar(diff_rt[:, h, 0:META], bank(2 * h + 1, META), RMS_EPS, None, ALU.add).then_inc(head_var, 1)
            for h in range(DIFF_HEADS):
                dve.wait_ge(head_root, h + 1)
                dve_chain.mark(nc.vector.reciprocal(diff_rt[:, h], diff_rt[:, h]))
                dve_chain.settle(dve)
                nc.vector.scalar_tensor_tensor(diff_o[:, h], diff_o[:, h], small[:, 5:6], diff_rt[:, h], ALU.mult, ALU.mult).then_inc(head_t, 1)
            for h in range(DIFF_HEADS):
                dve.wait_ge(diff_hi_s, h + 1)
                nc.vector.tensor_tensor(x_lo[:, h], diff_o[:, h], x_hi[:, h], ALU.subtract).then_inc(diff_lo_s, 1)

        def residual_dve(dve, name, wide, factor):
            def add(tile, done):
                dve.wait_ge(chunk_done, done)
                o = halves(x32[:, one(tile)].rearrange("p a n -> p (a n)"), wide)
                u = tile.plus(FIRST_TILE[name])
                nc.vector.scalar_tensor_tensor(o, o, factor, tile_out(u, wide), ALU.mult, ALU.add).then_inc(evicted[u.mod(2)], 1)
            side_stage(dve, split_lo, name, add)

        def only_split(eng, split, name):
            side_stage(eng, split, name, None)

        norms = {"all": 0, "layer": 0}
        norm_mean, norm_less, norm_squared, norm_var, norm_veps, norm_root, norm_scaled, norm_y, norm_hi, norm_lo = (
            sem(f"norm_{n}") for n in ("mean", "less", "squared", "var", "veps", "root", "scaled", "y", "hi", "lo"))
        mlp_squared, mlp_hi, mlp_lo = (sem(f"mlp_{n}") for n in ("squared", "hi", "lo"))

        class Norm:

            def __init__(self, name, tile, wide, g, b=None, eps=LN_EPS, start=None, last=False):
                self.last = last
                self.name, self.tile, self.wide, self.g, self.b, self.eps = name, tile, wide, g, b, eps
                self.c0 = 0 if wide else META
                placed["next"] = shared if start is None else start
                self.xc = at(name + "_xc", [P, KT, T])
                self.sq = at(name + "_sq", [P, KT, T])
                self.rt = at(name + "_rt", [P, T])
                self.n = norms["all"]
                self.nl = norms["layer"]
                norms["all"] += 1
                norms["layer"] += b is not None
                self.lo_at = KT * (self.n + 1)
                self.y = x32 if b is not None else self.sq

            def cols(self):
                return [(META, T, 0)] + ([(0, META, 512)] if self.wide else [])

            def pe(self, pe):
                tiles_out(pe, self.tile)
                if self.b is not None:
                    for k in range(KT):
                        for a, b, o in self.cols():
                            last = nc.tensor.matmul(flat[:, 2048 + o:2048 + o + b - a], ones_d[:], x32[:, k, a:b],
                                                    start=k == 0, stop=k == KT - 1)
                    last.then_inc(norm_mean, 1)
                for k in range(KT):
                    pe.wait_ge(norm_squared, KT * self.n + k + 1)
                    for a, b, o in self.cols():
                        last = nc.tensor.matmul(flat[:, 3072 + o:3072 + o + b - a], ones_d[:], self.sq[:, k, a:b],
                                                start=k == 0, stop=k == KT - 1)
                last.then_inc(norm_var, 1)

            def dve(self, dve):
                xc = self.xc if self.b is not None else x32
                if self.b is not None:
                    dve.wait_ge(norm_mean, self.nl + 1)
                    for k in range(KT):
                        for a, b, o in self.cols():
                            last = nc.vector.tensor_tensor(xc[:, k, a:b], x32[:, k, a:b], flat[:, 2048 + o:2048 + o + b - a], ALU.subtract)
                        last.then_inc(norm_less, 1)
                dve.wait_ge(norm_var, self.n + 1)
                for a, b, o in self.cols():
                    last = nc.vector.tensor_scalar(self.rt[:, a:b], flat[:, 3072 + o:3072 + o + b - a], self.eps, None, ALU.add)
                last.then_inc(norm_veps, 1)
                dve.wait_ge(norm_root, self.n + 1)
                dve_chain.mark(nc.vector.reciprocal(self.rt[:, self.c0:T], self.rt[:, self.c0:T]))
                dve_chain.settle(dve)
                for k in range(KT):
                    nc.vector.tensor_tensor(self.xc[:, k, self.c0:T], xc[:, k, self.c0:T], self.rt[:, self.c0:T], ALU.mult).then_inc(norm_scaled, 1)
                for k in range(0 if self.last else KT):
                    dve.wait_ge(norm_hi, KT * self.n + k + 1)
                    nc.vector.tensor_tensor(x_lo[:, k, self.c0:T], self.y[:, k, self.c0:T], x_hi[:, k, self.c0:T], ALU.subtract).then_inc(norm_lo, 1)

            def act(self, act):
                src = self.xc if self.b is not None else x32
                if self.b is None:
                    tiles_out(act, self.tile)
                    wait(act, norm_y, KT * self.n)
                for k in range(KT):
                    if self.b is not None:
                        act.wait_ge(norm_less, KT * self.nl + k + 1)
                    nc.scalar.activation(self.sq[:, k, self.c0:T], src[:, k, self.c0:T], ACT.Square).then_inc(norm_squared, 1)
                act.wait_ge(norm_veps, self.n + 1)
                nc.scalar.activation(self.rt[:, self.c0:T], self.rt[:, self.c0:T], ACT.Sqrt).then_inc(norm_root, 1)
                for k in range(KT):
                    act.wait_ge(norm_scaled, KT * self.n + k + 1)
                    g = par[:, self.g + k:self.g + k + 1]
                    kw = {"bias": par[:, self.b + k:self.b + k + 1]} if self.b is not None else {}
                    nc.scalar.activation(self.y[:, k, self.c0:T], self.xc[:, k, self.c0:T], ACT.Identity, scale=g, **kw).then_inc(norm_y, 1)
                    if self.last:
                        continue
                    nc.scalar.activation(x_hi[:, k, self.c0:T], self.xc[:, k, self.c0:T], ACT.Identity, scale=g, **kw).then_inc(norm_hi, 1)

        class Mlp:

            def __init__(self, layer, wide):
                self.layer, self.wide = layer, wide
                placed["next"] = shared
                self.h_hi = at(f"h_hi{layer}", [P, 16, T], F32R)
                self.h_lo = at(f"h_lo{layer}", [P, 16, T], F32R)
                self.pos = at(f"h_pos{layer}", [P, 2, T])
                self.sq = at(f"h_sq{layer}", [P, 2, T])

            def pe(self, pe, norm):
                def from_hidden(half):
                    def before(t):
                        if not t.stride and t.start < 2:
                            pe.wait_ge(mlp_lo, 32 * self.layer + 16 * half + 8 * (t.start + 1))
                    return before
                pe.wait_ge(norm_lo, norm.lo_at)
                for half, hn in enumerate("ab"):
                    pe_stage(pe, f"up{self.layer}{hn}", x_hi, x_lo, self.wide)
                    pe_stage(pe, f"down{self.layer}{hn}", self.h_hi, self.h_lo, self.wide, before=from_hidden(half))

            def act(self, act):
                for half, hn in enumerate("ab"):
                    name = f"up{self.layer}{hn}"

                    def keep(tile, done):
                        u = tile.plus(FIRST_TILE[name])
                        act.wait_ge(chunk_done, done)
                        wait(act, mlp_squared, tile.at(plus=32 * self.layer + 16 * half - 1))
                        nc.scalar.activation(halves(self.pos[:, tile.mod(2)], self.wide), tile_out(u, self.wide), ACT.Relu) \
                            .then_inc(evicted[u.mod(2)], 1)
                        act.wait_ge(mlp_squared, tile.at(plus=32 * self.layer + 16 * half + 1))
                        nc.scalar.activation(halves(self.h_hi[:, one(tile)].rearrange("p a n -> p (a n)"), self.wide),
                                             halves(self.sq[:, tile.mod(2)], self.wide), ACT.Copy).then_inc(mlp_hi, 1)
                    side_stage(act, split_hi, name, keep, peel=int(self.layer == half == 0))
                    only_split(act, split_hi, f"down{self.layer}{hn}")

            def dve(self, dve):
                for half, hn in enumerate("ab"):
                    name = f"up{self.layer}{hn}"

                    def keep(tile, done):
                        u = tile.plus(FIRST_TILE[name])
                        dve.wait_ge(evicted[u.mod(2)], u.over(2).at(plus=1))
                        pos = halves(self.pos[:, tile.mod(2)], self.wide)
                        sq = halves(self.sq[:, tile.mod(2)], self.wide)
                        nc.vector.tensor_tensor(sq, pos, pos, ALU.mult).then_inc(mlp_squared, 1)
                        dve.wait_ge(mlp_hi, tile.at(plus=32 * self.layer + 16 * half + 1))
                        row = one(tile)
                        nc.vector.tensor_tensor(halves(self.h_lo[:, row].rearrange("p a n -> p (a n)"), self.wide), sq,
                                                halves(self.h_hi[:, row].rearrange("p a n -> p (a n)"), self.wide), ALU.subtract) \
                            .then_inc(mlp_lo, 1)
                    side_stage(dve, split_lo, name, keep)
                    residual_dve(dve, f"down{self.layer}{hn}", self.wide, ALPHA if half == 0 else 1.0)

        ln00 = Norm("ln00", FIRST_TILE["up0a"], True, PARAM["ln_g"], PARAM["ln_b"])
        mlp0 = Mlp(0, True)
        ln01 = Norm("ln01", FIRST_TILE["ret0"], True, PARAM["ln_g"] + 8, PARAM["ln_b"] + 8)

        placed["next"] = shared
        ret_hi = at("ret_hi", [P, 8, T], F32R)
        ret_lo = at("ret_lo", [P, 8, T], F32R)
        rq = at("rq", [P, 2, T])
        rk = at("rk", [P, 2, T])
        rv_slot = at("rv_slot", [P, 2, T])
        rv = at("rv", [P, 5, 512])
        decayed = at("decayed", [P, 5, SEQ])
        ro = at("ro", [P, 4, SEQ])
        rg = at("rg", [P, 4, SEQ])
        rsq = at("rsq", [P, 4, SEQ])
        decay = at("decay", [P, SEQ])
        decay_meta = at("decay_meta", [META, SEQ])
        ret_rt = at("ret_rt", [P, SEQ])
        (decay_in, rv_turned, rv_stored, ret_scored, ret_decayed, ret_weighed, ret_squared, ret_copied, ret_var, ret_veps,
         ret_root, ret_gated, ret_hi_s, ret_lo_s) = (
            sem(n) for n in ("decay_in", "rv_turned", "rv_stored", "ret_scored", "ret_decayed", "ret_weighed", "ret_squared",
                             "ret_copied", "ret_var", "ret_veps", "ret_root", "ret_gated", "ret_hi_s", "ret_lo_s"))

        def ret_loads(pool):
            for h in range(RET_HEADS):
                if h == 0:
                    pool.wait_ge(norm_lo, ln01.lo_at)
                else:
                    pool.wait_ge(ret_decayed, 5 * h)
                a, b = TABLE["decay"] + h * SEQ, TABLE["decay_meta"] + h * SEQ
                pool.dma_start(decay[:], tables[:, a:a + SEQ]).then_inc(decay_in, 16)
                pool.dma_start(decay_meta[:], tables[0:META, b:b + SEQ]).then_inc(decay_in, 16)

        def ret_pe(pe, h):
            name = f"ret{h}"
            for c in range(12):
                chunk_products(pe, name, Step(c), x_hi, x_lo, 2 <= c < 8)
                if 5 <= c < 9:
                    t = c - 5
                    u = FIRST_TILE[name] + 4 + t
                    pe.wait_ge(evicted[u % 2], u // 2 + 1)
                    wait(pe, rv_stored, 4 * h + t)
                    if t == 0:
                        wait(pe, ret_decayed, 5 * h)
                        wait(pe, ret_veps, h)
                    for b in range(5):
                        c0, n = q_rows(b)
                        o = 2048 + (512 if b == 0 else (b - 1) * P)
                        last = nc.tensor.transpose(flat[0:n, o:o + P], rv_slot[:, t % 2, c0:c0 + n], ident[:, :])
                    last.then_inc(rv_turned, 1)
            pe.wait_ge(rv_stored, 4 * h + 4)
            for i, b in enumerate((1, 2, 3, 4, 0)):
                c0, n = q_rows(b)
                w = SEQ if b == 0 else SEQ - (b - 1) * P
                if i >= 2:
                    pe.wait_ge(ret_decayed, 5 * h + i - 1)
                for k in range(2):
                    last = nc.tensor.matmul(flat[0:n, 2048 + (i % 2) * 512:2048 + (i % 2) * 512 + w], rk[:, k, c0:c0 + n],
                                            rq[:, k, T - w:T], start=k == 0, stop=k == 1)
                last.then_inc(ret_scored, 1)
            for e in range(4):
                n0 = 4 * h + e
                if e == 0:
                    pe.wait_ge(ret_decayed, 5 * h + 5)
                wait(pe, ret_copied, n0 - 1)
                o = (6 + e % 2) * 512
                for i, b in enumerate((1, 2, 3, 4, 0)):
                    n = q_rows(b)[1]
                    w = SEQ if b == 0 else SEQ - (b - 1) * P
                    last = nc.tensor.matmul(flat[:, o + SEQ - w:o + SEQ], rv[0:n, b, e * P:(e + 1) * P],
                                            decayed[0:n, b, SEQ - w:SEQ], start=i == 0, stop=i == 4)
                last.then_inc(ret_weighed, 1)
            for e in range(4):
                pe.wait_ge(ret_squared, 4 * h + e + 1)
                last = nc.tensor.matmul(bank(4, SEQ), ones_g[:], rsq[:, e], start=e == 0, stop=e == 3)
            last.then_inc(ret_var, 1)

        def ret_act(act, h):
            name = f"ret{h}"
            for c in range(12):
                u = Step(FIRST_TILE[name] + c)
                split_hi(act, Step(FIRST_CHUNK[name] + c + AHEAD))
                act.wait_ge(chunk_done, FIRST_CHUNK[name] + c + 1)
                wide = 2 <= c < 8
                src = tile_out(u, wide)
                if c < 2:
                    if c == 0:
                        wait(act, ret_scored, 5 * h)
                    nc.scalar.activation(halves(rq[:, c], wide), src, ACT.Copy).then_inc(evicted[u.mod(2)], 1)
                elif c < 4:
                    nc.scalar.activation(halves(rk[:, c - 2], wide), src, ACT.Copy, scale=1.0 / 16).then_inc(evicted[u.mod(2)], 1)
                elif c < 8:
                    wait(act, rv_turned, 4 * h + c - 4 - 1)
                    nc.scalar.activation(halves(rv_slot[:, c % 2], wide), src, ACT.Copy).then_inc(evicted[u.mod(2)], 1)
                else:
                    if c == 8:
                        wait(act, ret_gated, 4 * h)
                    nc.scalar.activation(rg[:, c - 8:c - 7], src, ACT.Silu).then_inc(evicted[u.mod(2)], 1)
            for e in range(4):
                act.wait_ge(ret_copied, 4 * h + e + 1)
                if e == 0:
                    wait(act, ret_var, h)
                nc.scalar.activation(rsq[:, e], ro[:, e], ACT.Square).then_inc(ret_squared, 1)
            act.wait_ge(ret_veps, h + 1)
            nc.scalar.activation(ret_rt[:], ret_rt[:], ACT.Sqrt).then_inc(ret_root, 1)
            for e in range(4):
                act.wait_ge(ret_gated, 4 * h + e + 1)
                if e == 0 and h == 2:
                    act.wait_ge(chunk_done, FIRST_CHUNK["ret_out0"] + 8)
                nc.scalar.activation(ret_hi[:, 4 * (h % 2) + e, META:T], ro[:, e], ACT.Copy).then_inc(ret_hi_s, 1)

        def ret_dve(dve, h):
            name = f"ret{h}"
            for c in range(12):
                split_lo(dve, Step(FIRST_CHUNK[name] + c + AHEAD))
                if 5 <= c < 9:
                    t = c - 5
                    dve.wait_ge(rv_turned, 4 * h + t + 1)
                    if t == 0:
                        wait(dve, ret_weighed, 4 * h)
                    nc.vector.tensor_copy(rv[:, 1:5, t * P:(t + 1) * P], bank(4, 512).rearrange("p (b n) -> p b n", b=4))
                    nc.vector.tensor_copy(rv[0:META, 0, t * P:(t + 1) * P], flat[0:META, 2560:2560 + P]).then_inc(rv_stored, 1)
            dve.wait_ge(decay_in, 32 * (h + 1))
            for i, b in enumerate((1, 2, 3, 4, 0)):
                n = q_rows(b)[1]
                w = SEQ if b == 0 else SEQ - (b - 1) * P
                dve.wait_ge(ret_scored, 5 * h + i + 1)
                d = decay_meta[:, 0:w] if b == 0 else decay[:, 0:w]
                o = 2048 + (i % 2) * 512
                nc.vector.tensor_tensor(decayed[0:n, b, SEQ - w:SEQ], flat[0:n, o:o + w], d, ALU.mult).then_inc(ret_decayed, 1)
            for e in range(4):
                dve.wait_ge(ret_weighed, 4 * h + e + 1)
                if e == 0:
                    wait(dve, ret_hi_s, 4 * h)
                    wait(dve, ret_lo_s, 4 * h)
                nc.vector.tensor_copy(ro[:, e], bank(6 + e % 2, SEQ)).then_inc(ret_copied, 1)
            dve.wait_ge(ret_var, h + 1)
            nc.vector.tensor_scalar(ret_rt[:], bank(4, SEQ), RMS_EPS, None, ALU.add).then_inc(ret_veps, 1)
            dve.wait_ge(ret_root, h + 1)
            dve_chain.mark(nc.vector.reciprocal(ret_rt[:], ret_rt[:]))
            dve_chain.settle(dve)
            for e in range(4):
                dve_chain.mark(nc.vector.tensor_tensor(ro[:, e], ro[:, e], ret_rt[:], ALU.mult))
            dve_chain.settle(dve)
            for e in range(4):
                nc.vector.tensor_tensor(ro[:, e], ro[:, e], rg[:, e], ALU.mult).then_inc(ret_gated, 1)
            for e in range(4):
                dve.wait_ge(ret_hi_s, 4 * h + e + 1)
                nc.vector.tensor_tensor(ret_lo[:, 4 * (h % 2) + e, META:T], ro[:, e], ret_hi[:, 4 * (h % 2) + e, META:T],
                                        ALU.subtract).then_inc(ret_lo_s, 1)

        def retention_pe(pe):
            pe.wait_ge(norm_lo, ln01.lo_at)
            for h in range(RET_HEADS):
                ret_pe(pe, h)
                if h % 2:
                    pe.wait_ge(ret_lo_s, 4 * h + 4)
                    pe_stage(pe, f"ret_out{h // 2}", ret_hi, ret_lo, False)

        def retention_act(act):
            for h in range(RET_HEADS):
                ret_act(act, h)
                if h % 2:
                    only_split(act, split_hi, f"ret_out{h // 2}")

        def retention_dve(dve):
            for h in range(RET_HEADS):
                ret_dve(dve, h)
                if h % 2:
                    residual_dve(dve, f"ret_out{h // 2}", False, ALPHA if h == 1 else 1.0)

        ln10 = Norm("ln10", FIRST_TILE["up1a"], False, PARAM["ln_g"] + 16, PARAM["ln_b"] + 16)
        mlp1 = Mlp(1, False)
        ln11 = Norm("ln11", FIRST_TILE["latq"], False, PARAM["ln_g"] + 24, PARAM["ln_b"] + 24)

        rms_mix = Norm("rms_mix", FIRST_TILE["latq"], False, PARAM["norm_mix"], eps=RMS_EPS)
        placed["next"] = shared
        merged = at("merged", [P, KT, SEQ])
        after_merged = placed["next"]
        lq = nc.alloc_sbuf_tensor_at("lq", [P, KT, SEQ], F32, offset=shared)
        key_row = at("key_row", [P, SEQ])
        key_tok = at("key_tok", [P, QT, P])
        wuk = at("wuk", [P, 8, P])
        wuv = at("wuv", [P, 8, P])
        select = at("select", [P, 1280])
        att_hi = at("att_hi", [P, KT, T], F32R)
        att_lo = at("att_lo", [P, KT, T], F32R)
        dsa_work = placed["next"]
        bias_near = at("bias_near", [P, 2, 2 * P])
        q_lat = at("q_lat", [P, 2, SEQ])
        d_buf = at("d_buf", [P, 4, SEQ])
        d_norm = at("d_norm", [P, 3, SEQ])
        d_turn = at("d_turn", [P, 2, SEQ])
        att_lat = at("att_lat", [P, 2, SEQ])
        d_stat = at("d_stat", [P, 3, 64])
        dsa_causal = at("dsa_causal", [P, P])
        key_raw = at("key_raw", [P, SEQ], start=dsa_work)
        key_sq = at("key_sq", [P, SEQ])
        key_rt = at("key_rt", [P, SEQ])
        iq = at("iq", [P, 4, SEQ])
        ik = at("ik", [P, SEQ])
        iw_row = at("iw_row", [IDX_HEADS, SEQ])
        iw = at("iw", [P, QT, IDX_HEADS])
        i_relu = at("i_relu", [P, 2, SEQ])
        top = at("top", [P, 3, 8])
        bucket = at("bucket", [32, 640])
        rel_sb = at("rel_sb", [32, ATT_HEADS])
        line_sb = at("line_sb", [ATT_HEADS, 640])

        (dsa_loaded, line_done, line_kept, line_out, key_squared, key_mean, key_veps, key_root, key_ready,
         key_turned, key_kept, idx_turned, idx_kept, idx_scored, idx_relu, idx_added, selected) = (
            sem(n) for n in ("dsa_loaded", "line_done", "line_kept", "line_out", "key_squared", "key_mean", "key_veps",
                             "key_root", "key_ready", "key_turned", "key_kept", "idx_turned", "idx_kept", "idx_scored", "idx_relu",
                             "idx_added", "selected"))
        (ql_done, ql_kept, d_scored, d_biased, d_expd, d_inverse, d_normed, d_turned, d_kept, d_weighed, lat_kept, att_done, att_hi_s,
         att_lo_s, gate_done) = (
            sem(n) for n in ("ql_done", "ql_kept", "d_scored", "d_biased", "d_expd", "d_inverse", "d_normed", "d_turned", "d_kept",
                             "d_weighed", "lat_kept", "att_done", "att_hi_s", "att_lo_s", "gate_done"))

        skew_out = sem("skew_out")
        near_in = [sem(f"near_in{n}") for n in range(2)]

        def sel_cols(i):
            a = P * i * (i + 1) // 2
            return slice(a, a + P * (i + 1))

        def dsa_loads(pool):
            pool.wait_ge(norm_lo, rms_mix.lo_at)
            for dst, src in ((bucket[:], tables[0:32, TABLE["bucket"]:TABLE["bucket"] + 640]), (rel_sb[:], rel),
                             (wuk[:], w_uk), (wuv[:].rearrange("p a n -> p (a n)"), w_uv),
                             (dsa_causal[:], tables[:, TABLE["causal"] + 400:TABLE["causal"] + 528])):
                pool.dma_start(dst, src).then_inc(dsa_loaded, 16)
            pool.wait_ge(line_kept, 1)
            pool.dma_start(line, line_sb[:]).then_inc(line_out, 16)
            pool.wait_ge(line_out, 16)
            for h in range(ATT_HEADS):
                src = bass.AP(tensor=line.tensor, offset=h * 640 + 256, ap=[[0, P], [1, 384]])
                dst = bass.AP(tensor=skewed.tensor, offset=h * SKEW + 256, ap=[[641, P], [1, 384]])
                pool.dma_start(dst, src).then_inc(skew_out, 16)
            pool.wait_ge(skew_out, 16 * ATT_HEADS)
            pool.wait_ge(selected, 1)
            for h in range(ATT_HEADS):
                if h >= 2:
                    pool.wait_ge(d_biased, 4 * (h - 1))
                src = bass.AP(tensor=skewed.tensor, offset=h * SKEW + 383, ap=[[640, P], [1, 2 * P]])
                pool.dma_start(bias_near[:, h % 2], src).then_inc(near_in[h % 2], 16)

        def single(eng, split, name):
            split(eng, Step(FIRST_CHUNK[name] + AHEAD))

        def keep_tiles(act, name, dst, func=ACT.Copy, scale=1.0, rows=P, n=None):
            def keep(tile, done):
                act.wait_ge(chunk_done, done)
                u = tile.plus(FIRST_TILE[name])
                o = dst[0:rows, one(tile), 0:SEQ] if len(dst.shape) == 3 else dst[0:rows, :].rearrange("p (a n) -> p a n", a=1)
                nc.scalar.activation(o, tile_out(u, False)[0:rows], func, scale=scale).then_inc(evicted[u.mod(2)], 1)
            side_stage(act, split_hi, name, keep)

        def tile_kept(eng, name, n=1):
            tiles_out(eng, FIRST_TILE[name] + n)

        def select_pe(pe):
            pe.wait_ge(norm_lo, rms_mix.lo_at)
            pe_stage(pe, "latq", x_hi, x_lo, False)
            pe_stage(pe, "latc", x_hi, x_lo, False)
            pe_stage(pe, "idxq", x_hi, x_lo, False)
            pe_stage(pe, "idxk", x_hi, x_lo, False)
            pe_stage(pe, "idxw", x_hi, x_lo, False)
            pe.wait_ge(dsa_loaded, 5 * 16)
            nc.tensor.matmul(flat[0:ATT_HEADS, 3072:3584], rel_sb[:], bucket[:, 0:512], start=True, stop=True)
            nc.tensor.matmul(flat[0:ATT_HEADS, 3584:3712], rel_sb[:], bucket[:, 512:640], start=True, stop=True).then_inc(line_done, 1)
            pe.wait_ge(key_squared, 1)
            nc.tensor.matmul(bank(4, SEQ), ones_h[:], key_sq[:], start=True, stop=True).then_inc(key_mean, 1)
            tiles_out(pe, FIRST_TILE["att_out"])
            for j in range(QT):
                last = nc.tensor.transpose(flat[:, 1024 + 8 * j:1024 + 8 * j + 8], iw_row[:, j * P:(j + 1) * P], ident[0:8, 0:8])
            last.then_inc(idx_turned, 1)
            for n in range(3 * IDX_HEADS):
                i, h = 1 + n // IDX_HEADS, n % IDX_HEADS
                rows = slice(64 * (h % 2), 64 * (h % 2) + 64)
                if n < 2:
                    pe.wait_ge(idx_kept, 1)
                else:
                    pe.wait_ge(idx_relu, n - 1)
                nc.tensor.matmul(bank(2 + n % 2, P * (i + 1)), iq[rows, h // 2, i * P:(i + 1) * P], ik[rows, 0:P * (i + 1)],
                                 start=True, stop=True).then_inc(idx_scored, 1)
            pe.wait_ge(key_ready, 1)
            for j in range(QT):
                last = nc.tensor.transpose(flat[:, 2560 + j * P:2560 + (j + 1) * P], key_row[:, j * P:(j + 1) * P], ident[:])
            last.then_inc(key_turned, 1)

        def select_act(act):
            keep_tiles(act, "latq", lq, scale=0.125)
            keep_tiles(act, "latc", key_raw)
            keep_tiles(act, "idxq", iq)
            keep_tiles(act, "idxk", ik)
            keep_tiles(act, "idxw", iw_row, rows=IDX_HEADS)
            tile_kept(act, "latc")
            nc.scalar.activation(key_sq[:], key_raw[:], ACT.Square).then_inc(key_squared, 1)
            act.wait_ge(line_done, 1)
            nc.scalar.activation(line_sb[:], flat[0:ATT_HEADS, 3072:3712], ACT.Copy).then_inc(line_kept, 1)
            act.wait_ge(key_veps, 1)
            nc.scalar.activation(key_rt[:], key_rt[:], ACT.Sqrt).then_inc(key_root, 1)
            for n in range(3 * IDX_HEADS):
                i = 1 + n // IDX_HEADS
                act.wait_ge(idx_scored, n + 1)
                if n >= 2:
                    act.wait_ge(idx_added, n - 1)
                nc.scalar.activation(i_relu[:, n % 2, 0:P * (i + 1)], bank(2 + n % 2, P * (i + 1)), ACT.Relu).then_inc(idx_relu, 1)

        def select_dve(dve):
            for name in ("latq", "latc", "idxq", "idxk", "idxw"):
                only_split(dve, split_lo, name)
            dve.wait_ge(key_mean, 1)
            nc.vector.tensor_scalar(key_rt[:], bank(4, SEQ), RMS_EPS, None, ALU.add).then_inc(key_veps, 1)
            dve.wait_ge(key_root, 1)
            dve_chain.mark(nc.vector.reciprocal(key_rt[:], key_rt[:]))
            dve_chain.settle(dve)
            g = par[:, PARAM["kv_norm"]:PARAM["kv_norm"] + 1]
            nc.vector.scalar_tensor_tensor(key_row[:], key_raw[:], g, key_rt[:], ALU.mult, ALU.mult).then_inc(key_ready, 1)
            dve.wait_ge(idx_turned, 1)
            nc.vector.tensor_copy(iw[:].rearrange("p a n -> p (a n)"), flat[:, 1024:1056]).then_inc(idx_kept, 1)
            dve.wait_ge(idx_kept, 1)
            dve.wait_ge(dsa_loaded, 5 * 16)
            nc.vector.tensor_copy(select[:, 0:P], dsa_causal[:])
            for n in range(3 * IDX_HEADS):
                i, h = 1 + n // IDX_HEADS, n % IDX_HEADS
                w = iw[:, i, h:h + 1]
                s = select[:, sel_cols(i)]
                r = i_relu[:, n % 2, 0:P * (i + 1)]
                dve.wait_ge(idx_relu, n + 1)
                if h == 0:
                    nc.vector.tensor_scalar(s, r, w, None, ALU.mult).then_inc(idx_added, 1)
                else:
                    dve.wait_ge(idx_added, n)
                    nc.vector.scalar_tensor_tensor(s, r, w, s, ALU.mult, ALU.add).then_inc(idx_added, 1)
                if h == IDX_HEADS - 1:
                    dve.wait_ge(idx_added, n + 1)
                    d = select[:, sel_cols(i).stop - P:sel_cols(i).stop]
                    dve_chain.mark(nc.vector.tensor_tensor(d, d, dsa_causal[:], ALU.add))
            for _ in range(16):
                dve_chain.settle(dve)
                for i in range(1, QT):
                    dve_chain.mark(nc.vector.max(top[:, i - 1], select[:, sel_cols(i)]))
                dve_chain.settle(dve)
                for i in range(1, QT):
                    s = select[:, sel_cols(i)]
                    dve_chain.mark(nc.vector.match_replace(s, top[:, i - 1], s, FILL))
            dve_chain.settle(dve)
            s = select[:, P:1280]
            dve_chain.mark(nc.vector.tensor_scalar(s, s, FILL, 1.0, ALU.is_equal, ALU.subtract))
            dve_chain.settle(dve)
            dve_chain.mark(nc.vector.tensor_scalar(s, s, -NEG, None, ALU.mult))
            dve_chain.settle(dve)
            dve.wait_ge(key_turned, 1)
            nc.vector.tensor_copy(key_tok[:].rearrange("p a n -> p (a n)"), bank(5, SEQ)).then_inc(selected, 1)

        ND = ATT_HEADS * QT

        def d_query(pe, h):
            rows = slice(64 * (h % 2), 64 * (h % 2) + 64)
            if h >= 2:
                pe.wait_ge(ql_kept, h - 1)
            nc.tensor.matmul(bank(2 + h % 2, SEQ), wuk[rows, h // 2, :], lq[rows, h // 2, :], start=True, stop=True).then_inc(ql_done, 1)

        def d_scores(pe, p):
            h, i = divmod(p, QT)
            if i == 0:
                pe.wait_ge(ql_kept, h + 1)
            if p >= 2:
                pe.wait_ge(d_biased, p - 1)
            nc.tensor.matmul(bank(4 + p % 2, P * (i + 1)), q_lat[:, h % 2, i * P:(i + 1) * P], key_row[:, 0:P * (i + 1)],
                             start=True, stop=True).then_inc(d_scored, 1)

        def d_bias(dve, p):
            h, i = divmod(p, QT)
            w = P * (i + 1)
            near = min(w, 2 * P)
            s = d_buf[:, p % 4]
            dve.wait_ge(d_scored, p + 1)
            dve.wait_ge(near_in[h % 2], 16 * (h // 2 + 1))
            if p >= 4:
                dve.wait_ge(d_normed, p - 3)
            dve_chain.mark(nc.vector.tensor_tensor(s[:, w - near:w], bank(4 + p % 2, w)[:, w - near:w], bias_near[:, h % 2, 2 * P - near:2 * P], ALU.add))
            if w > near:
                far = par[:, PARAM["rel_far"] + h:PARAM["rel_far"] + h + 1]
                dve_chain.mark(nc.vector.tensor_scalar(s[:, 0:w - near], bank(4 + p % 2, w - near), far, None, ALU.add))
            dve_chain.settle(dve)
            nc.vector.tensor_tensor_reduce(s[:, 0:w], s[:, 0:w], select[:, sel_cols(i)], -1.0, FIRST_MIN, ALU.add, ALU.min,
                                           d_stat[:, 0, p:p + 1]).then_inc(d_biased, 1)

        def d_exp(act, p):
            w = P * (p % QT + 1)
            s = d_buf[:, p % 4, 0:w]
            act.wait_ge(d_biased, p + 1)
            nc.scalar.activation(s, s, ACT.Exp, scale=-1.0, bias=d_stat[:, 0, p:p + 1], accum_out=d_stat[:, 1, p:p + 1]).then_inc(d_expd, 1)

        def d_invert(dve, p):
            dve.wait_ge(d_expd, p + 1)
            nc.vector.reciprocal(d_stat[:, 2, p:p + 1], d_stat[:, 1, p:p + 1]).then_inc(d_inverse, 1)

        def d_divide(act, p):
            w = P * (p % QT + 1)
            act.wait_ge(d_inverse, p + 1)
            if p >= 3:
                act.wait_ge(d_turned, p - 2)
            nc.scalar.activation(d_norm[:, p % 3, 0:w], d_buf[:, p % 4, 0:w], ACT.Copy, scale=d_stat[:, 2, p:p + 1]).then_inc(d_normed, 1)

        def d_turn_pe(pe, p):
            pe.wait_ge(d_normed, p + 1)
            if p:
                pe.wait_ge(d_kept, p)
            for b in range(p % QT + 1):
                last = nc.tensor.transpose(flat[:, 3072 + b * P:3072 + (b + 1) * P], d_norm[:, p % 3, b * P:(b + 1) * P], ident[:])
            last.then_inc(d_turned, 1)

        def d_keep(act, p):
            w = P * (p % QT + 1)
            act.wait_ge(d_turned, p + 1)
            if p >= 2:
                act.wait_ge(d_weighed, p - 1)
            nc.scalar.activation(d_turn[:, p % 2, 0:w], bank(6, w), ACT.Copy).then_inc(d_kept, 1)

        def d_values(pe, p):
            h, i = divmod(p, QT)
            pe.wait_ge(d_kept, p + 1)
            if i == 0:
                wait(pe, lat_kept, h)
            for b in range(i + 1):
                last = nc.tensor.matmul(flat[:, 3584 + i * P:3584 + (i + 1) * P], key_tok[:, b, :], d_turn[:, p % 2, b * P:(b + 1) * P],
                                        start=b == 0, stop=b == i)
            last.then_inc(d_weighed, 1)

        def d_out(pe, h):
            rows = slice(64 * (h % 2), 64 * (h % 2) + 64)
            pe.wait_ge(lat_kept, h + 1)
            if h >= 4 and h % 2 == 0:
                pe.wait_ge(att_lo_s, h // 2 - 1)
            nc.tensor.matmul(bank((h // 2) % 2, SEQ, rows), wuv[:, h // 2, 64 * (h % 2):64 * (h % 2) + 64], att_lat[:, h % 2],
                             start=True, stop=True).then_inc(att_done, 1)

        def sparse_pe(pe):
            pe.wait_ge(selected, 1)
            pe.wait_ge(idx_relu, 3 * IDX_HEADS)
            d_query(pe, 0)
            d_query(pe, 1)
            for s in range(ND + 5):
                if s < ND:
                    d_scores(pe, s)
                if s % QT == 2 and 2 <= s // QT + 2 < ATT_HEADS and s < ND:
                    d_query(pe, s // QT + 2)
                if 3 <= s < ND + 3:
                    d_turn_pe(pe, s - 3)
                if 4 <= s < ND + 4:
                    d_values(pe, s - 4)
                if s >= 5 and (s - 5) % QT == QT - 1:
                    d_out(pe, (s - 5) // QT)

        def sparse_act(act):
            act.wait_ge(selected, 1)

            def query(h):
                act.wait_ge(ql_done, h + 1)
                if h >= 2:
                    act.wait_ge(d_scored, QT * (h - 1))
                nc.scalar.activation(q_lat[:, h % 2], bank(2 + h % 2, SEQ), ACT.Copy).then_inc(ql_kept, 1)
            query(0)
            query(1)
            for s in range(ND + 6):
                if s < ND:
                    d_exp(act, s)
                if s % QT == 3 and s // QT + 2 < ATT_HEADS:
                    query(s // QT + 2)
                if 1 <= s < ND + 1:
                    d_divide(act, s - 1)
                if 3 <= s < ND + 3:
                    d_keep(act, s - 3)
                if s >= 5 and (s - 5) % QT == QT - 1 and s - 5 < ND:
                    h = (s - 5) // QT
                    act.wait_ge(d_weighed, QT * (h + 1))
                    if h >= 2:
                        act.wait_ge(att_done, h - 1)
                    nc.scalar.activation(att_lat[:, h % 2], bank(7, SEQ), ACT.Copy).then_inc(lat_kept, 1)
                if s >= 6 and (s - 6) % (2 * QT) == 2 * QT - 1:
                    k = (s - 6) // (2 * QT)
                    act.wait_ge(att_done, 2 * k + 2)
                    nc.scalar.activation(att_hi[:, k, META:T], bank(k % 2, SEQ), ACT.Copy).then_inc(att_hi_s, 1)

        def sparse_dve(dve):
            for s in range(ND + 7):
                if s < ND:
                    d_bias(dve, s)
                if 1 <= s < ND + 1:
                    d_invert(dve, s - 1)
                if s >= 7 and (s - 7) % (2 * QT) == 2 * QT - 1:
                    k = (s - 7) // (2 * QT)
                    dve.wait_ge(att_hi_s, k + 1)
                    nc.vector.tensor_tensor(att_lo[:, k, META:T], bank(k % 2, SEQ), att_hi[:, k, META:T], ALU.subtract).then_inc(att_lo_s, 1)

        gate = nc.alloc_sbuf_tensor_at("gate", [P, 2, SEQ], F32, offset=dsa_work)
        gate_dve_done = sem("gate_dve_done")

        def att_merge_pe(pe):
            pe.wait_ge(att_lo_s, KT)
            pe_stage(pe, "att_out", att_hi, att_lo, False)
            pe_stage(pe, "gate_att", x_hi, x_lo, False)

        def att_merge_act(act):
            keep_tiles(act, "att_out", merged)
            gate_act(act, "gate_att", 0)

        def gate_act(act, name, base):
            def keep(tile, done):
                act.wait_ge(chunk_done, done)
                u = tile.plus(FIRST_TILE[name])
                wait(act, gate_dve_done, tile.at(plus=base - 1))
                nc.scalar.activation(gate[:, tile.mod(2):tile.mod(2) + 1], tile_out(u, False), ACT.Sigmoid).then_inc(evicted[u.mod(2)], 1)
            side_stage(act, split_hi, name, keep, peel=0 if base else 1)

        def att_merge_dve(dve):
            only_split(dve, split_lo, "att_out")

            def gated(tile, done):
                u = tile.plus(FIRST_TILE["gate_att"])
                dve.wait_ge(evicted[u.mod(2)], u.over(2).at(plus=1))
                if not tile.stride and tile.start == 0:
                    tiles_out(dve, FIRST_TILE["gate_att"])
                o = merged[:, one(tile)].rearrange("p a n -> p (a n)")
                nc.vector.tensor_tensor(o, o, gate[:, tile.mod(2)], ALU.mult).then_inc(gate_dve_done, 1)
            side_stage(dve, split_lo, "gate_att", gated, peel=1)

        CH = QT
        placed["next"] = after_merged
        y_ssm = at("y_ssm", [P, KT, SEQ])
        u_hi = at("u_hi", [P, 4, T], F32R)
        u_lo = at("u_lo", [P, 4, T], F32R)
        ssm_work = placed["next"]
        xs = at("xs", [P, 4, SEQ])
        b_row = at("b_row", [P, SEQ])
        c_row = at("c_row", [P, SEQ])
        z_buf = at("z_buf", [P, 4, SEQ])
        conv_in = at("conv_in", [P, 2, SEQ + 4])
        abc_start = placed["next"] = (placed["next"] + 31) // 32 * 32
        steps_abc = at("steps_abc", [P, 2, 8, P])
        seg = at("seg", [P, 8, P])
        c_dec = at("c_dec", [P, 8, P])
        x_dt = at("x_dt", [P, 2, SEQ])
        x_dec = at("x_dec", [P, SEQ])
        b_tok = at("b_tok", [P, P])
        cb = at("cb", [P, P])
        tri = at("tri", [P, P])
        state = at("state", [P, SEQ])
        dec_end = at("dec_end", [P, 2, 8])
        dt_tok = at("dt_tok", [P, CH, 32])
        acum_tok = at("acum_tok", [P, CH, 32])
        a_col = at("a_col", [32, 1])
        ssm_end = placed["next"]
        dt_row = nc.alloc_sbuf_tensor_at("dt_row", [32, 4, SEQ], F32, offset=ssm_work)
        dt_one = nc.alloc_sbuf_tensor_at("dt_one", [32, P], F32, offset=ssm_work + 4 * SEQ * 4)
        acum_row = nc.alloc_sbuf_tensor_at("acum_row", [32, SEQ], F32, offset=ssm_work + 5 * SEQ * 4)
        g_sq = nc.alloc_sbuf_tensor_at("g_sq", [P, 4, SEQ], F32, offset=abc_start)
        g_rt = nc.alloc_sbuf_tensor_at("g_rt", [P, SEQ], F32, offset=abc_start + 4 * SEQ * 4)

        (dt_a, dt_b, acum_ready, acum_out, ssm_loaded, dt_turned, dt_kept, conv_done, conv_silu, ssm_turned, seg_args, dec_args,
         seg_exp, dec_exp, abc_exp, y_ready, end_ready, y_done, state_done, abc_used, z_ready, u_done, u_sq, ssm_var, ssm_veps, ssm_root,
         u_norm, u_hi_s, u_lo_s, zeroed, m_sum, m_hi_s, m_lo_s) = (
            sem(n) for n in ("dt_a", "dt_b", "acum_ready", "acum_out", "ssm_loaded", "dt_turned", "dt_kept", "conv_done", "conv_silu",
                             "ssm_turned", "seg_args", "dec_args", "seg_exp", "dec_exp", "abc_exp", "y_ready", "end_ready", "y_done",
                             "state_done", "abc_used", "z_ready", "u_done", "u_sq", "ssm_var", "ssm_veps", "ssm_root", "u_norm",
                             "u_hi_s", "u_lo_s", "zeroed", "m_sum", "m_hi_s", "m_lo_s"))
        abc_in = [sem(f"abc_in{n}") for n in range(2)]

        def ssm_loads(pool):
            pool.wait_ge(gate_dve_done, KT)
            pool.wait_ge(chunk_done, FIRST_CHUNK["gate_att"])
            nc.gpsimd.memset(conv_in[:, :, 0:3], 0.0).then_inc(zeroed, 1)
            nc.gpsimd.memset(dt_one[:], 1.0).then_inc(zeroed, 1)
            pool.dma_start(tri[:], tables[:, TABLE["tri"]:TABLE["tri"] + P]).then_inc(ssm_loaded, 16)
            pool.wait_ge(acum_ready, 1)
            pool.dma_start(acum_dram, acum_row[:]).then_inc(acum_out, 16)
            pool.wait_ge(acum_out, 16)
            for n in range(SSM_GROUPS * CH):
                g, c = divmod(n, CH)
                if n >= 2:
                    pool.wait_ge(abc_used, n - 1)
                if c < 2 and g:
                    pool.wait_ge(ssm_var, g)
                src = bass.AP(tensor=acum_dram.tensor, offset=8 * g * SEQ + c * P, ap=[[0, P], [SEQ, 8], [1, P]])
                pool.dma_start(steps_abc[:, n % 2], src).then_inc(abc_in[n % 2], 16)

        def dt_pe(pe):
            chunk_products(pe, "dt", Step(0), x_hi, x_lo, False)
            pe.wait_ge(acum_ready, 1)
            for src, o in ((dt_row[:, 3], 2048), (acum_row[:], 2176)):
                for c in range(CH):
                    last = nc.tensor.transpose(flat[:, o + 32 * c:o + 32 * c + 32], src[:, c * P:(c + 1) * P], ident[0:32, 0:32])
            last.then_inc(dt_turned, 1)

        def dt_act(act):
            u = Step(FIRST_TILE["dt"])
            split_hi(act, Step(FIRST_CHUNK["dt"] + AHEAD))
            act.wait_ge(chunk_done, FIRST_CHUNK["dt"] + 1)
            act.wait_ge(gate_dve_done, KT)
            act_chain.mark(nc.scalar.activation(dt_row[:, 0:1], tile_out(u, False)[0:32], ACT.Identity,
                                                bias=par[0:32, PARAM["dt_bias"]:PARAM["dt_bias"] + 1]))
            act_chain.settle(act)
            nc.scalar.activation(dt_row[:, 1], dt_row[:, 0], ACT.Abs).then_inc(evicted[u.mod(2)], 1)
            act.wait_ge(evicted[u.mod(2)], u.start // 2 + 1)
            act_chain.mark(nc.scalar.activation(dt_row[:, 1], dt_row[:, 1], ACT.Exp, scale=-1.0))
            nc.scalar.activation(a_col[:], par[0:32, PARAM["a_log"]:PARAM["a_log"] + 1], ACT.Exp).then_inc(dt_a, 1)
            act_chain.settle(act)
            nc.scalar.activation(dt_row[:, 2], dt_row[:, 1], ACT.Ln, bias=1.0).then_inc(dt_a, 1)

        def dt_dve(dve):
            split_lo(dve, Step(FIRST_CHUNK["dt"] + AHEAD))
            dve.wait_ge(dt_a, 2)
            dve_chain.mark(nc.vector.tensor_scalar(dt_row[:, 3], dt_row[:, 0], 0.0, None, ALU.max))
            dve_chain.settle(dve)
            dve_chain.mark(nc.vector.tensor_tensor(dt_row[:, 3], dt_row[:, 3], dt_row[:, 2], ALU.add))
            dve_chain.settle(dve)
            dve_chain.mark(nc.vector.tensor_scalar(dt_row[:, 1], dt_row[:, 3], a_col[:], -1.0, ALU.mult, ALU.mult))
            dve_chain.settle(dve)
            dve.wait_ge(zeroed, 2)
            for c in range(CH):
                cols = slice(c * P, (c + 1) * P)
                ins = nc.vector.tensor_tensor_scan(acum_row[:, cols], dt_one[:], dt_row[:, 1, cols], 0.0, ALU.mult, ALU.add)
            ins.then_inc(acum_ready, 1)
            dve.wait_ge(dt_turned, 1)
            nc.vector.tensor_copy(dt_tok[:].rearrange("p c h -> p (c h)"), flat[:, 2048:2176])
            nc.vector.tensor_copy(acum_tok[:].rearrange("p c h -> p (c h)"), flat[:, 2176:2304]).then_inc(dt_kept, 1)
            dve.wait_ge(dt_kept, 1)
            dve.wait_ge(ssm_loaded, 16)
            dve.wait_ge(acum_out, 16)

        def ssm_turn(pe, g, c):
            n = CH * g + c
            cols = slice(c * P, (c + 1) * P)
            if n:
                pe.wait_ge(y_ready, n)
            for t in range(4):
                nc.tensor.transpose(flat[:, 2048 + t * P:2048 + (t + 1) * P], xs[:, t, cols], ident[:])
            nc.tensor.transpose(flat[:, 2560:2560 + P], b_row[:, cols], ident[:])
            nc.tensor.matmul(flat[:, 2688:2688 + P], b_row[:, cols], c_row[:, cols], start=True, stop=True).then_inc(ssm_turned, 1)

        def ssm_outputs(pe, g, c):
            n = CH * g + c
            pe.wait_ge(y_ready, n + 1)
            if n:
                pe.wait_ge(y_done, n)
            for h in range(HEADS_PER_GROUP):
                rows = slice(64 * (h % 2), 64 * (h % 2) + 64)
                o = flat[rows, 3072 + (h // 2) * P:3072 + (h // 2 + 1) * P]
                last = nc.tensor.matmul(o, x_dt[:, n % 2, 64 * h:64 * h + 64], seg[:, h], start=True, stop=c == 0)
                if c:
                    last = nc.tensor.matmul(o, state[:, 64 * h:64 * h + 64], c_dec[:, h], start=False, stop=True)
            if c == CH - 1:
                last.then_inc(end_ready, 1)
            else:
                nc.tensor.matmul(bank(7, SEQ), b_tok[:], x_dec[:], start=True, stop=True).then_inc(end_ready, 1)

        def ssm_pe(pe, g):
            for t in range(6):
                chunk_products(pe, f"xs{g}", Step(t), x_hi, x_lo, False)
            pe.wait_ge(conv_silu, 3 * g + 3)
            for c in range(CH):
                ssm_turn(pe, g, c)
                chunk_products(pe, f"z{g}", Step(c), x_hi, x_lo, False)
                ssm_outputs(pe, g, c)
            for t in range(4):
                pe.wait_ge(u_sq, 4 * g + t + 1)
                last = nc.tensor.matmul(bank(4, SEQ), ones_g[:], g_sq[:, t], start=t == 0, stop=t == 3)
            last.then_inc(ssm_var, 1)
            pe.wait_ge(u_lo_s, 4 * g + 4)
            for k in range(4):
                ck = FIRST_CHUNK[f"so{g}"] + k
                pe.wait_ge(lo_ready, ck + 1)
                for m in range(2):
                    u = FIRST_TILE[f"so{g}"] + 2 * k + m
                    pe.wait_ge(evicted[u % 2], u // 2)
                    for f in range(4):
                        for w, (a, b) in enumerate(((w_hi, u_hi), (w_hi, u_lo), (w_lo, u_hi))):
                            last = nc.tensor.matmul(ps[:, 2 * (u % 2), 0:SEQ], a[:, ck % RING, 2 * f + m], b[:, f, META:T],
                                                    start=f == 0 and w == 0, stop=f == 3 and w == 2)
                last.then_inc(chunk_done, 1)

        def ssm_act(act, g):
            name = f"xs{g}"
            act.wait_ge(zeroed, 2)
            for t in range(6):
                u = FIRST_TILE[name] + t
                split_hi(act, Step(FIRST_CHUNK[name] + t + AHEAD))
                act.wait_ge(chunk_done, FIRST_CHUNK[name] + t + 1)
                wait(act, conv_done, 6 * g + t - 1)
                nc.scalar.activation(conv_in[:, t % 2:t % 2 + 1, 3:3 + SEQ], tile_out(Step(u), False), ACT.Copy).then_inc(evicted[u % 2], 1)
            act.wait_ge(conv_done, 6 * g + 6)
            for buf in (xs, b_row, c_row):
                nc.scalar.activation(buf[:], buf[:], ACT.Silu).then_inc(conv_silu, 1)
            name = f"z{g}"
            for c in range(CH):
                n = CH * g + c
                act.wait_ge(dec_args, n + 1)
                nc.scalar.activation(dec_end[:, n % 2], dec_end[:, n % 2], ACT.Exp).then_inc(dec_exp, 1)
                act.wait_ge(seg_args, n + 1)
                nc.scalar.activation(seg[:], seg[:], ACT.Exp).then_inc(seg_exp, 1)
                nc.scalar.activation(steps_abc[:, n % 2], steps_abc[:, n % 2], ACT.Exp).then_inc(abc_exp, 1)
                u = FIRST_TILE[name] + c
                split_hi(act, Step(FIRST_CHUNK[name] + c + AHEAD))
                act.wait_ge(chunk_done, FIRST_CHUNK[name] + c + 1)
                ins = nc.scalar.activation(z_buf[:, c:c + 1], tile_out(Step(u), False), ACT.Copy)
                ins.then_inc(evicted[u % 2], 1)
            tiles_out(act, FIRST_TILE[name] + 4)
            nc.scalar.activation(z_buf[:], z_buf[:], ACT.Silu).then_inc(z_ready, 1)
            for t in range(4):
                act.wait_ge(u_done, 4 * g + t + 1)
                nc.scalar.activation(g_sq[:, t], xs[:, t], ACT.Square).then_inc(u_sq, 1)
            act.wait_ge(ssm_veps, g + 1)
            nc.scalar.activation(g_rt[:], g_rt[:], ACT.Sqrt).then_inc(ssm_root, 1)
            for t in range(4):
                act.wait_ge(u_norm, 4 * g + t + 1)
                nc.scalar.activation(u_hi[:, t, META:T], xs[:, t], ACT.Copy).then_inc(u_hi_s, 1)
            only_split(act, split_hi, f"so{g}")

        def convolve(dve, dst, taps, col, src, bias, done):
            for j in reversed(range(taps)):
                w = par[:, col(j)]
                x = src[:, j:j + SEQ]
                if j == taps - 1:
                    dve_chain.mark(nc.vector.tensor_scalar(dst, x, w, par[:, bias], ALU.mult, ALU.add))
                else:
                    dve_chain.settle(dve)
                    ins = nc.vector.scalar_tensor_tensor(dst, x, w, dst, ALU.mult, ALU.add)
                    if j:
                        dve_chain.mark(ins)
            ins.then_inc(done, 1)

        def ssm_dve(dve, g):
            name = f"xs{g}"
            for t in range(6):
                u = FIRST_TILE[name] + t
                split_lo(dve, Step(FIRST_CHUNK[name] + t + AHEAD))
                dve.wait_ge(evicted[u % 2], u // 2 + 1)
                if t == 0:
                    wait(dve, u_hi_s, 4 * g)
                    wait(dve, u_lo_s, 4 * g)
                k = 4 * g + t if t < 4 else (16 + g if t == 4 else 20 + g)
                dst = xs[:, t] if t < 4 else (b_row[:] if t == 4 else c_row[:])
                c0, b0 = PARAM["conv_ssm_w"], PARAM["conv_ssm_b"] + k
                convolve(dve, dst, 4, lambda j: slice(c0 + 24 * j + k, c0 + 24 * j + k + 1), conv_in[:, t % 2], slice(b0, b0 + 1), conv_done)
            heads = slice(8 * g, 8 * g + 8)
            name = f"z{g}"
            for c in range(CH):
                n = CH * g + c
                cols = slice(c * P, (c + 1) * P)
                abc = steps_abc[:, n % 2]
                dve.wait_ge(abc_in[n % 2], 16 * (n // 2 + 1))
                if n >= 1:
                    dve.wait_ge(x_end_used, n)
                nc.vector.tensor_tensor(dec_end[:, n % 2].unsqueeze(2), abc[:, :, P - 1:P], acum_tok[:, c, heads].unsqueeze(2), ALU.subtract) \
                    .then_inc(dec_args, 1)
                wait(dve, end_ready, n)
                for h in range(8):
                    ins = nc.vector.tensor_scalar(seg[:, h], abc[:, h], acum_tok[:, c, 8 * g + h:8 * g + h + 1], 0.0, ALU.subtract, ALU.min)
                ins.then_inc(seg_args, 1)
                split_lo(dve, Step(FIRST_CHUNK[name] + c + AHEAD))
                dve.wait_ge(ssm_turned, n + 1)
                x3 = x_dt[:, n % 2].rearrange("p (h d) -> p h d", h=8)
                dt3 = dt_tok[:, c, heads].unsqueeze(2).broadcast_to([P, 8, 64])
                dve_chain.mark(nc.vector.tensor_tensor(x3, bank(4, SEQ).rearrange("p (h d) -> p h d", h=8), dt3, ALU.mult))
                nc.vector.tensor_copy(b_tok[:], flat[:, 2560:2560 + P])
                dve_chain.mark(nc.vector.tensor_tensor(cb[:], flat[:, 2688:2688 + P], tri[:], ALU.mult))
                dve.wait_ge(dec_exp, n + 1)
                dve_chain.settle(dve)
                nc.vector.tensor_tensor(x_dec[:].rearrange("p (h d) -> p h d", h=8), x3,
                                        dec_end[:, n % 2].unsqueeze(2).broadcast_to([P, 8, 64]), ALU.mult).then_inc(x_end_used, 1)
                dve.wait_ge(seg_exp, n + 1)
                nc.vector.tensor_tensor(seg[:], seg[:], cb[:].unsqueeze(1).broadcast_to([P, 8, P]), ALU.mult)
                dve.wait_ge(abc_exp, n + 1)
                nc.vector.tensor_tensor(c_dec[:], abc, c_row[:, cols].unsqueeze(1).broadcast_to([P, 8, P]), ALU.mult).then_inc(y_ready, 1)
                dve.wait_ge(end_ready, n + 1)
                if c < CH - 1:
                    s3 = state[:].rearrange("p (h d) -> p h d", h=8)
                    if c == 0:
                        ins = nc.vector.tensor_copy(state[:], bank(7, SEQ))
                    else:
                        dve_chain.mark(nc.vector.tensor_tensor(s3, s3, abc[:, :, P - 1:P].broadcast_to([P, 8, 64]), ALU.mult))
                        dve_chain.settle(dve)
                        ins = nc.vector.tensor_tensor(state[:], state[:], bank(7, SEQ), ALU.add)
                    dve_chain.mark(ins)
                for t in range(4):
                    d = PARAM["d_skip"] + 4 * g + t
                    ins = nc.vector.scalar_tensor_tensor(xs[:, t, cols], xs[:, t, cols], par[:, d:d + 1],
                                                         flat[:, 3072 + t * P:3072 + (t + 1) * P], ALU.mult, ALU.add)
                ins.then_inc(y_done, 1)
                dve_chain.settle(dve)
                nc.vector.tensor_copy(small[:, 16:17], small[:, 4:5]).then_inc(abc_used, 1)
            dve.wait_ge(y_done, CH * g + CH)
            dve.wait_ge(z_ready, g + 1)
            for t in range(4):
                nc.vector.tensor_tensor(xs[:, t], xs[:, t], z_buf[:, t], ALU.mult).then_inc(u_done, 1)
            dve.wait_ge(ssm_var, g + 1)
            nc.vector.tensor_scalar(g_rt[:], bank(4, SEQ), RMS_EPS, None, ALU.add).then_inc(ssm_veps, 1)
            dve.wait_ge(ssm_root, g + 1)
            dve_chain.mark(nc.vector.reciprocal(g_rt[:], g_rt[:]))
            dve_chain.settle(dve)
            for t in range(4):
                k = PARAM["ssm_norm"] + 4 * g + t
                nc.vector.scalar_tensor_tensor(xs[:, t], xs[:, t], par[:, k:k + 1], g_rt[:], ALU.mult, ALU.mult).then_inc(u_norm, 1)
            for t in range(4):
                dve.wait_ge(u_hi_s, 4 * g + t + 1)
                nc.vector.tensor_tensor(u_lo[:, t, META:T], xs[:, t], u_hi[:, t, META:T], ALU.subtract).then_inc(u_lo_s, 1)
            for k in range(4):
                split_lo(dve, Step(FIRST_CHUNK[f"so{g}"] + k + AHEAD))
                dve.wait_ge(chunk_done, FIRST_CHUNK[f"so{g}"] + k + 1)
                for m in range(2):
                    u = FIRST_TILE[f"so{g}"] + 2 * k + m
                    src = ps[:, 2 * (u % 2), 0:SEQ]
                    if g == 0:
                        ins = nc.vector.tensor_copy(y_ssm[:, 2 * k + m], src)
                    else:
                        ins = nc.vector.tensor_tensor(y_ssm[:, 2 * k + m], y_ssm[:, 2 * k + m], src, ALU.add)
                    ins.then_inc(evicted[u % 2], 1)

        x_end_used = sem("x_end_used")

        m_hi = nc.alloc_sbuf_tensor_at("m_hi", [P, KT, T], F32R, offset=ssm_work)
        m_lo = nc.alloc_sbuf_tensor_at("m_lo", [P, KT, T], F32R, offset=ssm_work + KT * T * 4)
        placed["next"] = ssm_work + 2 * KT * T * 4
        gate2 = at("gate2", [P, 2, SEQ])

        def mix_pe(pe):
            pe_stage(pe, "gate_ssm", x_hi, x_lo, False)
            pe.wait_ge(m_lo_s, KT)
            pe_stage(pe, "mix_out", m_hi, m_lo, False)

        def mix_act(act):
            def keep(tile, done):
                act.wait_ge(chunk_done, done)
                u = tile.plus(FIRST_TILE["gate_ssm"])
                wait(act, m_sum, tile.at(plus=-1))
                nc.scalar.activation(gate2[:, tile.mod(2):tile.mod(2) + 1], tile_out(u, False), ACT.Sigmoid).then_inc(evicted[u.mod(2)], 1)
                act.wait_ge(m_sum, tile.at(plus=1))
                nc.scalar.activation(m_hi[:, one(tile), META:T], merged[:, one(tile)], ACT.Copy).then_inc(m_hi_s, 1)
            side_stage(act, split_hi, "gate_ssm", keep, peel=1)
            only_split(act, split_hi, "mix_out")

        def mix_dve(dve):
            def add(tile, done):
                u = tile.plus(FIRST_TILE["gate_ssm"])
                dve.wait_ge(evicted[u.mod(2)], u.over(2).at(plus=1))
                gt = gate2[:, tile.mod(2)]
                row = one(tile)
                dve_chain.mark(nc.vector.tensor_tensor(gt, gt, y_ssm[:, row].rearrange("p a n -> p (a n)"), ALU.mult))
                dve_chain.settle(dve)
                o = merged[:, row].rearrange("p a n -> p (a n)")
                nc.vector.tensor_tensor(o, o, gt, ALU.add).then_inc(m_sum, 1)
                dve.wait_ge(m_hi_s, tile.at(plus=1))
                nc.vector.tensor_tensor(m_lo[:, row, META:T], merged[:, row], m_hi[:, row, META:T], ALU.subtract).then_inc(m_lo_s, 1)
            side_stage(dve, split_lo, "gate_ssm", add, peel=2)
            residual_dve(dve, "mix_out", False, 1.0)

        rms_ffn = Norm("rms_ffn", FIRST_TILE["gv0"], False, PARAM["norm_ffn"], eps=RMS_EPS)
        placed["next"] = shared
        f_hi = at("f_hi", [P, 8, T], F32R)
        f_lo = at("f_lo", [P, 8, T], F32R)
        f_in = at("f_in", [P, 4, SEQ + 4])
        f_conv = at("f_conv", [P, 4, SEQ])
        f_zero, f_conved, f_silu, f_prod, f_hi_s, f_lo_s = (sem(n) for n in ("f_zero", "f_conved", "f_silu", "f_prod", "f_hi_s", "f_lo_s"))
        GROUPS = (8, 8, 6)

        def ffn_pool(pool):
            pool.wait_ge(norm_lo, rms_ffn.lo_at)
            nc.gpsimd.memset(f_in[:, :, 0:2], 0.0).then_inc(f_zero, 1)

        def ffn_pe(pe):
            pe.wait_ge(norm_lo, rms_ffn.lo_at)
            done = 0
            for g, n in enumerate(GROUPS):
                pe_stage(pe, f"gv{g}", x_hi, x_lo, False)
                done += n
                pe.wait_ge(f_lo_s, done)
                loop(pe, 8, 4, lambda t: chunk_products(pe, f"fd{g}", t, f_hi, f_lo, False, nk=n))

        def ffn_act(act):
            act.wait_ge(f_zero, 1)
            f0 = 0
            for g, n in enumerate(GROUPS):
                name = f"gv{g}"

                def keep(t, done):
                    pair = t.over(2).plus(f0)
                    slot = 2 * (t.start // 2 % 2) + t.start % 2
                    u = t.plus(FIRST_TILE[name])
                    act.wait_ge(chunk_done, done)
                    wait(act, f_conved, pair.at(2, t.start % 2 - 3))
                    nc.scalar.activation(f_in[:, slot:slot + 1, 2:2 + SEQ], tile_out(u, False), ACT.Copy).then_inc(evicted[u.mod(2)], 1)
                    if t.start % 2:
                        act.wait_ge(f_conved, pair.at(2, 1))
                        nc.scalar.activation(f_conv[:, slot - 1], f_conv[:, slot - 1], ACT.Silu).then_inc(f_silu, 1)
                        act.wait_ge(f_prod, pair.at(1, 1))
                        nc.scalar.activation(f_hi[:, one(t.over(2)), META:T], f_conv[:, slot:slot + 1], ACT.Copy).then_inc(f_hi_s, 1)
                side_stage(act, split_hi, name, keep, peel=1 if g == 0 else 0)
                only_split(act, split_hi, f"fd{g}")
                f0 += n

        def ffn_dve(dve):
            f0 = 0
            for g, n in enumerate(GROUPS):
                name = f"gv{g}"

                def conv(t, done):
                    pair = t.over(2).plus(f0)
                    slot = 2 * (t.start // 2 % 2) + t.start % 2
                    u = t.plus(FIRST_TILE[name])
                    half = FFN2 * (t.start % 2)
                    dve.wait_ge(evicted[u.mod(2)], u.over(2).at(plus=1))
                    wait(dve, f_lo_s, pair.at(1, -1))

                    def col(j):
                        return one(pair.plus(PARAM["conv_ffn_w"] + 44 * j + half))
                    convolve(dve, f_conv[:, slot], 3, col, f_in[:, slot], one(pair.plus(PARAM["conv_ffn_b"] + half)), f_conved)
                    if t.start % 2:
                        dve.wait_ge(f_silu, pair.at(1, 1))
                        dve.wait_ge(f_conved, pair.at(2, 2))
                        o = f_conv[:, slot]
                        nc.vector.tensor_tensor(o, o, f_conv[:, slot - 1], ALU.mult).then_inc(f_prod, 1)
                        dve.wait_ge(f_hi_s, pair.at(1, 1))
                        row = one(t.over(2))
                        nc.vector.tensor_tensor(f_lo[:, row, META:T], f_conv[:, slot:slot + 1], f_hi[:, row, META:T], ALU.subtract).then_inc(f_lo_s, 1)
                side_stage(dve, split_lo, name, conv, peel=1 if g == 0 else 0, chains=[(dve_chain, 2)])
                residual_dve(dve, f"fd{g}", False, 1.0)
                f0 += n

        final = Norm("final", TOTAL_TILES, False, PARAM["norm_final"], eps=RMS_EPS, last=True)

        stored = sem("stored")
        block = ctx.enter_context(nc.Block())

        @block.sync
        def _(sp):
            stream_weights(sp)
            sp.wait_ge(norm_y, KT * norms["all"])
            sp.dma_start(out, final.y[:, :, META:T]).then_inc(stored, 16)
            sp.wait_ge(stored, 16)

        @block.gpsimd
        def _(pool):
            even_loads(pool)
            ret_loads(pool)
            dsa_loads(pool)
            ssm_loads(pool)
            ffn_pool(pool)

        @block.tensor
        def _(pe):
            pe.wait_ge(x_split_lo, KT)
            pe_stage(pe, "qk", x_hi, x_lo, True)
            chunk_products(pe, "forget", Step(0), x_hi, x_lo, True)
            v_pe(pe)
            even_attention_pe(pe)
            pe.wait_ge(diff_lo_s, DIFF_HEADS)
            pe_stage(pe, "even_out", x_hi, x_lo, True)
            ln00.pe(pe)
            mlp0.pe(pe, ln00)
            ln01.pe(pe)
            retention_pe(pe)
            ln10.pe(pe)
            mlp1.pe(pe, ln10)
            ln11.pe(pe)
            rms_mix.pe(pe)
            select_pe(pe)
            sparse_pe(pe)
            att_merge_pe(pe)
            dt_pe(pe)
            for g in range(SSM_GROUPS):
                ssm_pe(pe, g)
            mix_pe(pe)
            rms_ffn.pe(pe)
            ffn_pe(pe)
            final.pe(pe)

        @block.scalar
        def _(act):
            even_act_start(act)
            qk_act(act)
            forget_act(act)
            v_act(act)
            even_attention_act(act)
            only_split(act, split_hi, "even_out")
            ln00.act(act)
            mlp0.act(act)
            ln01.act(act)
            retention_act(act)
            ln10.act(act)
            mlp1.act(act)
            ln11.act(act)
            rms_mix.act(act)
            select_act(act)
            sparse_act(act)
            att_merge_act(act)
            dt_act(act)
            for g in range(SSM_GROUPS):
                ssm_act(act, g)
            mix_act(act)
            rms_ffn.act(act)
            ffn_act(act)
            final.act(act)

        @block.vector
        def _(dve):
            even_dve_start(dve)
            only_split(dve, split_lo, "qk")
            forget_dve(dve)
            v_dve(dve)
            even_attention_dve(dve)
            residual_dve(dve, "even_out", True, ALPHA)
            ln00.dve(dve)
            mlp0.dve(dve)
            ln01.dve(dve)
            retention_dve(dve)
            ln10.dve(dve)
            mlp1.dve(dve)
            ln11.dve(dve)
            rms_mix.dve(dve)
            select_dve(dve)
            sparse_dve(dve)
            att_merge_dve(dve)
            dt_dve(dve)
            for g in range(SSM_GROUPS):
                ssm_dve(dve, g)
            mix_dve(dve)
            rms_ffn.dve(dve)
            ffn_dve(dve)
            final.dve(dve)


def pack(w):
    even, eo, r, ro = w["even_w_in"][0], w["even_w_out"][0], w["ret_w_in"][0], w["ret_w_out"][0]
    w2, parts = w["w_in_2"][0], []

    def cols(m, c0, n, rows=(0, 1024)):
        for c in range(n):
            for r0 in range(rows[0], rows[1], 1024):
                chunk = np.zeros((P, 8, P), np.float32)
                block = m[r0:min(r0 + 1024, rows[1]), c0 + c * P:min(c0 + (c + 1) * P, m.shape[1])]
                k = block.shape[0] // P
                chunk[:, 0:k, 0:block.shape[1]] = block.reshape(k, P, -1).transpose(1, 0, 2)
                parts.append(chunk)

    cols(even, 0, 8)
    cols(even, 1536, 8)
    cols(even, 3072, 1)
    cols(even, 1024, 4)
    cols(even, 2560, 4)
    cols(eo, 0, 8)

    def mlp(layer):
        for half in range(2):
            cols(w["ffn_w1"][layer], 2048 * half, 16)
            cols(w["ffn_w2"][layer], 0, 8, (2048 * half, 2048 * half + 2048))
    mlp(0)
    for h in range(RET_HEADS):
        cols(r, 256 * h, 2)
        cols(r, 1024 + 256 * h, 2)
        cols(r, 2048 + 512 * h, 4)
        cols(r, 4096 + 512 * h, 4)
        if h % 2:
            cols(ro, 0, 8, (1024 * (h // 2), 1024 * (h // 2) + 1024))
    mlp(1)
    cols(w2, 0, 8)
    cols(w2, 1024, 1)
    cols(w2, 1152, 4)
    k_idx = w2[:, 1664:1728]
    cols(np.concatenate([k_idx, k_idx], 1), 0, 1)
    cols(w2[:, 1728:1736], 0, 1)
    cols(w["w_att_out_2"][0], 0, 8)
    cols(w2, 6888, 8)
    cols(w2[:, 6856:6888], 0, 1)
    for g in range(SSM_GROUPS):
        cols(w2, 3784 + 512 * g, 4)
        cols(w2, 3784 + 2048 + 128 * g, 1)
        cols(w2, 3784 + 2560 + 128 * g, 1)
        cols(w2, 1736 + 512 * g, 4)
        rows = w["w_ssm_out_2"][0][512 * g:512 * g + 512]
        for c in range(4):
            parts.append(rows[:, 256 * c:256 * c + 256].reshape(4, P, 2 * P).transpose(1, 0, 2).reshape(P, 8, P))
    cols(w2, 6888 + 1024, 8)
    cols(w["w_out_2"][0], 0, 8)
    up, down, f = w["w_ffn_up_2"][0], w["w_ffn_down_2"][0], 0
    for n in (8, 8, 6):
        for t in range(f, f + n):
            cols(up, t * P, 1)
            cols(up, (FFN2 + t) * P, 1)
        cols(down, 0, 8, (f * P, (f + n) * P))
        f += n
    assert len(parts) == TOTAL_CHUNKS
    return np.stack(parts).reshape(TOTAL_CHUNKS, P, 8 * P)


def pack_params(w):
    out = np.zeros((P, PARAMS), np.float32)

    def put(name, a):
        a = np.asarray(a)
        out[:a.shape[-1], PARAM[name]:PARAM[name] + a.shape[0]] = a.T
    put("ln_g", w["ln_g"].reshape(32, P))
    put("ln_b", w["ln_b"].reshape(32, P))
    put("subln_g", w["diff_subln_g"])
    put("f_bias", w["even_f_bias"])
    put("norm_mix", w["norm_mix_2"].reshape(8, P))
    put("norm_ffn", w["norm_ffn_2"].reshape(8, P))
    put("norm_final", w["norm_final_2"].reshape(8, P))
    put("kv_norm", w["kv_norm_2"])
    put("conv_ssm_w", w["conv_ssm_w_2"][0].reshape(96, P))
    put("conv_ssm_b", w["conv_ssm_b_2"].reshape(24, P))
    put("ssm_norm", w["ssm_norm_2"].reshape(16, P))
    put("d_skip", np.repeat(w["d_skip_2"][0], 64).reshape(16, P))
    put("dt_bias", w["dt_bias_2"])
    put("a_log", w["a_log_2"])
    put("conv_ffn_w", w["conv_ffn_w_2"][0].reshape(132, P))
    put("conv_ffn_b", w["conv_ffn_b_2"].reshape(44, P))
    out[:, PARAM["rel_far"]:PARAM["rel_far"] + 16] = w["rel_bias_2"][31][None]
    return out


def shape_tables():
    out = np.zeros((P, TABLES), np.float32)

    def put(name, a):
        out[:a.shape[0], TABLE[name]:TABLE[name] + a.shape[1]] = a
    r, m = np.arange(P)[:, None], np.arange(P)[None]
    put("ident", np.eye(P))
    put("tri", (m >= r).astype(np.float32))
    sel = np.zeros((8, 8, P), np.float32)
    sel[np.arange(8), np.arange(8)] = 1
    put("sel", sel.reshape(8, -1))
    q, k = META + 384 + np.arange(P)[:, None], np.arange(T)[None]
    put("causal", np.where(k <= q, 0, NEG))
    seen = (k + 48) // 64 <= (q + 48) // 64
    slopes = 2.0 ** (-8.0 * np.arange(1, 5) / 4)
    put("alibi", np.concatenate([np.where(seen, -s * np.abs(q - k), NEG) for s in slopes], 1))
    gamma = 1 - 2.0 ** (-5.0 - np.arange(RET_HEADS))
    m = np.arange(SEQ)[None]
    put("decay", np.concatenate([np.where(r // 64 <= m // 64, g ** np.abs(m - r), 0) for g in gamma], 1))
    s = np.arange(META)[:, None]
    put("decay_meta", np.concatenate([g ** (META + m - s) for g in gamma], 1))
    dist = 511 - np.arange(640)
    n = np.maximum(dist, 0)
    large = 16 + (np.log(np.maximum(n, 1).astype(np.float32) / 16) / np.float32(math.log(8)) * 16).astype(np.int32)
    bucket = np.where(n < 16, n, np.minimum(large, 31))
    put("bucket", (np.arange(32)[:, None] == bucket[None]).astype(np.float32))
    return out


def kernel(**inputs):
    import concourse.bacc as _bacc
    from concourse.bass_utils import run_bass_kernel_spmd as _run

    w = {k: np.asarray(v) for k, v in inputs.items()}
    tokens = np.concatenate([w["meta_tokens"], w["x"][0]], 0)
    arrays = {
        "x_by_feature": np.ascontiguousarray(tokens.T.reshape(KT, P, T).transpose(1, 0, 2)),
        "weights": pack(w),
        "params": pack_params(w),
        "tables": shape_tables(),
        "lam": np.ascontiguousarray(np.broadcast_to(w["diff_lambda"].reshape(1, 256), (P, 256))),
        "w_uk": np.ascontiguousarray(w["w_uk_2"][0].reshape(8, P, P).transpose(1, 0, 2)),
        "w_uv": np.ascontiguousarray(w["w_uv_2"][0].transpose(2, 0, 1).reshape(P, 1024)),
        "rel": np.ascontiguousarray(w["rel_bias_2"]),
    }
    nc = _bacc.Bacc("TRN2", target_bir_lowering=False, num_devices=1)
    args = [nc.dram_tensor(f"in_{k}", a.shape, F32, kind="ExternalInput").ap() for k, a in arrays.items()]
    line = nc.dram_tensor("bias_line", (ATT_HEADS, 640), F32, kind="Internal").ap()
    skewed = nc.dram_tensor("bias_skewed", (ATT_HEADS, SKEW), F32, kind="Internal").ap()
    acum = nc.dram_tensor("acum_rows", (32, SEQ), F32, kind="Internal").ap()
    out = nc.dram_tensor("out", (P, KT, SEQ), F32, kind="ExternalOutput").ap()
    program(nc, *args, line, skewed, acum, out)
    r = _run(nc, [{f"in_{k}": a for k, a in arrays.items()}], core_ids=[0])
    return np.ascontiguousarray(r.results[0]["out"].transpose(2, 1, 0).reshape(1, SEQ, D))
```

```python
import math
from contextlib import ExitStack

import concourse.bass as bass
import numpy as np
from concourse import mybir

ALU = mybir.AluOpType
ACT = mybir.ActivationFunctionType
F32 = mybir.dt.float32
F32R = mybir.dt.float32r

P = 128
D = 1024
KT = D // P
META = 16
SEQ = 512
T = META + SEQ
HALF = T // 2
QT = SEQ // P
NEG = -1.0e30
FILL = -3.0e38
FIRST_MIN = 3.0e38
ALPHA = 4.0 ** 0.25
LN_EPS = 1e-5
RMS_EPS = 1e-6
LAM_INIT = 0.8 - 0.6 * math.exp(-0.3 * 0)

DIFF_HEADS, FOX_HEADS, RET_HEADS = 4, 8, 4
ATT_HEADS, IDX_HEADS = 16, 8
SSM_GROUPS, HEADS_PER_GROUP = 4, 8
FFN2 = 2816 // P

SKEW = 641 * P

RING = 4
AHEAD = RING - 1

STAGES = [("qk", 16), ("forget", 1), ("v", 8), ("even_out", 8),
          ("up0a", 16), ("down0a", 16), ("up0b", 16), ("down0b", 16)]
STAGES += [("ret0", 12), ("ret1", 12), ("ret_out0", 8), ("ret2", 12), ("ret3", 12), ("ret_out1", 8)]
STAGES += [("up1a", 16), ("down1a", 16), ("up1b", 16), ("down1b", 16)]
STAGES += [("latq", 8), ("latc", 1), ("idxq", 4), ("idxk", 1), ("idxw", 1), ("att_out", 8), ("gate_att", 8), ("dt", 1)]
STAGES += [("xs0", 6), ("xs1", 6), ("z0", 4), ("xs2", 6), ("so0", 4), ("z1", 4), ("xs3", 6), ("so1", 4), ("z2", 4)]
STAGES += [("z3", 4), ("so2", 4), ("gate_ssm", 8), ("so3", 4), ("mix_out", 8)]
STAGES += [s for g, n in enumerate((8, 8, 6)) for s in ((f"gv{g}", 2 * n), (f"fd{g}", 8))]
CHUNKS = dict(STAGES)
KGROUPS = {n: 2 for n in ("down0a", "down0b", "down1a", "down1b")}
FIRST_CHUNK, FIRST_TILE = {}, {}
_c = _t = 0
for _n, _k in STAGES:
    FIRST_CHUNK[_n], FIRST_TILE[_n] = _c, _t
    _c += _k
    _t += 2 * _k if _n.startswith("so") else _k // KGROUPS.get(_n, 1)
TOTAL_CHUNKS, TOTAL_TILES = _c, _t

PARAM = {}
_c = 0
for _n, _k in [("ln_g", 32), ("ln_b", 32), ("subln_g", 1), ("f_bias", 1), ("norm_mix", 8), ("norm_ffn", 8),
               ("norm_final", 8), ("kv_norm", 1), ("conv_ssm_w", 96), ("conv_ssm_b", 24), ("ssm_norm", 16),
               ("d_skip", 16), ("dt_bias", 1), ("a_log", 1), ("conv_ffn_w", 132), ("conv_ffn_b", 44),
               ("rel_far", 16)]:
    PARAM[_n] = _c
    _c += _k
PARAMS = _c


class Step:

    def __init__(self, start, i=0, stride=0):
        self.start, self.i, self.stride = start, i, stride

    def plus(self, k):
        return Step(self.start + k, self.i, self.stride)

    def over(self, n):
        assert self.stride % n == 0
        return Step(self.start // n, self.i, self.stride // n)

    def mod(self, n):
        assert self.stride % n == 0
        return self.start % n

    def at(self, factor=1, plus=0):
        fixed = self.start * factor + plus
        return fixed + self.i * (self.stride * factor) if self.stride else fixed


def loop(eng, n, unroll, body, peel=0, tail=0, chains=()):
    done = peel * unroll
    turns = (n - done) // unroll - tail
    for t in range(done):
        body(Step(t))
    if turns >= 2:
        before = [chain.count for chain, _ in chains]
        with eng.Fori(0, turns) as i:
            for chain, per_step in chains:
                chain.turn = i * (per_step * unroll)
            for j in range(unroll):
                body(Step(done + j, i, unroll))
        for (chain, per_step), first in zip(chains, before):
            assert chain.count == first + per_step * unroll
            chain.count, chain.turn = first + per_step * unroll * turns, 0
        done += turns * unroll
    for t in range(done, n):
        body(Step(t))


def wait(eng, sem, value):
    if not isinstance(value, int) or value > 0:
        eng.wait_ge(sem, value)


class Chain:

    def __init__(self, sem):
        self.sem, self.count, self.turn = sem, 0, 0

    def mark(self, ins):
        ins.then_inc(self.sem, 1)
        self.count += 1

    def settle(self, eng):
        eng.wait_ge(self.sem, self.turn + self.count)


def one(step):
    return bass.ds(step.at(), 1) if step.stride else slice(step.start, step.start + 1)


TABLE = {}
_c = 0
for _n, _k in [("ident", P), ("tri", P), ("sel", FOX_HEADS * P), ("causal", T), ("alibi", DIFF_HEADS * T),
               ("decay", RET_HEADS * SEQ), ("decay_meta", RET_HEADS * SEQ), ("bucket", 640)]:
    TABLE[_n] = _c
    _c += _k
TABLES = _c


def program(nc, x_in, weights, params, tables, lam_in, w_uk, w_uv, rel, line, skewed, acum_dram, merged_dram, out, until="end"):
    with ExitStack() as ctx:
        def sb(name, shape, dt=F32):
            return ctx.enter_context(nc.sbuf_tensor(name, shape, dt))

        def sem(name):
            return ctx.enter_context(nc.semaphore(name))

        raw = sb("raw", [P, RING, 8, P])
        w_hi = sb("w_hi", [P, RING, 8, P], F32R)
        w_lo = sb("w_lo", [P, RING, 8, P], F32R)
        x32 = sb("x32", [P, KT, T])
        x_hi = sb("x_hi", [P, KT, T], F32R)
        x_lo = sb("x_lo", [P, KT, T], F32R)
        ident = sb("ident", [P, P])
        ones_d = sb("ones_d", [P, P])
        ones_h = sb("ones_h", [P, P])
        ones_g = sb("ones_g", [P, P])
        par = sb("par", [P, PARAMS])
        small = sb("small", [P, 64])
        shared = nc.sbuf_base
        placed = {}

        def at(name, shape, dt=F32, start=None):
            off = placed["next"] if start is None else start
            off = (off + 31) // 32 * 32
            size = int(np.prod(shape[1:])) * 4
            assert off + size <= nc.sbuf_usable_end, (name, off + size, nc.sbuf_usable_end)
            placed["next"] = off + size
            return nc.alloc_sbuf_tensor_at(name, shape, dt, offset=off)

        ps = ctx.enter_context(nc.psum_tensor("ps", [P, 8, 512], F32))
        flat = ps[:, :, :].rearrange("p b n -> p (b n)")

        def bank(b, n=1024, rows=slice(0, P)):
            return flat[rows, b * 512:b * 512 + n]

        landed = [sem(f"landed{s}") for s in range(RING)]
        hi_ready = sem("hi_ready")
        lo_ready = sem("lo_ready")
        chunk_done = sem("chunk_done")
        evicted = [sem(f"evicted{s}") for s in range(2)]
        dve_own, act_own, pool_own = sem("dve_own"), sem("act_own"), sem("pool_own")
        dve_chain, act_chain, pool_chain = Chain(dve_own), Chain(act_own), Chain(pool_own)
        loaded = sem("loaded")

        def tiles_out(eng, tile):
            for s in range(2):
                wait(eng, evicted[s], (tile - s + 1) // 2)

        def stream_weights(sp):
            def body(g):
                s = g.mod(RING)
                wait(sp, lo_ready, g.at(plus=1 - RING))
                src = weights[one(g), :, :].rearrange("g p n -> p (g n)")
                sp.dma_start(raw[:, s, :, :].rearrange("p k n -> p (k n)"), src).then_inc(landed[s], 16)
            loop(sp, TOTAL_CHUNKS, RING, body, peel=1)

        def split_hi(act, g):
            if not g.stride and g.start >= TOTAL_CHUNKS:
                return
            s = g.mod(RING)
            act.wait_ge(landed[s], g.over(RING).at(16, 16))
            wait(act, chunk_done, g.at(plus=1 - RING))
            nc.scalar.activation(w_hi[:, s], raw[:, s], ACT.Copy).then_inc(hi_ready, 1)

        def split_lo(dve, g):
            if not g.stride and g.start >= TOTAL_CHUNKS:
                return
            s = g.mod(RING)
            dve.wait_ge(hi_ready, g.at(plus=1))
            nc.vector.tensor_tensor(w_lo[:, s], raw[:, s], w_hi[:, s], ALU.subtract).then_inc(lo_ready, 1)

        def tile_out(tile, wide):
            s = tile.mod(2)
            return ps[:, 2 * s:2 * s + 2, 0:HALF] if wide else ps[:, 2 * s:2 * s + 1, 0:SEQ]

        def halves(ap, wide):
            return ap[:, 0:T].rearrange("p (h n) -> p h n", h=2) if wide else ap[:, META:T].rearrange("p (h n) -> p h n", h=1)

        def chunk_products(pe, name, t, act_hi, act_lo, wide, nk=8, k0=0, start=True, stop=True, ready=None):
            kg = KGROUPS.get(name, 1)
            g = t.plus(FIRST_CHUNK[name])
            tile = t.over(kg).plus(FIRST_TILE[name])
            s = g.mod(RING)
            pe.wait_ge(lo_ready, g.at(plus=1))
            if start:
                wait(pe, evicted[tile.mod(2)], tile.over(2).at())
            o = tile_out(tile, wide)
            parts = [(h, slice(h * HALF, (h + 1) * HALF)) for h in range(2)] if wide else [(0, slice(META, T))]
            for k in range(nk):
                if ready:
                    pe.wait_ge(ready[0], ready[1] + k0 + k + 1)
                for n, (w, a) in enumerate(((w_hi, act_hi), (w_hi, act_lo), (w_lo, act_hi))):
                    for h, cols in parts:
                        last = nc.tensor.matmul(o[:, h, :], w[:, s, k], a[:, k0 + k, cols],
                                                start=start and k == 0 and n == 0, stop=stop and k == nk - 1 and n == 2)
            last.then_inc(chunk_done, 1)

        def pe_stage(pe, name, act_hi, act_lo, wide, ready=None, after=None):
            kg = KGROUPS.get(name, 1)

            def body(t):
                c = t.mod(kg) if kg > 1 else 0
                first = not t.stride and t.start < kg
                chunk_products(pe, name, t, act_hi, act_lo, wide, k0=8 * c, start=c == 0, stop=c == kg - 1,
                               ready=ready if first else None)
                if after and c == kg - 1:
                    after(t.over(kg).plus(-1))
            loop(pe, CHUNKS[name], 4, body, peel=1 if ready or after or FIRST_CHUNK[name] == 0 else 0)

        def side_stage(eng, split, name, evict, chains=(), peel=0, unroll=4):
            kg = KGROUPS.get(name, 1)
            last = FIRST_CHUNK[name] + CHUNKS[name] + AHEAD > TOTAL_CHUNKS

            def body(t):
                split(eng, t.plus(FIRST_CHUNK[name] + AHEAD))
                if t.mod(kg) == kg - 1 and evict:
                    evict(t.over(kg), t.plus(FIRST_CHUNK[name]).at(plus=1))
            loop(eng, CHUNKS[name], unroll, body, peel=max(peel, FIRST_CHUNK[name] == 0), tail=1 if last else 0,
                 chains=chains)

        placed["next"] = shared
        qk = at("qk", [P, 16, T])
        vt = at("vt", [P, 5, D])
        diff_o = at("diff_o", [P, DIFF_HEADS, T])
        alibi = at("alibi", [P, DIFF_HEADS, T])
        causal = at("causal", [P, T])
        sel = at("sel", [FOX_HEADS, FOX_HEADS, P])
        cum_f = at("cum_f", [FOX_HEADS, T])
        neg_cum = at("neg_cum", [FOX_HEADS, T])
        work = placed["next"]
        v_slot = at("v_slot", [P, 2, T])
        f_row = at("f_row", [FOX_HEADS, 4, T])
        s_buf = at("s_buf", [P, 4, T], start=work)
        p_norm = at("p_norm", [P, 3, T])
        p_turn = at("p_turn", [P, 2, 5, P])
        stat = at("stat", [P, 4, 64])
        lam_row = at("lam_row", [P, 4, 64])
        even_end = placed["next"]

        products = [("a", h, j) for h in range(DIFF_HEADS) for j in range(5)]
        products += [("b", h, j) for h in range(FOX_HEADS) for j in range(5)]
        maps = {}
        for p, (kind, h, j) in enumerate(products):
            n = sum(len(m) for m in maps.values())
            maps[p] = [n, n + 1] if kind == "a" else [n]
        NPROD = len(products)
        product_of = {u: p for p in maps for u in maps[p]}
        v_turned, v_stored = sem("v_turned"), sem("v_stored")
        scored, masked, expd, normed = sem("scored"), sem("masked"), sem("expd"), sem("normed")
        turned, turn_kept, weighed = sem("turned"), sem("turn_kept"), sem("weighed")
        head_hi, head_lo = sem("head_hi"), sem("head_lo")
        forget_in, forget_ready, lam_ready = sem("forget_in"), sem("forget_ready"), sem("lam_ready")

        def q_rows(j):
            return (0, META) if j == 0 else (META + (j - 1) * P, P)

        def keys_of(j):
            return META if j == 0 else META + j * P

        def even_loads(pool):
            for dst, src in ((x32[:, :, :], x_in), (par[:], params), (ident[:], tables[:, 0:P]),
                             (alibi[:].rearrange("p h n -> p (h n)"), tables[:, TABLE["alibi"]:TABLE["alibi"] + 4 * T]),
                             (causal[:], tables[:, TABLE["causal"]:TABLE["causal"] + T]),
                             (sel[:].rearrange("p h n -> p (h n)"), tables[0:8, TABLE["sel"]:TABLE["sel"] + 8 * P]),
                             (lam_row[:].rearrange("p a n -> p (a n)"), lam_in)):
                pool.dma_start(dst, src).then_inc(loaded, 16)
            nc.gpsimd.memset(ones_d[:], 1.0 / D).then_inc(forget_in, 1)
            nc.gpsimd.memset(ones_h[:], 1.0 / P).then_inc(forget_in, 1)
            nc.gpsimd.memset(ones_g[:], 1.0 / 512).then_inc(forget_in, 1)
            nc.gpsimd.memset(f_row[:, 3, :], 1.0).then_inc(forget_in, 1)

        LOADS = 7 * 16
        x_split_hi, x_split_lo = sem("x_split_hi"), sem("x_split_lo")

        def even_act_start(act):
            act.wait_ge(loaded, LOADS)
            for k in range(KT):
                nc.scalar.activation(x_hi[:, k], x32[:, k], ACT.Copy).then_inc(x_split_hi, 1)
            for g in range(AHEAD):
                split_hi(act, Step(g))

        def even_dve_start(dve):
            dve.wait_ge(loaded, LOADS)
            for k in range(KT):
                dve.wait_ge(x_split_hi, k + 1)
                nc.vector.tensor_tensor(x_lo[:, k], x32[:, k], x_hi[:, k], ALU.subtract).then_inc(x_split_lo, 1)
            for g in range(AHEAD):
                split_lo(dve, Step(g))

        def qk_act(act):
            def keep(tile, done):
                act.wait_ge(chunk_done, done)
                nc.scalar.activation(halves(qk[:, one(tile)].rearrange("p a n -> p (a n)"), True),
                                     tile_out(tile.plus(FIRST_TILE["qk"]), True), ACT.Copy,
                                     scale=0.125 if tile.mod(8) < 4 else 1.0) \
                    .then_inc(evicted[tile.mod(2)], 1)
            side_stage(act, split_hi, "qk", keep, unroll=8, peel=0)

        def forget_act(act):
            tile = Step(FIRST_TILE["forget"])
            split_hi(act, Step(FIRST_CHUNK["forget"] + AHEAD))
            act.wait_ge(chunk_done, FIRST_CHUNK["forget"] + 1)
            bias = par[0:8, PARAM["f_bias"]:PARAM["f_bias"] + 1]
            act_chain.mark(nc.scalar.activation(halves(f_row[:, 0], True), tile_out(tile, True)[0:8], ACT.Identity, bias=bias))
            act_chain.settle(act)
            nc.scalar.activation(f_row[:, 1], f_row[:, 0], ACT.Abs).then_inc(evicted[tile.mod(2)], 1)
            act.wait_ge(evicted[tile.mod(2)], tile.start // 2 + 1)
            act_chain.mark(nc.scalar.activation(f_row[:, 1], f_row[:, 1], ACT.Exp, scale=-1.0))
            act_chain.settle(act)
            nc.scalar.activation(f_row[:, 2], f_row[:, 1], ACT.Ln, bias=1.0).then_inc(forget_in, 1)

        def forget_dve(dve):
            split_lo(dve, Step(FIRST_CHUNK["forget"] + AHEAD))
            dve.wait_ge(forget_in, 5)
            dve_chain.mark(nc.vector.tensor_scalar(f_row[:, 1], f_row[:, 0], 0.0, None, ALU.min))
            dve_chain.settle(dve)
            dve_chain.mark(nc.vector.tensor_tensor(f_row[:, 2], f_row[:, 1], f_row[:, 2], ALU.subtract))
            dve_chain.settle(dve)
            dve_chain.mark(nc.vector.tensor_tensor_scan(cum_f[:], f_row[:, 3], f_row[:, 2], 0.0, ALU.mult, ALU.add))
            dve_chain.settle(dve)
            nc.vector.tensor_scalar(neg_cum[:], cum_f[:], -1.0, None, ALU.mult).then_inc(forget_ready, 1)

        def v_act(act):
            def keep(tile, done):
                act.wait_ge(chunk_done, done)
                wait(act, v_turned, tile.at(plus=-1))
                nc.scalar.activation(halves(v_slot[:, tile.mod(2)], True), tile_out(tile.plus(FIRST_TILE["v"]), True),
                                     ACT.Copy).then_inc(evicted[tile.plus(FIRST_TILE["v"]).mod(2)], 1)
            side_stage(act, split_hi, "v", keep, peel=1)

        def v_pe(pe):
            def turn(t):
                tile = FIRST_TILE["v"] + t
                pe.wait_ge(evicted[tile % 2], tile // 2 + 1)
                wait(pe, v_stored, t)
                for b in range(5):
                    c, n = q_rows(b)
                    o = 2048 + (512 if b == 0 else (b - 1) * P)
                    last = nc.tensor.transpose(flat[0:n, o:o + P], v_slot[:, t % 2, c:c + n], ident[:, :])
                last.then_inc(v_turned, 1)
            pe.wait_ge(loaded, LOADS)
            for t in range(8):
                chunk_products(pe, "v", Step(t), x_hi, x_lo, True)
                if t:
                    turn(t - 1)
            turn(7)

        def v_dve(dve):
            for t in range(8):
                split_lo(dve, Step(FIRST_CHUNK["v"] + t + AHEAD))
                dve.wait_ge(v_turned, t + 1)
                nc.vector.tensor_copy(vt[:, 1:5, t * P:(t + 1) * P], bank(4, 512).rearrange("p (b n) -> p b n", b=4))
                nc.vector.tensor_copy(vt[0:META, 0, t * P:(t + 1) * P], flat[0:META, 2560:2560 + P]).then_inc(v_stored, 1)

        def lam_dve(dve):
            for m in range(2):
                dve_chain.mark(nc.vector.tensor_tensor_reduce(lam_row[:, 2 * m], lam_row[:, 2 * m], lam_row[:, 2 * m + 1], 1.0, 0.0,
                                                              ALU.mult, ALU.add, small[:, m:m + 1]))
            dve_chain.settle(dve)
            nc.vector.tensor_scalar(small[:, 8:10], small[:, 0:2], 1.0, None, ALU.mult).then_inc(lam_ready, 1)
            dve.wait_ge(lam_ready, 2)
            dve_chain.mark(nc.vector.tensor_tensor(small[:, 4:5], small[:, 3:4], small[:, 2:3], ALU.subtract))
            dve_chain.settle(dve)
            dve_chain.mark(nc.vector.tensor_scalar(small[:, 4:5], small[:, 4:5], -LAM_INIT, None, ALU.add))
            g = PARAM["subln_g"]
            dve_chain.mark(nc.vector.tensor_scalar(small[:, 5:6], par[:, g:g + 1], 1.0 - LAM_INIT, None, ALU.mult))
            dve_chain.settle(dve)

        def lam_act(act):
            act.wait_ge(lam_ready, 1)
            nc.scalar.activation(small[:, 2:4], small[:, 8:10], ACT.Exp).then_inc(lam_ready, 1)

        def even_scores(pe, p):
            kind, h, j = products[p]
            (c, n), keys = q_rows(j), keys_of(j)
            for m, u in enumerate(maps[p]):
                if u >= 2:
                    pe.wait_ge(masked, u - 1)
                o = (u % 2) * 1024
                if kind == "a":
                    rows, qt, kt_ = slice(64 * m, 64 * m + 64), h, 4 + h
                else:
                    rows, qt, kt_ = slice(64 * (h % 2), 64 * (h % 2) + 64), 8 + h // 2, 12 + h // 2
                for a in range(0, keys, 512):
                    b = min(keys, a + 512)
                    last = nc.tensor.matmul(flat[0:n, o + a:o + b], qk[rows, qt, c:c + n], qk[rows, kt_, a:b],
                                            start=True, stop=kind == "a")
                    if kind == "b":
                        for e in range(a, b, P):
                            f = min(b, e + P)
                            nc.tensor.matmul(flat[0:n, o + e:o + f], cum_f[:, c:c + n], sel[:, h, 0:f - e],
                                             start=False, stop=False, skip_group_check=True)
                        last = nc.tensor.matmul(flat[0:n, o + a:o + b], sel[:, h, 0:n], neg_cum[:, a:b], start=False, stop=True)
                last.then_inc(scored, 1)

        def even_mask(dve, p):
            kind, h, j = products[p]
            (c, n), keys = q_rows(j), keys_of(j)
            f0 = 400 if j == 0 else 528 - keys
            for u in maps[p]:
                bias = (alibi[0:n, h] if kind == "a" else causal[0:n])[:, f0:f0 + keys]
                dve.wait_ge(scored, u + 1)
                if u >= 4:
                    dve.wait_ge(normed, product_of[u - 4] + 1)
                nc.vector.tensor_tensor_reduce(s_buf[0:n, u % 4, 0:keys], bank((u % 2) * 2, keys, slice(0, n)), bias, -1.0,
                                               FIRST_MIN, ALU.add, ALU.min, stat[0:n, 0, u % 64:u % 64 + 1]).then_inc(masked, 1)

        def even_exp(act, p):
            kind, h, j = products[p]
            n, keys = q_rows(j)[1], keys_of(j)
            for u in maps[p]:
                act.wait_ge(masked, u + 1)
                s = s_buf[0:n, u % 4, 0:keys]
                nc.scalar.activation(s, s, ACT.Exp, scale=-1.0, bias=stat[0:n, 0, u % 64:u % 64 + 1],
                                     accum_out=stat[0:n, 1, u % 64:u % 64 + 1]).then_inc(expd, 1)

        def even_norm(dve, p):
            kind, h, j = products[p]
            n, keys = q_rows(j)[1], keys_of(j)
            dve.wait_ge(expd, maps[p][-1] + 1)
            for u in maps[p]:
                q = u % 64
                dve_chain.mark(nc.vector.reciprocal(stat[0:n, 2, q:q + 1], stat[0:n, 1, q:q + 1]))
            dve_chain.settle(dve)
            if p >= 3:
                dve.wait_ge(turned, p - 2)
            q = maps[p][0] % 64
            o = p_norm[0:n, p % 3, 0:keys]
            ins = nc.vector.tensor_scalar(o, s_buf[0:n, maps[p][0] % 4, 0:keys], stat[0:n, 2, q:q + 1], None, ALU.mult)
            if kind == "a":
                dve_chain.mark(ins)
                dve_chain.mark(nc.vector.tensor_scalar(stat[0:n, 3, q:q + 1], stat[0:n, 2, q + 1:q + 2], small[0:n, 4:5], None, ALU.mult))
                dve_chain.settle(dve)
                ins = nc.vector.scalar_tensor_tensor(o, s_buf[0:n, maps[p][1] % 4, 0:keys], stat[0:n, 3, q:q + 1], o, ALU.mult, ALU.add)
            ins.then_inc(normed, 1)

        def even_turn(pe, p):
            n, j = q_rows(products[p][2])[1], products[p][2]
            pe.wait_ge(normed, p + 1)
            if p:
                pe.wait_ge(turn_kept, p)
            for b in range(j + 1):
                c, k = q_rows(b)
                o = 2048 + (512 if b == 0 else (b - 1) * P)
                last = nc.tensor.transpose(flat[0:k, o:o + n], p_norm[0:n, p % 3, c:c + k], ident[0:n, 0:n])
            last.then_inc(turned, 1)

        def even_keep_turned(act, p):
            n, j = q_rows(products[p][2])[1], products[p][2]
            act.wait_ge(turned, p + 1)
            if p >= 2:
                act.wait_ge(weighed, p - 1)
            if j:
                nc.scalar.activation(p_turn[:, p % 2, 0:j, :], bank(4, j * P).rearrange("p (b n) -> p b n", b=j), ACT.Copy)
            nc.scalar.activation(p_turn[0:META, p % 2, 4, 0:n], flat[0:META, 2560:2560 + n], ACT.Copy).then_inc(turn_kept, 1)

        def groups_before(p):
            return sum(1 for q in range(p) if ends_group(q))

        def ends_group(p):
            kind, h, j = products[p]
            return j == 4 and (kind == "a" or h % 2 == 1)

        def even_values(pe, p):
            kind, h, j = products[p]
            c, n = q_rows(j)
            pe.wait_ge(turn_kept, p + 1)
            done = groups_before(p)
            if done and (p == 0 or ends_group(p - 1)):
                pe.wait_ge(head_hi, done)
                wait(pe, head_lo, done - DIFF_HEADS)
            rows = slice(0, P) if kind == "a" else slice(64 * (h % 2), 64 * (h % 2) + 64)
            col = h * P if kind == "a" else 512 + h * 64
            wide = P if kind == "a" else 64
            o = 3072 + (512 if j == 0 else (j - 1) * P)
            for b in range(j + 1):
                k = q_rows(b)[1]
                last = nc.tensor.matmul(flat[rows, o:o + n], vt[0:k, b, col:col + wide],
                                        p_turn[0:k, p % 2, 4 if b == 0 else b - 1, 0:n], start=b == 0, stop=b == j)
            last.then_inc(weighed, 1)

        def even_keep_head(act, p):
            kind, h, j = products[p]
            if not ends_group(p):
                return
            act.wait_ge(weighed, p + 1)
            dst = diff_o[:, h] if kind == "a" else x_hi[:, 4 + h // 2]
            nc.scalar.activation(dst[:, META:T], bank(6, 512), ACT.Copy)
            nc.scalar.activation(dst[:, 0:META], bank(7, META), ACT.Copy).then_inc(head_hi, 1)

        def even_head_lo(dve, p):
            kind, h, j = products[p]
            if not ends_group(p) or kind == "a":
                return
            k = 4 + h // 2
            dve.wait_ge(head_hi, groups_before(p) + 1)
            nc.vector.tensor_tensor(x_lo[:, k, META:T], bank(6, 512), x_hi[:, k, META:T], ALU.subtract)
            nc.vector.tensor_tensor(x_lo[:, k, 0:META], bank(7, META), x_hi[:, k, 0:META], ALU.subtract).then_inc(head_lo, 1)

        def even_attention_pe(pe):
            pe.wait_ge(forget_ready, 1)
            pe.wait_ge(v_stored, 8)
            tiles_out(pe, FIRST_TILE["even_out"])
            for p in range(NPROD + 3):
                if p < NPROD:
                    even_scores(pe, p)
                if 2 <= p < NPROD + 2:
                    even_turn(pe, p - 2)
                if 3 <= p:
                    even_values(pe, p - 3)
            pe.wait_ge(head_sq, 1)
            pe.wait_ge(head_lo, 4)
            for h in range(DIFF_HEADS):
                nc.tensor.matmul(bank(2 * h, 512), ones_h[:], diff_sq[:, h, META:T], start=True, stop=True)
                nc.tensor.matmul(bank(2 * h + 1, META), ones_h[:], diff_sq[:, h, 0:META], start=True, stop=True).then_inc(head_mean, 1)

        head_sq, head_mean, head_var, head_root, head_t, diff_hi_s, diff_lo_s = (
            sem(n) for n in ("head_sq", "head_mean", "head_var", "head_root", "head_t", "diff_hi", "diff_lo"))
        diff_sq = nc.alloc_sbuf_tensor_at("diff_sq", [P, DIFF_HEADS, T], F32, offset=shared)
        diff_rt = nc.alloc_sbuf_tensor_at("diff_rt", [P, DIFF_HEADS, T], F32, offset=shared + DIFF_HEADS * T * 4)

        def even_attention_act(act):
            lam_act(act)
            for p in range(NPROD + 4):
                if p < NPROD:
                    even_exp(act, p)
                if 2 <= p < NPROD + 2:
                    even_keep_turned(act, p - 2)
                if 4 <= p:
                    even_keep_head(act, p - 4)
            act.wait_ge(weighed, NPROD)
            nc.scalar.activation(diff_sq[:], diff_o[:], ACT.Square).then_inc(head_sq, 1)
            for h in range(DIFF_HEADS):
                act.wait_ge(head_var, h + 1)
                nc.scalar.activation(diff_rt[:, h], diff_rt[:, h], ACT.Sqrt).then_inc(head_root, 1)
            for h in range(DIFF_HEADS):
                act.wait_ge(head_t, h + 1)
                nc.scalar.activation(x_hi[:, h], diff_o[:, h], ACT.Copy).then_inc(diff_hi_s, 1)

        def even_attention_dve(dve):
            lam_dve(dve)
            for p in range(NPROD + 4):
                if p < NPROD:
                    even_mask(dve, p)
                if 1 <= p < NPROD + 1:
                    even_norm(dve, p - 1)
                if 4 <= p:
                    even_head_lo(dve, p - 4)
            for h in range(DIFF_HEADS):
                dve.wait_ge(head_mean, h + 1)
                nc.vector.tensor_scalar(diff_rt[:, h, META:T], bank(2 * h, 512), RMS_EPS, None, ALU.add)
                nc.vector.tensor_scalar(diff_rt[:, h, 0:META], bank(2 * h + 1, META), RMS_EPS, None, ALU.add).then_inc(head_var, 1)
            for h in range(DIFF_HEADS):
                dve.wait_ge(head_root, h + 1)
                dve_chain.mark(nc.vector.reciprocal(diff_rt[:, h], diff_rt[:, h]))
                dve_chain.settle(dve)
                nc.vector.scalar_tensor_tensor(diff_o[:, h], diff_o[:, h], small[:, 5:6], diff_rt[:, h], ALU.mult, ALU.mult).then_inc(head_t, 1)
            for h in range(DIFF_HEADS):
                dve.wait_ge(diff_hi_s, h + 1)
                nc.vector.tensor_tensor(x_lo[:, h], diff_o[:, h], x_hi[:, h], ALU.subtract).then_inc(diff_lo_s, 1)

        def residual_dve(dve, name, wide, factor):
            def add(tile, done):
                dve.wait_ge(chunk_done, done)
                o = halves(x32[:, one(tile)].rearrange("p a n -> p (a n)"), wide)
                u = tile.plus(FIRST_TILE[name])
                nc.vector.scalar_tensor_tensor(o, o, factor, tile_out(u, wide), ALU.mult, ALU.add).then_inc(evicted[u.mod(2)], 1)
            side_stage(dve, split_lo, name, add)

        def only_split(eng, split, name):
            side_stage(eng, split, name, None)

        norms = {"all": 0, "layer": 0}
        norm_mean, norm_less, norm_squared, norm_var, norm_veps, norm_root, norm_scaled, norm_y, norm_hi, norm_lo = (
            sem(f"norm_{n}") for n in ("mean", "less", "squared", "var", "veps", "root", "scaled", "y", "hi", "lo"))
        mlp_squared, mlp_hi, mlp_lo = (sem(f"mlp_{n}") for n in ("squared", "hi", "lo"))

        class Norm:

            def __init__(self, name, tile, wide, g, b=None, eps=LN_EPS, start=None, last=False):
                self.last = last
                self.name, self.tile, self.wide, self.g, self.b, self.eps = name, tile, wide, g, b, eps
                self.c0 = 0 if wide else META
                placed["next"] = shared if start is None else start
                self.xc = at(name + "_xc", [P, KT, T])
                self.sq = at(name + "_sq", [P, KT, T])
                self.rt = at(name + "_rt", [P, T])
                self.n = norms["all"]
                self.nl = norms["layer"]
                norms["all"] += 1
                norms["layer"] += b is not None
                self.hi_before = KT * self.n
                self.ready = (norm_lo, KT * self.n)
                self.lo_at = KT * (self.n + 1)
                self.y = x32 if b is not None else self.xc

            def cols(self):
                return [(META, T, 0)] + ([(0, META, 512)] if self.wide else [])

            def add_mean(self, pe, k):
                if not k.stride and k.start < 0:
                    return
                u = k.plus(self.tile - KT)
                pe.wait_ge(evicted[u.mod(2)], u.over(2).at(plus=1))
                for a, b, o in self.cols():
                    last = nc.tensor.matmul(flat[:, 2048 + o:2048 + o + b - a], ones_d[:],
                                            x32[:, one(k), a:b].rearrange("p k n -> p (k n)"),
                                            start=not k.stride and k.start == 0, stop=not k.stride and k.start == KT - 1,
                                            skip_group_check=True)
                return last

            def pe(self, pe):
                if self.b is not None:
                    self.add_mean(pe, Step(KT - 1)).then_inc(norm_mean, 1)
                for k in range(KT):
                    pe.wait_ge(norm_squared, KT * self.n + k + 1)
                    for a, b, o in self.cols():
                        last = nc.tensor.matmul(flat[:, 3072 + o:3072 + o + b - a], ones_d[:], self.sq[:, k, a:b],
                                                start=k == 0, stop=k == KT - 1)
                last.then_inc(norm_var, 1)

            def dve(self, dve):
                xc = self.xc if self.b is not None else x32
                if self.b is not None:
                    dve.wait_ge(norm_mean, self.nl + 1)
                    for k in range(KT):
                        for a, b, o in self.cols():
                            last = nc.vector.tensor_tensor(xc[:, k, a:b], x32[:, k, a:b], flat[:, 2048 + o:2048 + o + b - a], ALU.subtract)
                        last.then_inc(norm_less, 1)
                dve.wait_ge(norm_var, self.n + 1)
                for a, b, o in self.cols():
                    last = nc.vector.tensor_scalar(self.rt[:, a:b], flat[:, 3072 + o:3072 + o + b - a], self.eps, None, ALU.add)
                last.then_inc(norm_veps, 1)
                dve.wait_ge(norm_root, self.n + 1)
                dve_chain.mark(nc.vector.reciprocal(self.rt[:, self.c0:T], self.rt[:, self.c0:T]))
                dve_chain.settle(dve)
                for k in range(KT + 2):
                    if k < KT:
                        o, i = self.xc[:, k, self.c0:T], xc[:, k, self.c0:T]
                        if self.b is not None:
                            ins = nc.vector.tensor_tensor(o, i, self.rt[:, self.c0:T], ALU.mult)
                        else:
                            ins = nc.vector.scalar_tensor_tensor(o, i, par[:, self.g + k:self.g + k + 1], self.rt[:, self.c0:T],
                                                                 ALU.mult, ALU.mult)
                        ins.then_inc(norm_scaled, 1)
                    if k >= 2 and not self.last:
                        j = k - 2
                        dve.wait_ge(norm_hi, self.hi_before + j + 1)
                        nc.vector.tensor_tensor(x_lo[:, j, self.c0:T], self.y[:, j, self.c0:T], x_hi[:, j, self.c0:T], ALU.subtract).then_inc(norm_lo, 1)

            def act(self, act):
                src = self.xc if self.b is not None else x32
                if self.b is None:
                    tiles_out(act, self.tile)
                    wait(act, norm_y, KT * self.nl)
                for k in range(KT):
                    if self.b is not None:
                        act.wait_ge(norm_less, KT * self.nl + k + 1)
                    nc.scalar.activation(self.sq[:, k, self.c0:T], src[:, k, self.c0:T], ACT.Square).then_inc(norm_squared, 1)
                act.wait_ge(norm_veps, self.n + 1)
                nc.scalar.activation(self.rt[:, self.c0:T], self.rt[:, self.c0:T], ACT.Sqrt).then_inc(norm_root, 1)
                for k in range(KT):
                    act.wait_ge(norm_scaled, KT * self.n + k + 1)
                    o, i = self.y[:, k, self.c0:T], self.xc[:, k, self.c0:T]
                    if self.b is not None:
                        nc.scalar.activation(o, i, ACT.Identity, scale=par[:, self.g + k:self.g + k + 1],
                                             bias=par[:, self.b + k:self.b + k + 1]).then_inc(norm_y, 1)
                        act.wait_ge(norm_y, KT * self.nl + k + 1)
                    if not self.last:
                        nc.scalar.activation(x_hi[:, k, self.c0:T], o, ACT.Copy).then_inc(norm_hi, 1)

        class Mlp:

            def __init__(self, layer, wide):
                self.layer, self.wide = layer, wide
                placed["next"] = shared
                self.h_hi = at(f"h_hi{layer}", [P, 16, T], F32R)
                self.h_lo = at(f"h_lo{layer}", [P, 16, T], F32R)
                self.pos = at(f"h_pos{layer}", [P, 2, T])
                self.sq = at(f"h_sq{layer}", [P, 2, T])

            def pe(self, pe, norm, next_norm):
                for half, hn in enumerate("ab"):
                    pe_stage(pe, f"up{self.layer}{hn}", x_hi, x_lo, self.wide, ready=None if half else norm.ready)
                    pe_stage(pe, f"down{self.layer}{hn}", self.h_hi, self.h_lo, self.wide,
                             ready=(mlp_lo, 32 * self.layer + 16 * half),
                             after=(lambda k: next_norm.add_mean(pe, k)) if half else None)

            def act(self, act):
                for half, hn in enumerate("ab"):
                    name = f"up{self.layer}{hn}"

                    def keep(tile, done):
                        u = tile.plus(FIRST_TILE[name])
                        act.wait_ge(chunk_done, done)
                        wait(act, mlp_squared, tile.at(plus=32 * self.layer + 16 * half - 1))
                        nc.scalar.activation(halves(self.pos[:, tile.mod(2)], self.wide), tile_out(u, self.wide), ACT.Relu) \
                            .then_inc(evicted[u.mod(2)], 1)
                        act.wait_ge(mlp_squared, tile.at(plus=32 * self.layer + 16 * half + 1))
                        nc.scalar.activation(halves(self.h_hi[:, one(tile)].rearrange("p a n -> p (a n)"), self.wide),
                                             halves(self.sq[:, tile.mod(2)], self.wide), ACT.Copy).then_inc(mlp_hi, 1)
                    side_stage(act, split_hi, name, keep, peel=int(self.layer == half == 0))
                    only_split(act, split_hi, f"down{self.layer}{hn}")

            def dve(self, dve):
                for half, hn in enumerate("ab"):
                    name = f"up{self.layer}{hn}"

                    def keep(tile, done):
                        u = tile.plus(FIRST_TILE[name])
                        dve.wait_ge(evicted[u.mod(2)], u.over(2).at(plus=1))
                        pos = halves(self.pos[:, tile.mod(2)], self.wide)
                        sq = halves(self.sq[:, tile.mod(2)], self.wide)
                        nc.vector.tensor_tensor(sq, pos, pos, ALU.mult).then_inc(mlp_squared, 1)
                        dve.wait_ge(mlp_hi, tile.at(plus=32 * self.layer + 16 * half + 1))
                        row = one(tile)
                        nc.vector.tensor_tensor(halves(self.h_lo[:, row].rearrange("p a n -> p (a n)"), self.wide), sq,
                                                halves(self.h_hi[:, row].rearrange("p a n -> p (a n)"), self.wide), ALU.subtract) \
                            .then_inc(mlp_lo, 1)
                    side_stage(dve, split_lo, name, keep)
                    residual_dve(dve, f"down{self.layer}{hn}", self.wide, ALPHA if half == 0 else 1.0)

        ln00 = Norm("ln00", FIRST_TILE["up0a"], True, PARAM["ln_g"], PARAM["ln_b"])
        mlp0 = Mlp(0, True)
        ln01 = Norm("ln01", FIRST_TILE["ret0"], True, PARAM["ln_g"] + 8, PARAM["ln_b"] + 8)

        placed["next"] = shared
        ret_hi = at("ret_hi", [P, 8, T], F32R)
        ret_lo = at("ret_lo", [P, 8, T], F32R)
        rq = at("rq", [P, 2, T])
        rk = at("rk", [P, 2, T])
        rv_slot = at("rv_slot", [P, 2, T])
        rv = at("rv", [P, 5, 512])
        decayed = at("decayed", [P, 5, SEQ])
        ro = at("ro", [P, 4, SEQ])
        rg = at("rg", [P, 4, SEQ])
        rsq = at("rsq", [P, 4, SEQ])
        decay = at("decay", [P, SEQ])
        decay_meta = at("decay_meta", [META, SEQ])
        ret_rt = at("ret_rt", [P, SEQ])
        (decay_in, rv_turned, rv_stored, ret_scored, ret_decayed, ret_weighed, ret_squared, ret_copied, ret_var, ret_veps,
         ret_root, ret_gated, ret_hi_s, ret_lo_s) = (
            sem(n) for n in ("decay_in", "rv_turned", "rv_stored", "ret_scored", "ret_decayed", "ret_weighed", "ret_squared",
                             "ret_copied", "ret_var", "ret_veps", "ret_root", "ret_gated", "ret_hi_s", "ret_lo_s"))

        def ret_loads(pool):
            for h in range(RET_HEADS):
                if h == 0:
                    pool.wait_ge(norm_lo, ln01.lo_at)
                else:
                    pool.wait_ge(ret_decayed, 5 * h)
                a, b = TABLE["decay"] + h * SEQ, TABLE["decay_meta"] + h * SEQ
                pool.dma_start(decay[:], tables[:, a:a + SEQ]).then_inc(decay_in, 16)
                pool.dma_start(decay_meta[:], tables[0:META, b:b + SEQ]).then_inc(decay_in, 16)

        def ret_pe(pe, h):
            name = f"ret{h}"
            for c in range(12):
                chunk_products(pe, name, Step(c), x_hi, x_lo, 2 <= c < 8, ready=ln01.ready if h == c == 0 else None)
                if 5 <= c < 9:
                    t = c - 5
                    u = FIRST_TILE[name] + 4 + t
                    pe.wait_ge(evicted[u % 2], u // 2 + 1)
                    wait(pe, rv_stored, 4 * h + t)
                    if t == 0:
                        wait(pe, ret_decayed, 5 * h)
                        wait(pe, ret_veps, h)
                    for b in range(5):
                        c0, n = q_rows(b)
                        o = 2048 + (512 if b == 0 else (b - 1) * P)
                        last = nc.tensor.transpose(flat[0:n, o:o + P], rv_slot[:, t % 2, c0:c0 + n], ident[:, :])
                    last.then_inc(rv_turned, 1)
            pe.wait_ge(rv_stored, 4 * h + 4)
            for i, b in enumerate((1, 2, 3, 4, 0)):
                c0, n = q_rows(b)
                w = SEQ if b == 0 else SEQ - (b - 1) * P
                if i >= 2:
                    pe.wait_ge(ret_decayed, 5 * h + i - 1)
                for k in range(2):
                    last = nc.tensor.matmul(flat[0:n, 2048 + (i % 2) * 512:2048 + (i % 2) * 512 + w], rk[:, k, c0:c0 + n],
                                            rq[:, k, T - w:T], start=k == 0, stop=k == 1)
                last.then_inc(ret_scored, 1)
            for e in range(4):
                n0 = 4 * h + e
                if e == 0:
                    pe.wait_ge(ret_decayed, 5 * h + 5)
                wait(pe, ret_copied, n0 - 1)
                o = (6 + e % 2) * 512
                for i, b in enumerate((1, 2, 3, 4, 0)):
                    n = q_rows(b)[1]
                    w = SEQ if b == 0 else SEQ - (b - 1) * P
                    last = nc.tensor.matmul(flat[:, o + SEQ - w:o + SEQ], rv[0:n, b, e * P:(e + 1) * P],
                                            decayed[0:n, b, SEQ - w:SEQ], start=i == 0, stop=i == 4)
                last.then_inc(ret_weighed, 1)
            for e in range(4):
                pe.wait_ge(ret_squared, 4 * h + e + 1)
                last = nc.tensor.matmul(bank(4, SEQ), ones_g[:], rsq[:, e], start=e == 0, stop=e == 3)
            last.then_inc(ret_var, 1)

        def ret_act(act, h):
            name = f"ret{h}"
            for c in range(12):
                u = Step(FIRST_TILE[name] + c)
                split_hi(act, Step(FIRST_CHUNK[name] + c + AHEAD))
                act.wait_ge(chunk_done, FIRST_CHUNK[name] + c + 1)
                wide = 2 <= c < 8
                src = tile_out(u, wide)
                if c < 2:
                    if c == 0:
                        wait(act, ret_scored, 5 * h)
                    nc.scalar.activation(halves(rq[:, c], wide), src, ACT.Copy).then_inc(evicted[u.mod(2)], 1)
                elif c < 4:
                    nc.scalar.activation(halves(rk[:, c - 2], wide), src, ACT.Copy, scale=1.0 / 16).then_inc(evicted[u.mod(2)], 1)
                elif c < 8:
                    wait(act, rv_turned, 4 * h + c - 4 - 1)
                    nc.scalar.activation(halves(rv_slot[:, c % 2], wide), src, ACT.Copy).then_inc(evicted[u.mod(2)], 1)
                else:
                    if c == 8:
                        wait(act, ret_gated, 4 * h)
                    nc.scalar.activation(rg[:, c - 8:c - 7], src, ACT.Silu).then_inc(evicted[u.mod(2)], 1)
            for e in range(4):
                act.wait_ge(ret_copied, 4 * h + e + 1)
                if e == 0:
                    wait(act, ret_var, h)
                nc.scalar.activation(rsq[:, e], ro[:, e], ACT.Square).then_inc(ret_squared, 1)
            act.wait_ge(ret_veps, h + 1)
            nc.scalar.activation(ret_rt[:], ret_rt[:], ACT.Sqrt).then_inc(ret_root, 1)
            for e in range(4):
                act.wait_ge(ret_gated, 4 * h + e + 1)
                if e == 0 and h == 2:
                    act.wait_ge(chunk_done, FIRST_CHUNK["ret_out0"] + 8)
                nc.scalar.activation(ret_hi[:, 4 * (h % 2) + e, META:T], ro[:, e], ACT.Copy).then_inc(ret_hi_s, 1)

        def ret_dve(dve, h):
            name = f"ret{h}"
            for c in range(12):
                split_lo(dve, Step(FIRST_CHUNK[name] + c + AHEAD))
                if 5 <= c < 9:
                    t = c - 5
                    dve.wait_ge(rv_turned, 4 * h + t + 1)
                    if t == 0:
                        wait(dve, ret_weighed, 4 * h)
                    nc.vector.tensor_copy(rv[:, 1:5, t * P:(t + 1) * P], bank(4, 512).rearrange("p (b n) -> p b n", b=4))
                    nc.vector.tensor_copy(rv[0:META, 0, t * P:(t + 1) * P], flat[0:META, 2560:2560 + P]).then_inc(rv_stored, 1)
            dve.wait_ge(decay_in, 32 * (h + 1))
            for i, b in enumerate((1, 2, 3, 4, 0)):
                n = q_rows(b)[1]
                w = SEQ if b == 0 else SEQ - (b - 1) * P
                dve.wait_ge(ret_scored, 5 * h + i + 1)
                d = decay_meta[:, 0:w] if b == 0 else decay[:, 0:w]
                o = 2048 + (i % 2) * 512
                nc.vector.tensor_tensor(decayed[0:n, b, SEQ - w:SEQ], flat[0:n, o:o + w], d, ALU.mult).then_inc(ret_decayed, 1)
            for e in range(4):
                dve.wait_ge(ret_weighed, 4 * h + e + 1)
                if e == 0:
                    wait(dve, ret_hi_s, 4 * h)
                    wait(dve, ret_lo_s, 4 * h)
                nc.vector.tensor_copy(ro[:, e], bank(6 + e % 2, SEQ)).then_inc(ret_copied, 1)
            dve.wait_ge(ret_var, h + 1)
            nc.vector.tensor_scalar(ret_rt[:], bank(4, SEQ), RMS_EPS, None, ALU.add).then_inc(ret_veps, 1)
            dve.wait_ge(ret_root, h + 1)
            dve_chain.mark(nc.vector.reciprocal(ret_rt[:], ret_rt[:]))
            dve_chain.settle(dve)
            for e in range(4):
                dve_chain.mark(nc.vector.tensor_tensor(ro[:, e], ro[:, e], ret_rt[:], ALU.mult))
            dve_chain.settle(dve)
            for e in range(4):
                nc.vector.tensor_tensor(ro[:, e], ro[:, e], rg[:, e], ALU.mult).then_inc(ret_gated, 1)
            for e in range(4):
                dve.wait_ge(ret_hi_s, 4 * h + e + 1)
                nc.vector.tensor_tensor(ret_lo[:, 4 * (h % 2) + e, META:T], ro[:, e], ret_hi[:, 4 * (h % 2) + e, META:T],
                                        ALU.subtract).then_inc(ret_lo_s, 1)

        def retention_pe(pe):
            for h in range(RET_HEADS):
                ret_pe(pe, h)
                if h % 2:
                    pe.wait_ge(ret_lo_s, 4 * h + 4)
                    pe_stage(pe, f"ret_out{h // 2}", ret_hi, ret_lo, False, after=(lambda k: ln10.add_mean(pe, k)) if h == 3 else None)

        def retention_act(act):
            for h in range(RET_HEADS):
                ret_act(act, h)
                if h % 2:
                    only_split(act, split_hi, f"ret_out{h // 2}")

        def retention_dve(dve):
            for h in range(RET_HEADS):
                ret_dve(dve, h)
                if h % 2:
                    residual_dve(dve, f"ret_out{h // 2}", False, ALPHA if h == 1 else 1.0)

        ln10 = Norm("ln10", FIRST_TILE["up1a"], False, PARAM["ln_g"] + 16, PARAM["ln_b"] + 16)
        mlp1 = Mlp(1, False)
        ln11 = Norm("ln11", FIRST_TILE["latq"], False, PARAM["ln_g"] + 24, PARAM["ln_b"] + 24)

        rms_mix = Norm("rms_mix", FIRST_TILE["latq"], False, PARAM["norm_mix"], eps=RMS_EPS)
        placed["next"] = shared
        merged = at("merged", [P, KT, SEQ])
        after_merged = placed["next"]
        lq = nc.alloc_sbuf_tensor_at("lq", [P, KT, SEQ], F32, offset=shared)
        key_row = at("key_row", [P, SEQ])
        key_tok = at("key_tok", [P, QT, P])
        wuk = at("wuk", [P, 8, P])
        wuv = at("wuv", [P, 8, P])
        select = at("select", [P, 1280])
        att_hi = at("att_hi", [P, KT, T], F32R)
        att_lo = at("att_lo", [P, KT, T], F32R)
        dsa_work = placed["next"]
        bias_near = at("bias_near", [P, 2, 2 * P])
        q_lat = at("q_lat", [P, 2, SEQ])
        d_buf = at("d_buf", [P, 4, SEQ])
        d_norm = at("d_norm", [P, 3, SEQ])
        d_turn = at("d_turn", [P, 2, SEQ])
        att_lat = at("att_lat", [P, 2, SEQ])
        d_stat = at("d_stat", [P, 3, 64])
        dsa_causal = at("dsa_causal", [P, P])
        key_raw = at("key_raw", [P, SEQ], start=dsa_work)
        key_sq = at("key_sq", [P, SEQ])
        key_rt = at("key_rt", [P, SEQ])
        iq = at("iq", [P, 4, SEQ])
        ik = at("ik", [P, SEQ])
        iw_row = at("iw_row", [IDX_HEADS, SEQ])
        iw = at("iw", [P, QT, IDX_HEADS])
        i_relu = at("i_relu", [P, 2, SEQ])
        top = at("top", [P, 3, 8])
        bucket = at("bucket", [32, 640])
        rel_sb = at("rel_sb", [32, ATT_HEADS])
        line_sb = at("line_sb", [ATT_HEADS, 640])

        (dsa_loaded, line_done, line_kept, line_out, key_squared, key_mean, key_veps, key_root, key_ready,
         key_turned, key_kept, idx_turned, idx_kept, idx_scored, idx_relu, idx_added, selected) = (
            sem(n) for n in ("dsa_loaded", "line_done", "line_kept", "line_out", "key_squared", "key_mean", "key_veps",
                             "key_root", "key_ready", "key_turned", "key_kept", "idx_turned", "idx_kept", "idx_scored", "idx_relu",
                             "idx_added", "selected"))
        (ql_done, ql_kept, d_scored, d_biased, d_expd, d_inverse, d_normed, d_turned, d_kept, d_weighed, lat_kept, att_done, att_hi_s,
         att_lo_s, gate_done) = (
            sem(n) for n in ("ql_done", "ql_kept", "d_scored", "d_biased", "d_expd", "d_inverse", "d_normed", "d_turned", "d_kept",
                             "d_weighed", "lat_kept", "att_done", "att_hi_s", "att_lo_s", "gate_done"))

        skew_out = sem("skew_out")
        near_in = [sem(f"near_in{n}") for n in range(2)]

        def sel_cols(i):
            a = P * i * (i + 1) // 2
            return slice(a, a + P * (i + 1))

        def dsa_loads(pool):
            pool.wait_ge(norm_lo, rms_mix.lo_at)
            for dst, src in ((bucket[:], tables[0:32, TABLE["bucket"]:TABLE["bucket"] + 640]), (rel_sb[:], rel),
                             (wuk[:], w_uk), (wuv[:].rearrange("p a n -> p (a n)"), w_uv),
                             (dsa_causal[:], tables[:, TABLE["causal"] + 400:TABLE["causal"] + 528])):
                pool.dma_start(dst, src).then_inc(dsa_loaded, 16)
            pool.wait_ge(line_kept, 1)
            pool.dma_start(line, line_sb[:]).then_inc(line_out, 16)
            pool.wait_ge(line_out, 16)
            for h in range(ATT_HEADS):
                src = bass.AP(tensor=line.tensor, offset=h * 640 + 256, ap=[[0, P], [1, 384]])
                dst = bass.AP(tensor=skewed.tensor, offset=h * SKEW + 256, ap=[[641, P], [1, 384]])
                pool.dma_start(dst, src).then_inc(skew_out, 16)
            pool.wait_ge(skew_out, 16 * ATT_HEADS)
            pool.wait_ge(selected, 1)
            for h in range(ATT_HEADS):
                if h >= 2:
                    pool.wait_ge(d_biased, 4 * (h - 1))
                src = bass.AP(tensor=skewed.tensor, offset=h * SKEW + 383, ap=[[640, P], [1, 2 * P]])
                pool.dma_start(bias_near[:, h % 2], src).then_inc(near_in[h % 2], 16)

        def single(eng, split, name):
            split(eng, Step(FIRST_CHUNK[name] + AHEAD))

        def keep_tiles(act, name, dst, func=ACT.Copy, scale=1.0, rows=P, n=None):
            def keep(tile, done):
                act.wait_ge(chunk_done, done)
                u = tile.plus(FIRST_TILE[name])
                o = dst[0:rows, one(tile), 0:SEQ] if len(dst.shape) == 3 else dst[0:rows, :].rearrange("p (a n) -> p a n", a=1)
                nc.scalar.activation(o, tile_out(u, False)[0:rows], func, scale=scale).then_inc(evicted[u.mod(2)], 1)
            side_stage(act, split_hi, name, keep)

        def tile_kept(eng, name, n=1):
            tiles_out(eng, FIRST_TILE[name] + n)

        def select_pe(pe):
            pe_stage(pe, "latq", x_hi, x_lo, False, ready=rms_mix.ready)
            pe_stage(pe, "latc", x_hi, x_lo, False)
            pe_stage(pe, "idxq", x_hi, x_lo, False)
            pe_stage(pe, "idxk", x_hi, x_lo, False)
            pe_stage(pe, "idxw", x_hi, x_lo, False)
            pe.wait_ge(dsa_loaded, 5 * 16)
            nc.tensor.matmul(flat[0:ATT_HEADS, 3072:3584], rel_sb[:], bucket[:, 0:512], start=True, stop=True)
            nc.tensor.matmul(flat[0:ATT_HEADS, 3584:3712], rel_sb[:], bucket[:, 512:640], start=True, stop=True).then_inc(line_done, 1)
            pe.wait_ge(key_squared, 1)
            nc.tensor.matmul(bank(4, SEQ), ones_h[:], key_sq[:], start=True, stop=True).then_inc(key_mean, 1)
            tiles_out(pe, FIRST_TILE["att_out"])
            for j in range(QT):
                last = nc.tensor.transpose(flat[:, 1024 + 8 * j:1024 + 8 * j + 8], iw_row[:, j * P:(j + 1) * P], ident[0:8, 0:8])
            last.then_inc(idx_turned, 1)
            for n in range(3 * IDX_HEADS):
                i, h = 1 + n // IDX_HEADS, n % IDX_HEADS
                rows = slice(64 * (h % 2), 64 * (h % 2) + 64)
                if n < 2:
                    pe.wait_ge(idx_kept, 1)
                else:
                    pe.wait_ge(idx_relu, n - 1)
                nc.tensor.matmul(bank(2 + n % 2, P * (i + 1)), iq[rows, h // 2, i * P:(i + 1) * P], ik[rows, 0:P * (i + 1)],
                                 start=True, stop=True).then_inc(idx_scored, 1)
            pe.wait_ge(key_ready, 1)
            for j in range(QT):
                last = nc.tensor.transpose(flat[:, 2560 + j * P:2560 + (j + 1) * P], key_row[:, j * P:(j + 1) * P], ident[:])
            last.then_inc(key_turned, 1)

        def select_act(act):
            keep_tiles(act, "latq", lq, scale=0.125)
            keep_tiles(act, "latc", key_raw)
            keep_tiles(act, "idxq", iq)
            keep_tiles(act, "idxk", ik)
            keep_tiles(act, "idxw", iw_row, rows=IDX_HEADS)
            tile_kept(act, "latc")
            nc.scalar.activation(key_sq[:], key_raw[:], ACT.Square).then_inc(key_squared, 1)
            act.wait_ge(line_done, 1)
            nc.scalar.activation(line_sb[:], flat[0:ATT_HEADS, 3072:3712], ACT.Copy).then_inc(line_kept, 1)
            act.wait_ge(key_veps, 1)
            nc.scalar.activation(key_rt[:], key_rt[:], ACT.Sqrt).then_inc(key_root, 1)
            for n in range(3 * IDX_HEADS):
                i = 1 + n // IDX_HEADS
                act.wait_ge(idx_scored, n + 1)
                if n >= 2:
                    act.wait_ge(idx_added, n - 1)
                nc.scalar.activation(i_relu[:, n % 2, 0:P * (i + 1)], bank(2 + n % 2, P * (i + 1)), ACT.Relu).then_inc(idx_relu, 1)

        def select_dve(dve):
            for name in ("latq", "latc", "idxq", "idxk", "idxw"):
                only_split(dve, split_lo, name)
            dve.wait_ge(key_mean, 1)
            nc.vector.tensor_scalar(key_rt[:], bank(4, SEQ), RMS_EPS, None, ALU.add).then_inc(key_veps, 1)
            dve.wait_ge(key_root, 1)
            dve_chain.mark(nc.vector.reciprocal(key_rt[:], key_rt[:]))
            dve_chain.settle(dve)
            g = par[:, PARAM["kv_norm"]:PARAM["kv_norm"] + 1]
            nc.vector.scalar_tensor_tensor(key_row[:], key_raw[:], g, key_rt[:], ALU.mult, ALU.mult).then_inc(key_ready, 1)
            dve.wait_ge(idx_turned, 1)
            nc.vector.tensor_copy(iw[:].rearrange("p a n -> p (a n)"), flat[:, 1024:1056]).then_inc(idx_kept, 1)
            dve.wait_ge(idx_kept, 1)
            dve.wait_ge(dsa_loaded, 5 * 16)
            nc.vector.tensor_copy(select[:, 0:P], dsa_causal[:])
            for n in range(3 * IDX_HEADS):
                i, h = 1 + n // IDX_HEADS, n % IDX_HEADS
                w = iw[:, i, h:h + 1]
                s = select[:, sel_cols(i)]
                r = i_relu[:, n % 2, 0:P * (i + 1)]
                dve.wait_ge(idx_relu, n + 1)
                if h == 0:
                    nc.vector.tensor_scalar(s, r, w, None, ALU.mult).then_inc(idx_added, 1)
                else:
                    dve.wait_ge(idx_added, n)
                    nc.vector.scalar_tensor_tensor(s, r, w, s, ALU.mult, ALU.add).then_inc(idx_added, 1)
                if h == IDX_HEADS - 1:
                    dve.wait_ge(idx_added, n + 1)
                    d = select[:, sel_cols(i).stop - P:sel_cols(i).stop]
                    dve_chain.mark(nc.vector.tensor_tensor(d, d, dsa_causal[:], ALU.add))
            for _ in range(16):
                dve_chain.settle(dve)
                for i in range(1, QT):
                    dve_chain.mark(nc.vector.max(top[:, i - 1], select[:, sel_cols(i)]))
                dve_chain.settle(dve)
                for i in range(1, QT):
                    s = select[:, sel_cols(i)]
                    dve_chain.mark(nc.vector.match_replace(s, top[:, i - 1], s, FILL))
            dve_chain.settle(dve)
            s = select[:, P:1280]
            dve_chain.mark(nc.vector.tensor_scalar(s, s, FILL, 1.0, ALU.is_equal, ALU.subtract))
            dve_chain.settle(dve)
            dve_chain.mark(nc.vector.tensor_scalar(s, s, -NEG, None, ALU.mult))
            dve_chain.settle(dve)
            dve.wait_ge(key_turned, 1)
            nc.vector.tensor_copy(key_tok[:].rearrange("p a n -> p (a n)"), bank(5, SEQ)).then_inc(selected, 1)

        ND = ATT_HEADS * QT

        def d_query(pe, h):
            rows = slice(64 * (h % 2), 64 * (h % 2) + 64)
            if h >= 2:
                pe.wait_ge(ql_kept, h - 1)
            nc.tensor.matmul(bank(2 + h % 2, SEQ), wuk[rows, h // 2, :], lq[rows, h // 2, :], start=True, stop=True).then_inc(ql_done, 1)

        def d_scores(pe, p):
            h, i = divmod(p, QT)
            if i == 0:
                pe.wait_ge(ql_kept, h + 1)
            if p >= 2:
                pe.wait_ge(d_biased, p - 1)
            nc.tensor.matmul(bank(4 + p % 2, P * (i + 1)), q_lat[:, h % 2, i * P:(i + 1) * P], key_row[:, 0:P * (i + 1)],
                             start=True, stop=True).then_inc(d_scored, 1)

        def d_bias(dve, p):
            h, i = divmod(p, QT)
            w = P * (i + 1)
            near = min(w, 2 * P)
            s = d_buf[:, p % 4]
            dve.wait_ge(d_scored, p + 1)
            dve.wait_ge(near_in[h % 2], 16 * (h // 2 + 1))
            if p >= 4:
                dve.wait_ge(d_normed, p - 3)
            dve_chain.mark(nc.vector.tensor_tensor(s[:, w - near:w], bank(4 + p % 2, w)[:, w - near:w], bias_near[:, h % 2, 2 * P - near:2 * P], ALU.add))
            if w > near:
                far = par[:, PARAM["rel_far"] + h:PARAM["rel_far"] + h + 1]
                dve_chain.mark(nc.vector.tensor_scalar(s[:, 0:w - near], bank(4 + p % 2, w - near), far, None, ALU.add))
            dve_chain.settle(dve)
            nc.vector.tensor_tensor_reduce(s[:, 0:w], s[:, 0:w], select[:, sel_cols(i)], -1.0, FIRST_MIN, ALU.add, ALU.min,
                                           d_stat[:, 0, p:p + 1]).then_inc(d_biased, 1)

        def d_exp(act, p):
            w = P * (p % QT + 1)
            s = d_buf[:, p % 4, 0:w]
            act.wait_ge(d_biased, p + 1)
            nc.scalar.activation(s, s, ACT.Exp, scale=-1.0, bias=d_stat[:, 0, p:p + 1], accum_out=d_stat[:, 1, p:p + 1]).then_inc(d_expd, 1)

        def d_invert(dve, p):
            dve.wait_ge(d_expd, p + 1)
            nc.vector.reciprocal(d_stat[:, 2, p:p + 1], d_stat[:, 1, p:p + 1]).then_inc(d_inverse, 1)

        def d_divide(act, p):
            w = P * (p % QT + 1)
            act.wait_ge(d_inverse, p + 1)
            if p >= 3:
                act.wait_ge(d_turned, p - 2)
            nc.scalar.activation(d_norm[:, p % 3, 0:w], d_buf[:, p % 4, 0:w], ACT.Copy, scale=d_stat[:, 2, p:p + 1]).then_inc(d_normed, 1)

        def d_turn_pe(pe, p):
            pe.wait_ge(d_normed, p + 1)
            if p:
                pe.wait_ge(d_kept, p)
            for b in range(p % QT + 1):
                last = nc.tensor.transpose(flat[:, 3072 + b * P:3072 + (b + 1) * P], d_norm[:, p % 3, b * P:(b + 1) * P], ident[:])
            last.then_inc(d_turned, 1)

        def d_keep(act, p):
            w = P * (p % QT + 1)
            act.wait_ge(d_turned, p + 1)
            if p >= 2:
                act.wait_ge(d_weighed, p - 1)
            nc.scalar.activation(d_turn[:, p % 2, 0:w], bank(6, w), ACT.Copy).then_inc(d_kept, 1)

        def d_values(pe, p):
            h, i = divmod(p, QT)
            pe.wait_ge(d_kept, p + 1)
            if i == 0:
                wait(pe, lat_kept, h)
            for b in range(i + 1):
                last = nc.tensor.matmul(flat[:, 3584 + i * P:3584 + (i + 1) * P], key_tok[:, b, :], d_turn[:, p % 2, b * P:(b + 1) * P],
                                        start=b == 0, stop=b == i)
            last.then_inc(d_weighed, 1)

        def d_out(pe, h):
            rows = slice(64 * (h % 2), 64 * (h % 2) + 64)
            pe.wait_ge(lat_kept, h + 1)
            if h >= 4 and h % 2 == 0:
                pe.wait_ge(att_lo_s, h // 2 - 1)
            nc.tensor.matmul(bank((h // 2) % 2, SEQ, rows), wuv[:, h // 2, 64 * (h % 2):64 * (h % 2) + 64], att_lat[:, h % 2],
                             start=True, stop=True).then_inc(att_done, 1)

        def sparse_pe(pe):
            pe.wait_ge(selected, 1)
            pe.wait_ge(idx_relu, 3 * IDX_HEADS)
            d_query(pe, 0)
            d_query(pe, 1)
            for s in range(ND + 5):
                if s < ND:
                    d_scores(pe, s)
                if s % QT == 2 and 2 <= s // QT + 2 < ATT_HEADS and s < ND:
                    d_query(pe, s // QT + 2)
                if 3 <= s < ND + 3:
                    d_turn_pe(pe, s - 3)
                if 4 <= s < ND + 4:
                    d_values(pe, s - 4)
                if s >= 5 and (s - 5) % QT == QT - 1:
                    d_out(pe, (s - 5) // QT)

        def sparse_act(act):
            act.wait_ge(selected, 1)

            def query(h):
                act.wait_ge(ql_done, h + 1)
                if h >= 2:
                    act.wait_ge(d_scored, QT * (h - 1))
                nc.scalar.activation(q_lat[:, h % 2], bank(2 + h % 2, SEQ), ACT.Copy).then_inc(ql_kept, 1)
            query(0)
            query(1)
            for s in range(ND + 6):
                if s < ND:
                    d_exp(act, s)
                if s % QT == 3 and s // QT + 2 < ATT_HEADS:
                    query(s // QT + 2)
                if 1 <= s < ND + 1:
                    d_divide(act, s - 1)
                if 3 <= s < ND + 3:
                    d_keep(act, s - 3)
                if s >= 5 and (s - 5) % QT == QT - 1 and s - 5 < ND:
                    h = (s - 5) // QT
                    act.wait_ge(d_weighed, QT * (h + 1))
                    if h >= 2:
                        act.wait_ge(att_done, h - 1)
                    nc.scalar.activation(att_lat[:, h % 2], bank(7, SEQ), ACT.Copy).then_inc(lat_kept, 1)
                if s >= 6 and (s - 6) % (2 * QT) == 2 * QT - 1:
                    k = (s - 6) // (2 * QT)
                    act.wait_ge(att_done, 2 * k + 2)
                    nc.scalar.activation(att_hi[:, k, META:T], bank(k % 2, SEQ), ACT.Copy).then_inc(att_hi_s, 1)

        def sparse_dve(dve):
            for s in range(ND + 7):
                if s < ND:
                    d_bias(dve, s)
                if 1 <= s < ND + 1:
                    d_invert(dve, s - 1)
                if s >= 7 and (s - 7) % (2 * QT) == 2 * QT - 1:
                    k = (s - 7) // (2 * QT)
                    dve.wait_ge(att_hi_s, k + 1)
                    nc.vector.tensor_tensor(att_lo[:, k, META:T], bank(k % 2, SEQ), att_hi[:, k, META:T], ALU.subtract).then_inc(att_lo_s, 1)

        gate = nc.alloc_sbuf_tensor_at("gate", [P, 2, SEQ], F32, offset=dsa_work)
        gate_dve_done = sem("gate_dve_done")

        def att_merge_pe(pe):
            pe_stage(pe, "att_out", att_hi, att_lo, False, ready=(att_lo_s, 0))
            pe_stage(pe, "gate_att", x_hi, x_lo, False)

        def att_merge_act(act):
            keep_tiles(act, "att_out", merged)
            gate_act(act, "gate_att", 0)

        def gate_act(act, name, base):
            def keep(tile, done):
                act.wait_ge(chunk_done, done)
                u = tile.plus(FIRST_TILE[name])
                wait(act, gate_dve_done, tile.at(plus=base - 1))
                nc.scalar.activation(gate[:, tile.mod(2):tile.mod(2) + 1], tile_out(u, False), ACT.Sigmoid).then_inc(evicted[u.mod(2)], 1)
            side_stage(act, split_hi, name, keep, peel=0 if base else 1)

        def att_merge_dve(dve):
            only_split(dve, split_lo, "att_out")

            def gated(tile, done):
                u = tile.plus(FIRST_TILE["gate_att"])
                dve.wait_ge(evicted[u.mod(2)], u.over(2).at(plus=1))
                if not tile.stride and tile.start == 0:
                    tiles_out(dve, FIRST_TILE["gate_att"])
                o = merged[:, one(tile)].rearrange("p a n -> p (a n)")
                nc.vector.tensor_tensor(o, o, gate[:, tile.mod(2)], ALU.mult).then_inc(gate_dve_done, 1)
            side_stage(dve, split_lo, "gate_att", gated, peel=1)

        CH = QT
        placed["next"] = after_merged
        y_ssm = at("y_ssm", [P, KT, SEQ])
        u_hi = at("u_hi", [P, 4, T], F32R)
        u_lo = at("u_lo", [P, 4, T], F32R)
        ssm_work = placed["next"]
        xs, b_row, c_row = ([at(f"{n}0", shape)] for n, shape in (("xs", [P, 4, SEQ]), ("b_row", [P, SEQ]), ("c_row", [P, SEQ])))
        conv_in = at("conv_in", [P, 2, SEQ + 4])
        ssm_work2 = placed["next"]
        placed["next"] = shared
        for bufs, n, shape in ((xs, "xs1", [P, 4, SEQ]), (b_row, "b_row1", [P, SEQ]), (c_row, "c_row1", [P, SEQ])):
            bufs.append(at(n, shape))
        assert placed["next"] <= after_merged
        placed["next"] = ssm_work2
        z_buf = at("z_buf", [P, 4, SEQ])
        steps_abc = at("steps_abc", [P, 2, 8, P])
        seg = at("seg", [P, 8, P])
        c_dec = at("c_dec", [P, 8, P])
        x_dt = at("x_dt", [P, 2, SEQ])
        x_dec = at("x_dec", [P, SEQ])
        b_tok = at("b_tok", [P, P])
        cb = at("cb", [P, P])
        tri = at("tri", [P, P])
        state = at("state", [P, SEQ])
        dec_end = at("dec_end", [P, 2, 8])
        dt_tok = at("dt_tok", [P, CH, 32])
        acum_tok = at("acum_tok", [P, CH, 32])
        a_col = at("a_col", [32, 1])
        g_rt = z_buf[:, 0]
        gates = nc.alloc_sbuf_tensor_at("gates", [P, KT, SEQ], F32, offset=ssm_work)
        dt_row = nc.alloc_sbuf_tensor_at("dt_row", [32, 4, SEQ], F32, offset=ssm_work)
        dt_one = nc.alloc_sbuf_tensor_at("dt_one", [32, P], F32, offset=ssm_work + 4 * SEQ * 4)
        acum_row = nc.alloc_sbuf_tensor_at("acum_row", [32, SEQ], F32, offset=ssm_work + 5 * SEQ * 4)

        (dt_a, dt_b, acum_ready, acum_out, ssm_loaded, dt_turned, dt_kept, conv_done, conv_silu, ssm_turned, seg_args, dec_args,
         seg_exp, dec_exp, abc_exp, y_ready, end_ready, y_done, state_done, abc_used, z_ready, u_done, u_sq, ssm_var, ssm_veps, ssm_root,
         u_norm, u_hi_s, u_lo_s, zeroed, m_sum, m_hi_s, m_lo_s) = (
            sem(n) for n in ("dt_a", "dt_b", "acum_ready", "acum_out", "ssm_loaded", "dt_turned", "dt_kept", "conv_done", "conv_silu",
                             "ssm_turned", "seg_args", "dec_args", "seg_exp", "dec_exp", "abc_exp", "y_ready", "end_ready", "y_done",
                             "state_done", "abc_used", "z_ready", "u_done", "u_sq", "ssm_var", "ssm_veps", "ssm_root", "u_norm",
                             "u_hi_s", "u_lo_s", "zeroed", "m_sum", "m_hi_s", "m_lo_s"))
        abc_in = [sem(f"abc_in{n}") for n in range(2)]

        def ssm_loads(pool):
            pool.wait_ge(gate_dve_done, KT)
            pool.wait_ge(chunk_done, FIRST_CHUNK["gate_att"])
            nc.gpsimd.memset(conv_in[:, :, 0:3], 0.0).then_inc(zeroed, 1)
            nc.gpsimd.memset(dt_one[:], 1.0).then_inc(zeroed, 1)
            pool.dma_start(tri[:], tables[:, TABLE["tri"]:TABLE["tri"] + P]).then_inc(ssm_loaded, 16)
            pool.dma_start(merged_dram, merged[:].rearrange("p k n -> p (k n)")).then_inc(merged_out, 16)
            pool.wait_ge(acum_ready, 1)
            pool.dma_start(acum_dram, acum_row[:]).then_inc(acum_out, 16)
            pool.wait_ge(acum_out, 16)
            for n in range(SSM_GROUPS * CH):
                g, c = divmod(n, CH)
                if n >= 2:
                    pool.wait_ge(abc_used, n - 1)
                src = bass.AP(tensor=acum_dram.tensor, offset=8 * g * SEQ + c * P, ap=[[0, P], [SEQ, 8], [1, P]])
                pool.dma_start(steps_abc[:, n % 2], src).then_inc(abc_in[n % 2], 16)
            pool.wait_ge(merged_out, 16)
            pool.wait_ge(u_hi_s, 4 * SSM_GROUPS)
            pool.wait_ge(u_lo_s, 4 * SSM_GROUPS)
            pool.dma_start(merged[:].rearrange("p k n -> p (k n)"), merged_dram).then_inc(merged_in, 16)

        def dt_pe(pe):
            chunk_products(pe, "dt", Step(0), x_hi, x_lo, False)
            pe.wait_ge(acum_ready, 1)
            for src, o in ((dt_row[:, 3], 2048), (acum_row[:], 2176)):
                for c in range(CH):
                    last = nc.tensor.transpose(flat[:, o + 32 * c:o + 32 * c + 32], src[:, c * P:(c + 1) * P], ident[0:32, 0:32])
            last.then_inc(dt_turned, 1)

        def dt_act(act):
            u = Step(FIRST_TILE["dt"])
            split_hi(act, Step(FIRST_CHUNK["dt"] + AHEAD))
            act.wait_ge(chunk_done, FIRST_CHUNK["dt"] + 1)
            act.wait_ge(gate_dve_done, KT)
            act_chain.mark(nc.scalar.activation(dt_row[:, 0:1], tile_out(u, False)[0:32], ACT.Identity,
                                                bias=par[0:32, PARAM["dt_bias"]:PARAM["dt_bias"] + 1]))
            act_chain.settle(act)
            nc.scalar.activation(dt_row[:, 1], dt_row[:, 0], ACT.Abs).then_inc(evicted[u.mod(2)], 1)
            act.wait_ge(evicted[u.mod(2)], u.start // 2 + 1)
            act_chain.mark(nc.scalar.activation(dt_row[:, 1], dt_row[:, 1], ACT.Exp, scale=-1.0))
            nc.scalar.activation(a_col[:], par[0:32, PARAM["a_log"]:PARAM["a_log"] + 1], ACT.Exp).then_inc(dt_a, 1)
            act_chain.settle(act)
            nc.scalar.activation(dt_row[:, 2], dt_row[:, 1], ACT.Ln, bias=1.0).then_inc(dt_a, 1)

        def dt_dve(dve):
            split_lo(dve, Step(FIRST_CHUNK["dt"] + AHEAD))
            dve.wait_ge(dt_a, 2)
            dve_chain.mark(nc.vector.tensor_scalar(dt_row[:, 3], dt_row[:, 0], 0.0, None, ALU.max))
            dve_chain.settle(dve)
            dve_chain.mark(nc.vector.tensor_tensor(dt_row[:, 3], dt_row[:, 3], dt_row[:, 2], ALU.add))
            dve_chain.settle(dve)
            dve_chain.mark(nc.vector.tensor_scalar(dt_row[:, 1], dt_row[:, 3], a_col[:], -1.0, ALU.mult, ALU.mult))
            dve_chain.settle(dve)
            dve.wait_ge(zeroed, 2)
            for c in range(CH):
                cols = slice(c * P, (c + 1) * P)
                ins = nc.vector.tensor_tensor_scan(acum_row[:, cols], dt_one[:], dt_row[:, 1, cols], 0.0, ALU.mult, ALU.add)
            ins.then_inc(acum_ready, 1)
            dve.wait_ge(dt_turned, 1)
            nc.vector.tensor_copy(dt_tok[:].rearrange("p c h -> p (c h)"), flat[:, 2048:2176])
            nc.vector.tensor_copy(acum_tok[:].rearrange("p c h -> p (c h)"), flat[:, 2176:2304]).then_inc(dt_kept, 1)
            dve.wait_ge(dt_kept, 1)
            dve.wait_ge(ssm_loaded, 16)
            dve.wait_ge(acum_out, 16)

        def ssm_turn(pe, g, c):
            n = CH * g + c
            cols = slice(c * P, (c + 1) * P)
            if n:
                pe.wait_ge(y_ready, n)
            for t in range(4):
                nc.tensor.transpose(flat[:, 2048 + t * P:2048 + (t + 1) * P], xs[g % 2][:, t, cols], ident[:])
            nc.tensor.transpose(flat[:, 2560:2560 + P], b_row[g % 2][:, cols], ident[:])
            nc.tensor.matmul(flat[:, 2688:2688 + P], b_row[g % 2][:, cols], c_row[g % 2][:, cols], start=True, stop=True) \
                .then_inc(ssm_turned, 1)

        def ssm_outputs(pe, g, c):
            n = CH * g + c
            pe.wait_ge(y_ready, n + 1)
            if n:
                pe.wait_ge(y_done, n)
            for h in range(HEADS_PER_GROUP):
                rows = slice(64 * (h % 2), 64 * (h % 2) + 64)
                o = flat[rows, 3072 + (h // 2) * P:3072 + (h // 2 + 1) * P]
                last = nc.tensor.matmul(o, x_dt[:, n % 2, 64 * h:64 * h + 64], seg[:, h], start=True, stop=c == 0)
                if c:
                    last = nc.tensor.matmul(o, state[:, 64 * h:64 * h + 64], c_dec[:, h], start=False, stop=True)
            if c == CH - 1:
                last.then_inc(end_ready, 1)
            else:
                nc.tensor.matmul(bank(7, SEQ), b_tok[:], x_dec[:], start=True, stop=True).then_inc(end_ready, 1)

        def group_items(g):
            xs_next, so_last, z_own = ([(kind, h, t) for t in range(n)] for kind, h, n in (("xs", g + 1, 6), ("so", g - 1, 4), ("z", g, 4)))
            if g == SSM_GROUPS:
                return [[("gs", g, t) for t in range(3, KT)]]
            if g == SSM_GROUPS - 1:
                return [z_own[0:2], z_own[2:4] + so_last[0:1], so_last[1:4], [("gs", g, t) for t in range(3)]]
            if g == 0:
                return [xs_next[0:3], xs_next[3:6], z_own[0:2], z_own[2:4]]
            return [xs_next[0:3], xs_next[3:6] + so_last[0:1], so_last[1:4] + z_own[0:1], z_own[1:4]]

        def item_at(item):
            kind, g, t = item
            name = "gate_ssm" if kind == "gs" else f"{kind}{g}"
            return name, FIRST_CHUNK[name] + t, FIRST_TILE[name] + (2 * t if kind == "so" else t)

        def so_pe(pe, g, k):
            ck = FIRST_CHUNK[f"so{g}"] + k
            pe.wait_ge(lo_ready, ck + 1)
            pe.wait_ge(u_lo_s, 4 * g + 4)
            for m in range(2):
                u = FIRST_TILE[f"so{g}"] + 2 * k + m
                pe.wait_ge(evicted[u % 2], u // 2)
                for f in range(4):
                    for w, (a, b) in enumerate(((w_hi, u_hi), (w_hi, u_lo), (w_lo, u_hi))):
                        last = nc.tensor.matmul(ps[:, 2 * (u % 2), 0:SEQ], a[:, ck % RING, 2 * f + m], b[:, f, META:T],
                                                start=f == 0 and w == 0, stop=f == 3 and w == 2)
            last.then_inc(chunk_done, 1)

        def item_pe(pe, item):
            if item[0] == "so":
                so_pe(pe, item[1], item[2])
            else:
                chunk_products(pe, item_at(item)[0], Step(item[2]), x_hi, x_lo, False)

        def squares_pe(pe, g):
            for t in range(4):
                pe.wait_ge(u_sq, 4 * g + t + 1)
                last = nc.tensor.matmul(bank(1, SEQ), ones_g[:], z_buf[:, t], start=t == 0, stop=t == 3)
            last.then_inc(ssm_var, 1)

        def ssm_pe(pe, g):
            if g < SSM_GROUPS:
                pe.wait_ge(conv_silu, 3 * g + 3)
            for c, items in enumerate(group_items(g)):
                if g < SSM_GROUPS:
                    ssm_turn(pe, g, c)
                for i, item in enumerate(items):
                    item_pe(pe, item)
                    if g and c == 0 and i == 0:
                        squares_pe(pe, g - 1)
                if g < SSM_GROUPS:
                    ssm_outputs(pe, g, c)

        def first_inputs_pe(pe):
            for t in range(6):
                item_pe(pe, ("xs", 0, t))

        def item_split(eng, item, split):
            split(eng, Step(item_at(item)[1] + AHEAD))

        def item_act(act, item):
            kind, g, t = item
            name, chunk, u = item_at(item)
            if kind == "so":
                return
            act.wait_ge(chunk_done, chunk + 1)
            out = tile_out(Step(u), False)
            if kind == "xs":
                wait(act, conv_done, 6 * g + t - 1)
                nc.scalar.activation(conv_in[:, t % 2:t % 2 + 1, 3:3 + SEQ], out, ACT.Copy).then_inc(evicted[u % 2], 1)
            elif kind == "gs":
                nc.scalar.activation(gates[:, t:t + 1], out, ACT.Sigmoid).then_inc(evicted[u % 2], 1)
            else:
                nc.scalar.activation(z_buf[:, t:t + 1], out, ACT.Copy).then_inc(evicted[u % 2], 1)
                if t == 3:
                    tiles_out(act, u + 1)
                    nc.scalar.activation(z_buf[:], z_buf[:], ACT.Silu).then_inc(z_ready, 1)

        def inputs_silu(act, g):
            act.wait_ge(conv_done, 6 * g + 6)
            for buf in (xs, b_row, c_row):
                nc.scalar.activation(buf[g % 2][:], buf[g % 2][:], ACT.Silu).then_inc(conv_silu, 1)

        def first_inputs_act(act):
            act.wait_ge(zeroed, 2)
            for t in range(6):
                item_split(act, ("xs", 0, t), split_hi)
                item_act(act, ("xs", 0, t))
            inputs_silu(act, 0)

        def ssm_act(act, g):
            if g:
                for t in range(4):
                    act.wait_ge(u_done, 4 * (g - 1) + t + 1)
                    nc.scalar.activation(z_buf[:, t], xs[(g - 1) % 2][:, t], ACT.Square).then_inc(u_sq, 1)
            for c, items in enumerate(group_items(g)):
                n = CH * g + c
                if g < SSM_GROUPS:
                    act.wait_ge(dec_args, n + 1)
                    nc.scalar.activation(dec_end[:, n % 2], dec_end[:, n % 2], ACT.Exp).then_inc(dec_exp, 1)
                    act.wait_ge(seg_args, n + 1)
                    nc.scalar.activation(seg[:], seg[:], ACT.Exp).then_inc(seg_exp, 1)
                    nc.scalar.activation(steps_abc[:, n % 2], steps_abc[:, n % 2], ACT.Exp).then_inc(abc_exp, 1)
                for i, item in enumerate(items):
                    item_split(act, item, split_hi)
                    if g and c == 0 and i == 0:
                        finish_root_act(act, g - 1)
                    if g and c == 0 and i == (0 if item[0] == "z" else 1):
                        finish_hi_act(act, g - 1)
                    item_act(act, item)
                if c == 1 and g < SSM_GROUPS - 1:
                    inputs_silu(act, g + 1)

        def finish_root_act(act, g):
            act.wait_ge(ssm_veps, g + 1)
            nc.scalar.activation(g_rt, g_rt, ACT.Sqrt).then_inc(ssm_root, 1)

        def finish_hi_act(act, g):
            for t in range(4):
                act.wait_ge(u_norm, 4 * g + t + 1)
                nc.scalar.activation(u_hi[:, t, META:T], xs[g % 2][:, t], ACT.Copy).then_inc(u_hi_s, 1)

        def convolve(dve, dst, taps, col, src, bias, done):
            for j in reversed(range(taps)):
                w = par[:, col(j)]
                x = src[:, j:j + SEQ]
                if j == taps - 1:
                    dve_chain.mark(nc.vector.tensor_scalar(dst, x, w, par[:, bias], ALU.mult, ALU.add))
                else:
                    dve_chain.settle(dve)
                    ins = nc.vector.scalar_tensor_tensor(dst, x, w, dst, ALU.mult, ALU.add)
                    if j:
                        dve_chain.mark(ins)
            ins.then_inc(done, 1)

        def item_dve(dve, item):
            kind, g, t = item
            name, chunk, u = item_at(item)
            if kind == "xs":
                dve.wait_ge(evicted[u % 2], u // 2 + 1)
                if g == 1 and t == 0:
                    dve.wait_ge(merged_out, 16)
                if g >= 2 and t == 0:
                    dve.wait_ge(u_lo_s, 4 * (g - 1))
                k = 4 * g + t if t < 4 else (16 + g if t == 4 else 20 + g)
                dst = xs[g % 2][:, t] if t < 4 else (b_row[g % 2][:] if t == 4 else c_row[g % 2][:])
                c0, b0 = PARAM["conv_ssm_w"], PARAM["conv_ssm_b"] + k
                convolve(dve, dst, 4, lambda j: slice(c0 + 24 * j + k, c0 + 24 * j + k + 1), conv_in[:, t % 2], slice(b0, b0 + 1), conv_done)
            elif kind == "so":
                dve.wait_ge(chunk_done, chunk + 1)
                for m in range(2):
                    src = ps[:, 2 * ((u + m) % 2), 0:SEQ]
                    y = y_ssm[:, 2 * t + m]
                    ins = nc.vector.tensor_copy(y, src) if g == 0 else nc.vector.tensor_tensor(y, y, src, ALU.add)
                    ins.then_inc(evicted[(u + m) % 2], 1)

        def first_inputs_dve(dve):
            for t in range(6):
                item_split(dve, ("xs", 0, t), split_lo)
                item_dve(dve, ("xs", 0, t))

        def chunk_ready(dve, g, c):
            heads = slice(8 * g, 8 * g + 8)
            n = CH * g + c
            cols = slice(c * P, (c + 1) * P)
            abc = steps_abc[:, n % 2]
            dve.wait_ge(abc_in[n % 2], 16 * (n // 2 + 1))
            if n >= 1:
                dve.wait_ge(x_end_used, n)
            nc.vector.tensor_tensor(dec_end[:, n % 2].unsqueeze(2), abc[:, :, P - 1:P], acum_tok[:, c, heads].unsqueeze(2), ALU.subtract) \
                .then_inc(dec_args, 1)
            wait(dve, end_ready, n)
            for h in range(8):
                ins = nc.vector.tensor_scalar(seg[:, h], abc[:, h], acum_tok[:, c, 8 * g + h:8 * g + h + 1], 0.0, ALU.subtract, ALU.min)
            ins.then_inc(seg_args, 1)
            dve.wait_ge(ssm_turned, n + 1)
            x3 = x_dt[:, n % 2].rearrange("p (h d) -> p h d", h=8)
            dt3 = dt_tok[:, c, heads].unsqueeze(2).broadcast_to([P, 8, 64])
            dve_chain.mark(nc.vector.tensor_tensor(x3, bank(4, SEQ).rearrange("p (h d) -> p h d", h=8), dt3, ALU.mult))
            nc.vector.tensor_copy(b_tok[:], flat[:, 2560:2560 + P])
            dve_chain.mark(nc.vector.tensor_tensor(cb[:], flat[:, 2688:2688 + P], tri[:], ALU.mult))
            dve.wait_ge(dec_exp, n + 1)
            dve_chain.settle(dve)
            nc.vector.tensor_tensor(x_dec[:].rearrange("p (h d) -> p h d", h=8), x3,
                                    dec_end[:, n % 2].unsqueeze(2).broadcast_to([P, 8, 64]), ALU.mult).then_inc(x_end_used, 1)
            dve.wait_ge(seg_exp, n + 1)
            nc.vector.tensor_tensor(seg[:], seg[:], cb[:].unsqueeze(1).broadcast_to([P, 8, P]), ALU.mult)
            dve.wait_ge(abc_exp, n + 1)
            nc.vector.tensor_tensor(c_dec[:], abc, c_row[g % 2][:, cols].unsqueeze(1).broadcast_to([P, 8, P]), ALU.mult).then_inc(y_ready, 1)

        def chunk_end(dve, g, c):
            n = CH * g + c
            cols = slice(c * P, (c + 1) * P)
            dve.wait_ge(end_ready, n + 1)
            if c < CH - 1:
                s3 = state[:].rearrange("p (h d) -> p h d", h=8)
                if c == 0:
                    ins = nc.vector.tensor_copy(state[:], bank(7, SEQ))
                else:
                    dve_chain.mark(nc.vector.tensor_tensor(s3, s3, steps_abc[:, n % 2, :, P - 1:P].broadcast_to([P, 8, 64]), ALU.mult))
                    dve_chain.settle(dve)
                    ins = nc.vector.tensor_tensor(state[:], state[:], bank(7, SEQ), ALU.add)
                dve_chain.mark(ins)
            x = xs[g % 2]
            for t in range(4):
                d = PARAM["d_skip"] + 4 * g + t
                ins = nc.vector.scalar_tensor_tensor(x[:, t, cols], x[:, t, cols], par[:, d:d + 1],
                                                     flat[:, 3072 + t * P:3072 + (t + 1) * P], ALU.mult, ALU.add)
            ins.then_inc(y_done, 1)
            dve_chain.settle(dve)
            nc.vector.tensor_copy(small[:, 16:17], small[:, 4:5]).then_inc(abc_used, 1)

        def finish_norm_dve(dve, g):
            x = xs[g % 2]
            dve.wait_ge(ssm_var, g + 1)
            nc.vector.tensor_scalar(g_rt, bank(1, SEQ), RMS_EPS, None, ALU.add).then_inc(ssm_veps, 1)
            dve.wait_ge(ssm_root, g + 1)
            dve_chain.mark(nc.vector.reciprocal(g_rt, g_rt))
            dve_chain.settle(dve)
            for t in range(4):
                k = PARAM["ssm_norm"] + 4 * g + t
                nc.vector.scalar_tensor_tensor(x[:, t], x[:, t], par[:, k:k + 1], g_rt, ALU.mult, ALU.mult).then_inc(u_norm, 1)

        def finish_lo_dve(dve, g):
            x = xs[g % 2]
            for t in range(4):
                dve.wait_ge(u_hi_s, 4 * g + t + 1)
                nc.vector.tensor_tensor(u_lo[:, t, META:T], x[:, t], u_hi[:, t, META:T], ALU.subtract).then_inc(u_lo_s, 1)

        def ssm_dve(dve, g):
            for c, items in enumerate(group_items(g)):
                if g < SSM_GROUPS:
                    chunk_ready(dve, g, c)
                for i, item in enumerate(items):
                    item_split(dve, item, split_lo)
                    if g and c == 0 and i == 0:
                        finish_norm_dve(dve, g - 1)
                    if g and c == 0 and i == (0 if item[0] == "z" else 1):
                        finish_lo_dve(dve, g - 1)
                        item_dve(dve, items[0])
                    if not (g and c == 0 and i == 0):
                        item_dve(dve, item)
                if g < SSM_GROUPS:
                    chunk_end(dve, g, c)
            if g < SSM_GROUPS:
                dve.wait_ge(y_done, CH * g + CH)
                dve.wait_ge(z_ready, g + 1)
                for t in range(4):
                    nc.vector.tensor_tensor(xs[g % 2][:, t], xs[g % 2][:, t], z_buf[:, t], ALU.mult).then_inc(u_done, 1)

        x_end_used, merged_out, merged_in = sem("x_end_used"), sem("merged_out"), sem("merged_in")

        m_hi = nc.alloc_sbuf_tensor_at("m_hi", [P, KT, T], F32R, offset=ssm_work2)
        m_lo = nc.alloc_sbuf_tensor_at("m_lo", [P, KT, T], F32R, offset=ssm_work2 + KT * T * 4)
        assert ssm_work2 + 2 * KT * T * 4 <= nc.sbuf_usable_end
        LAST = SSM_GROUPS - 1

        def mix_pe(pe):
            for k in range(4):
                so_pe(pe, LAST, k)
            pe_stage(pe, "mix_out", m_hi, m_lo, False, ready=(m_lo_s, 0))

        def mix_act(act):
            act.wait_ge(u_norm, 4 * SSM_GROUPS)
            for k in range(4):
                split_hi(act, Step(FIRST_CHUNK[f"so{LAST}"] + k + AHEAD))
                for f in (2 * k, 2 * k + 1):
                    act.wait_ge(m_sum, f + 1)
                    nc.scalar.activation(m_hi[:, f:f + 1, META:T], merged[:, f:f + 1], ACT.Copy).then_inc(m_hi_s, 1)
            only_split(act, split_hi, "mix_out")

        def mix_dve(dve):
            for k in range(4):
                item_split(dve, ("so", LAST, k), split_lo)
                item_dve(dve, ("so", LAST, k))
                u = FIRST_TILE[f"so{LAST}"] + 2 * k
                tiles_out(dve, u + 2)
                if k == 0:
                    dve.wait_ge(merged_in, 16)
                for f in (2 * k, 2 * k + 1):
                    dve_chain.mark(nc.vector.tensor_tensor(gates[:, f], gates[:, f], y_ssm[:, f], ALU.mult))
                dve_chain.settle(dve)
                for f in (2 * k, 2 * k + 1):
                    nc.vector.tensor_tensor(merged[:, f], merged[:, f], gates[:, f], ALU.add).then_inc(m_sum, 1)
                for f in (2 * k, 2 * k + 1):
                    dve.wait_ge(m_hi_s, f + 1)
                    nc.vector.tensor_tensor(m_lo[:, f, META:T], merged[:, f], m_hi[:, f, META:T], ALU.subtract).then_inc(m_lo_s, 1)
            residual_dve(dve, "mix_out", False, 1.0)

        rms_ffn = Norm("rms_ffn", FIRST_TILE["gv0"], False, PARAM["norm_ffn"], eps=RMS_EPS)
        placed["next"] = shared
        f_hi = at("f_hi", [P, 8, T], F32R)
        f_lo = at("f_lo", [P, 8, T], F32R)
        f_in = at("f_in", [P, 4, SEQ + 4])
        f_conv = at("f_conv", [P, 4, SEQ])
        f_zero, f_conved, f_silu, f_prod, f_hi_s, f_lo_s = (sem(n) for n in ("f_zero", "f_conved", "f_silu", "f_prod", "f_hi_s", "f_lo_s"))
        GROUPS = (8, 8, 6)

        def ffn_pool(pool):
            pool.wait_ge(norm_lo, rms_ffn.lo_at)
            nc.gpsimd.memset(f_in[:, :, 0:2], 0.0).then_inc(f_zero, 1)

        def ffn_pe(pe):
            done = 0
            for g, n in enumerate(GROUPS):
                pe_stage(pe, f"gv{g}", x_hi, x_lo, False, ready=None if g else rms_ffn.ready)
                loop(pe, 8, 4, lambda t: chunk_products(pe, f"fd{g}", t, f_hi, f_lo, False, nk=n,
                                                        ready=(f_lo_s, done) if not t.stride and t.start == 0 else None), peel=1)
                done += n

        def ffn_act(act):
            act.wait_ge(f_zero, 1)
            f0 = 0
            for g, n in enumerate(GROUPS):
                name = f"gv{g}"

                def keep(t, done):
                    pair = t.over(2).plus(f0)
                    slot = 2 * (t.start // 2 % 2) + t.start % 2
                    u = t.plus(FIRST_TILE[name])
                    act.wait_ge(chunk_done, done)
                    wait(act, f_conved, pair.at(2, t.start % 2 - 3))
                    nc.scalar.activation(f_in[:, slot:slot + 1, 2:2 + SEQ], tile_out(u, False), ACT.Copy).then_inc(evicted[u.mod(2)], 1)
                    if t.start % 2:
                        act.wait_ge(f_conved, pair.at(2, 1))
                        nc.scalar.activation(f_conv[:, slot - 1], f_conv[:, slot - 1], ACT.Silu).then_inc(f_silu, 1)
                        act.wait_ge(f_prod, pair.at(1, 1))
                        nc.scalar.activation(f_hi[:, one(t.over(2)), META:T], f_conv[:, slot:slot + 1], ACT.Copy).then_inc(f_hi_s, 1)
                side_stage(act, split_hi, name, keep, peel=1 if g == 0 else 0)
                only_split(act, split_hi, f"fd{g}")
                f0 += n

        def ffn_dve(dve):
            f0 = 0
            for g, n in enumerate(GROUPS):
                name = f"gv{g}"

                def conv(t, done):
                    pair = t.over(2).plus(f0)
                    slot = 2 * (t.start // 2 % 2) + t.start % 2
                    u = t.plus(FIRST_TILE[name])
                    half = FFN2 * (t.start % 2)
                    dve.wait_ge(evicted[u.mod(2)], u.over(2).at(plus=1))
                    wait(dve, f_lo_s, pair.at(1, -1))

                    def col(j):
                        return one(pair.plus(PARAM["conv_ffn_w"] + 44 * j + half))
                    convolve(dve, f_conv[:, slot], 3, col, f_in[:, slot], one(pair.plus(PARAM["conv_ffn_b"] + half)), f_conved)
                    if t.start % 2:
                        dve.wait_ge(f_silu, pair.at(1, 1))
                        dve.wait_ge(f_conved, pair.at(2, 2))
                        o = f_conv[:, slot]
                        nc.vector.tensor_tensor(o, o, f_conv[:, slot - 1], ALU.mult).then_inc(f_prod, 1)
                        dve.wait_ge(f_hi_s, pair.at(1, 1))
                        row = one(t.over(2))
                        nc.vector.tensor_tensor(f_lo[:, row, META:T], f_conv[:, slot:slot + 1], f_hi[:, row, META:T], ALU.subtract).then_inc(f_lo_s, 1)
                side_stage(dve, split_lo, name, conv, peel=1 if g == 0 else 0, chains=[(dve_chain, 2)])
                residual_dve(dve, f"fd{g}", False, 1.0)
                f0 += n

        final = Norm("final", TOTAL_TILES, False, PARAM["norm_final"], eps=RMS_EPS, last=True)

        stored = sem("stored")
        block = ctx.enter_context(nc.Block())

        @block.sync
        def _(sp):
            stream_weights(sp)
            sp.wait_ge(norm_scaled, KT * norms["all"])
            sp.dma_start(out, final.y[:, :, META:T]).then_inc(stored, 16)
            sp.wait_ge(stored, 16)

        @block.gpsimd
        def _(pool):
            even_loads(pool)
            ret_loads(pool)
            dsa_loads(pool)
            ssm_loads(pool)
            ffn_pool(pool)

        @block.tensor
        def _(pe):
            pe.wait_ge(x_split_lo, KT)
            pe_stage(pe, "qk", x_hi, x_lo, True)
            chunk_products(pe, "forget", Step(0), x_hi, x_lo, True)
            v_pe(pe)
            even_attention_pe(pe)
            pe.wait_ge(diff_lo_s, DIFF_HEADS)
            pe_stage(pe, "even_out", x_hi, x_lo, True, after=lambda k: ln00.add_mean(pe, k))
            ln00.pe(pe)
            mlp0.pe(pe, ln00, ln01)
            ln01.pe(pe)
            retention_pe(pe)
            ln10.pe(pe)
            mlp1.pe(pe, ln10, ln11)
            ln11.pe(pe)
            rms_mix.pe(pe)
            select_pe(pe)
            sparse_pe(pe)
            att_merge_pe(pe)
            dt_pe(pe)
            first_inputs_pe(pe)
            for g in range(SSM_GROUPS + 1):
                ssm_pe(pe, g)
            mix_pe(pe)
            rms_ffn.pe(pe)
            ffn_pe(pe)
            final.pe(pe)

        @block.scalar
        def _(act):
            even_act_start(act)
            qk_act(act)
            forget_act(act)
            v_act(act)
            even_attention_act(act)
            only_split(act, split_hi, "even_out")
            ln00.act(act)
            mlp0.act(act)
            ln01.act(act)
            retention_act(act)
            ln10.act(act)
            mlp1.act(act)
            ln11.act(act)
            rms_mix.act(act)
            select_act(act)
            sparse_act(act)
            att_merge_act(act)
            dt_act(act)
            first_inputs_act(act)
            for g in range(SSM_GROUPS + 1):
                ssm_act(act, g)
            mix_act(act)
            rms_ffn.act(act)
            ffn_act(act)
            final.act(act)

        @block.vector
        def _(dve):
            even_dve_start(dve)
            only_split(dve, split_lo, "qk")
            forget_dve(dve)
            v_dve(dve)
            even_attention_dve(dve)
            residual_dve(dve, "even_out", True, ALPHA)
            ln00.dve(dve)
            mlp0.dve(dve)
            ln01.dve(dve)
            retention_dve(dve)
            ln10.dve(dve)
            mlp1.dve(dve)
            ln11.dve(dve)
            rms_mix.dve(dve)
            select_dve(dve)
            sparse_dve(dve)
            att_merge_dve(dve)
            dt_dve(dve)
            first_inputs_dve(dve)
            for g in range(SSM_GROUPS + 1):
                ssm_dve(dve, g)
            mix_dve(dve)
            rms_ffn.dve(dve)
            ffn_dve(dve)
            final.dve(dve)


def pack(w):
    even, eo, r, ro = w["even_w_in"][0], w["even_w_out"][0], w["ret_w_in"][0], w["ret_w_out"][0]
    w2, parts = w["w_in_2"][0], []

    def cols(m, c0, n, rows=(0, 1024)):
        for c in range(n):
            for r0 in range(rows[0], rows[1], 1024):
                chunk = np.zeros((P, 8, P), np.float32)
                block = m[r0:min(r0 + 1024, rows[1]), c0 + c * P:min(c0 + (c + 1) * P, m.shape[1])]
                k = block.shape[0] // P
                chunk[:, 0:k, 0:block.shape[1]] = block.reshape(k, P, -1).transpose(1, 0, 2)
                parts.append(chunk)

    cols(even, 0, 8)
    cols(even, 1536, 8)
    cols(even, 3072, 1)
    cols(even, 1024, 4)
    cols(even, 2560, 4)
    cols(eo, 0, 8)

    def mlp(layer):
        for half in range(2):
            cols(w["ffn_w1"][layer], 2048 * half, 16)
            cols(w["ffn_w2"][layer], 0, 8, (2048 * half, 2048 * half + 2048))
    mlp(0)
    for h in range(RET_HEADS):
        cols(r, 256 * h, 2)
        cols(r, 1024 + 256 * h, 2)
        cols(r, 2048 + 512 * h, 4)
        cols(r, 4096 + 512 * h, 4)
        if h % 2:
            cols(ro, 0, 8, (1024 * (h // 2), 1024 * (h // 2) + 1024))
    mlp(1)
    cols(w2, 0, 8)
    cols(w2, 1024, 1)
    cols(w2, 1152, 4)
    k_idx = w2[:, 1664:1728]
    cols(np.concatenate([k_idx, k_idx], 1), 0, 1)
    cols(w2[:, 1728:1736], 0, 1)
    cols(w["w_att_out_2"][0], 0, 8)
    cols(w2, 6888, 8)
    cols(w2[:, 6856:6888], 0, 1)
    def ssm(kind, g):
        if kind == "xs":
            cols(w2, 3784 + 512 * g, 4)
            cols(w2, 3784 + 2048 + 128 * g, 1)
            cols(w2, 3784 + 2560 + 128 * g, 1)
        elif kind == "z":
            cols(w2, 1736 + 512 * g, 4)
        else:
            rows = w["w_ssm_out_2"][0][512 * g:512 * g + 512]
            for c in range(4):
                parts.append(rows[:, 256 * c:256 * c + 256].reshape(4, P, 2 * P).transpose(1, 0, 2).reshape(P, 8, P))
    for name, _ in STAGES:
        if name[:-1] in ("xs", "z", "so"):
            ssm(name[:-1], int(name[-1]))
        elif name == "gate_ssm":
            cols(w2, 6888 + 1024, 8)
    cols(w["w_out_2"][0], 0, 8)
    up, down, f = w["w_ffn_up_2"][0], w["w_ffn_down_2"][0], 0
    for n in (8, 8, 6):
        for t in range(f, f + n):
            cols(up, t * P, 1)
            cols(up, (FFN2 + t) * P, 1)
        cols(down, 0, 8, (f * P, (f + n) * P))
        f += n
    assert len(parts) == TOTAL_CHUNKS
    return np.stack(parts).reshape(TOTAL_CHUNKS, P, 8 * P)


def pack_params(w):
    out = np.zeros((P, PARAMS), np.float32)

    def put(name, a):
        a = np.asarray(a)
        out[:a.shape[-1], PARAM[name]:PARAM[name] + a.shape[0]] = a.T
    put("ln_g", w["ln_g"].reshape(32, P))
    put("ln_b", w["ln_b"].reshape(32, P))
    put("subln_g", w["diff_subln_g"])
    put("f_bias", w["even_f_bias"])
    put("norm_mix", w["norm_mix_2"].reshape(8, P))
    put("norm_ffn", w["norm_ffn_2"].reshape(8, P))
    put("norm_final", w["norm_final_2"].reshape(8, P))
    put("kv_norm", w["kv_norm_2"])
    put("conv_ssm_w", w["conv_ssm_w_2"][0].reshape(96, P))
    put("conv_ssm_b", w["conv_ssm_b_2"].reshape(24, P))
    put("ssm_norm", w["ssm_norm_2"].reshape(16, P))
    put("d_skip", np.repeat(w["d_skip_2"][0], 64).reshape(16, P))
    put("dt_bias", w["dt_bias_2"])
    put("a_log", w["a_log_2"])
    put("conv_ffn_w", w["conv_ffn_w_2"][0].reshape(132, P))
    put("conv_ffn_b", w["conv_ffn_b_2"].reshape(44, P))
    out[:, PARAM["rel_far"]:PARAM["rel_far"] + 16] = w["rel_bias_2"][31][None]
    return out


def shape_tables():
    out = np.zeros((P, TABLES), np.float32)

    def put(name, a):
        out[:a.shape[0], TABLE[name]:TABLE[name] + a.shape[1]] = a
    r, m = np.arange(P)[:, None], np.arange(P)[None]
    put("ident", np.eye(P))
    put("tri", (m >= r).astype(np.float32))
    sel = np.zeros((8, 8, P), np.float32)
    sel[np.arange(8), np.arange(8)] = 1
    put("sel", sel.reshape(8, -1))
    q, k = META + 384 + np.arange(P)[:, None], np.arange(T)[None]
    put("causal", np.where(k <= q, 0, NEG))
    seen = (k + 48) // 64 <= (q + 48) // 64
    slopes = 2.0 ** (-8.0 * np.arange(1, 5) / 4)
    put("alibi", np.concatenate([np.where(seen, -s * np.abs(q - k), NEG) for s in slopes], 1))
    gamma = 1 - 2.0 ** (-5.0 - np.arange(RET_HEADS))
    m = np.arange(SEQ)[None]
    put("decay", np.concatenate([np.where(r // 64 <= m // 64, g ** np.abs(m - r), 0) for g in gamma], 1))
    s = np.arange(META)[:, None]
    put("decay_meta", np.concatenate([g ** (META + m - s) for g in gamma], 1))
    dist = 511 - np.arange(640)
    n = np.maximum(dist, 0)
    large = 16 + (np.log(np.maximum(n, 1).astype(np.float32) / 16) / np.float32(math.log(8)) * 16).astype(np.int32)
    bucket = np.where(n < 16, n, np.minimum(large, 31))
    put("bucket", (np.arange(32)[:, None] == bucket[None]).astype(np.float32))
    return out


def kernel(**inputs):
    import concourse.bacc as _bacc
    from concourse.bass_utils import run_bass_kernel_spmd as _run

    w = {k: np.asarray(v) for k, v in inputs.items()}
    tokens = np.concatenate([w["meta_tokens"], w["x"][0]], 0)
    arrays = {
        "x_by_feature": np.ascontiguousarray(tokens.T.reshape(KT, P, T).transpose(1, 0, 2)),
        "weights": pack(w),
        "params": pack_params(w),
        "tables": shape_tables(),
        "lam": np.ascontiguousarray(np.broadcast_to(w["diff_lambda"].reshape(1, 256), (P, 256))),
        "w_uk": np.ascontiguousarray(w["w_uk_2"][0].reshape(8, P, P).transpose(1, 0, 2)),
        "w_uv": np.ascontiguousarray(w["w_uv_2"][0].transpose(2, 0, 1).reshape(P, 1024)),
        "rel": np.ascontiguousarray(w["rel_bias_2"]),
    }
    nc = _bacc.Bacc("TRN2", target_bir_lowering=False, num_devices=1)
    args = [nc.dram_tensor(f"in_{k}", a.shape, F32, kind="ExternalInput").ap() for k, a in arrays.items()]
    line = nc.dram_tensor("bias_line", (ATT_HEADS, 640), F32, kind="Internal").ap()
    skewed = nc.dram_tensor("bias_skewed", (ATT_HEADS, SKEW), F32, kind="Internal").ap()
    acum = nc.dram_tensor("acum_rows", (32, SEQ), F32, kind="Internal").ap()
    out = nc.dram_tensor("out", (P, KT, SEQ), F32, kind="ExternalOutput").ap()
    merged = nc.dram_tensor("merged_kept", (P, KT * SEQ), F32, kind="Internal").ap()
    program(nc, *args, line, skewed, acum, merged, out)
    r = _run(nc, [{f"in_{k}": a for k, a in arrays.items()}], core_ids=[0])
    return np.ascontiguousarray(r.results[0]["out"].transpose(2, 1, 0).reshape(1, SEQ, D))
```

```python
import math
from contextlib import ExitStack

import concourse.bass as bass
import numpy as np
from concourse import mybir

ALU = mybir.AluOpType
ACT = mybir.ActivationFunctionType
F32 = mybir.dt.float32
F32R = mybir.dt.float32r

P = 128
D = 1024
KT = D // P
META = 16
SEQ = 512
T = META + SEQ
HALF = T // 2
QT = SEQ // P
NEG = -1.0e30
FILL = -3.0e38
FIRST_MIN = 3.0e38
ALPHA = 4.0 ** 0.25
LN_EPS = 1e-5
RMS_EPS = 1e-6
LAM_INIT = 0.8 - 0.6 * math.exp(-0.3 * 0)

DIFF_HEADS, FOX_HEADS, RET_HEADS = 4, 8, 4
ATT_HEADS, IDX_HEADS = 16, 8
SSM_GROUPS, HEADS_PER_GROUP = 4, 8
FFN2 = 2816 // P

SKEW = 641 * P

RING = 4
AHEAD = RING - 1

STAGES = [("qk", 16), ("forget", 1), ("v", 8), ("even_out", 8),
          ("up0a", 16), ("down0a", 16), ("up0b", 16), ("down0b", 16)]
STAGES += [("ret0", 12), ("ret1", 12), ("ret2", 12), ("ret_out0", 8), ("ret3", 12), ("ret_out1", 8)]
STAGES += [("up1a", 16), ("down1a", 16), ("up1b", 16), ("down1b", 16)]
STAGES += [("latq", 8), ("latc", 1), ("idxq", 4), ("idxk", 1), ("idxw", 1), ("gate_att", 8)]
STAGES += [("z1", 4), ("z2", 4), ("gate_ssm_a", 4), ("att_out", 8), ("dt", 1)]
STAGES += [("xs0", 6), ("xs1", 6), ("z0", 4), ("xs2", 6), ("so0", 4), ("xs3", 6), ("so1", 4)]
STAGES += [("z3", 4), ("so2", 4), ("gate_ssm_b", 4), ("so3", 4), ("mix_out", 8)]
STAGES += [s for g, n in enumerate((8, 8, 6)) for s in ((f"gv{g}", 2 * n), (f"fd{g}", 8))]
CHUNKS = dict(STAGES)
KGROUPS = {n: 2 for n in ("down0a", "down0b", "down1a", "down1b")}
FIRST_CHUNK, FIRST_TILE = {}, {}
_c = _t = 0
for _n, _k in STAGES:
    FIRST_CHUNK[_n], FIRST_TILE[_n] = _c, _t
    _c += _k
    _t += 2 * _k if _n.startswith("so") else _k // KGROUPS.get(_n, 1)
TOTAL_CHUNKS, TOTAL_TILES = _c, _t

KEPT = [(n, t) for n in ("z1", "z2", "gate_ssm_a") for t in range(4)]
KEPT_EARLY = 3

PARAM = {}
_c = 0
for _n, _k in [("ln_g", 32), ("ln_b", 32), ("subln_g", 1), ("f_bias", 1), ("norm_mix", 8), ("norm_ffn", 8),
               ("norm_final", 8), ("kv_norm", 1), ("conv_ssm_w", 96), ("conv_ssm_b", 24), ("ssm_norm", 16),
               ("d_skip", 16), ("dt_bias", 1), ("a_log", 1), ("conv_ffn_w", 132), ("conv_ffn_b", 44),
               ("rel_far", 16)]:
    PARAM[_n] = _c
    _c += _k
PARAMS = _c


class Step:

    def __init__(self, start, i=0, stride=0):
        self.start, self.i, self.stride = start, i, stride

    def plus(self, k):
        return Step(self.start + k, self.i, self.stride)

    def over(self, n):
        assert self.stride % n == 0
        return Step(self.start // n, self.i, self.stride // n)

    def mod(self, n):
        assert self.stride % n == 0
        return self.start % n

    def at(self, factor=1, plus=0):
        fixed = self.start * factor + plus
        return fixed + self.i * (self.stride * factor) if self.stride else fixed


def loop(eng, n, unroll, body, peel=0, tail=0, chains=()):
    done = peel * unroll
    turns = (n - done) // unroll - tail
    for t in range(done):
        body(Step(t))
    if turns >= 2:
        before = [chain.count for chain, _ in chains]
        with eng.Fori(0, turns) as i:
            for chain, per_step in chains:
                chain.turn = i * (per_step * unroll)
            for j in range(unroll):
                body(Step(done + j, i, unroll))
        for (chain, per_step), first in zip(chains, before):
            assert chain.count == first + per_step * unroll
            chain.count, chain.turn = first + per_step * unroll * turns, 0
        done += turns * unroll
    for t in range(done, n):
        body(Step(t))


def wait(eng, sem, value):
    if not isinstance(value, int) or value > 0:
        eng.wait_ge(sem, value)


class Chain:

    def __init__(self, sem):
        self.sem, self.count, self.turn = sem, 0, 0

    def mark(self, ins):
        ins.then_inc(self.sem, 1)
        self.count += 1

    def settle(self, eng):
        eng.wait_ge(self.sem, self.turn + self.count)


def one(step):
    return bass.ds(step.at(), 1) if step.stride else slice(step.start, step.start + 1)


TABLE = {}
_c = 0
for _n, _k in [("ident", P), ("tri", P), ("causal", P), ("alibi", DIFF_HEADS * T),
               ("decay", RET_HEADS * SEQ), ("decay_meta", RET_HEADS * SEQ), ("bucket", 640)]:
    TABLE[_n] = _c
    _c += _k
TABLES = _c


def program(nc, x_in, weights, params, tables, lam_in, w_uk, w_uv, rel, line, skewed, cum_dram, acum_dram, merged_dram, kept_dram, gate_dram, out, until="end"):
    with ExitStack() as ctx:
        def sb(name, shape, dt=F32):
            return ctx.enter_context(nc.sbuf_tensor(name, shape, dt))

        def sem(name):
            return ctx.enter_context(nc.semaphore(name))

        raw = sb("raw", [P, RING, 8, P])
        w_hi = sb("w_hi", [P, RING, 8, P], F32R)
        w_lo = sb("w_lo", [P, RING, 8, P], F32R)
        x32 = sb("x32", [P, KT, T])
        x_hi = sb("x_hi", [P, KT, T], F32R)
        x_lo = sb("x_lo", [P, KT, T], F32R)
        ident = sb("ident", [P, P])
        ones_d = sb("ones_d", [P, P])
        ones_h = sb("ones_h", [P, P])
        ones_g = sb("ones_g", [P, P])
        par = sb("par", [P, PARAMS])
        small = sb("small", [P, 64])
        shared = nc.sbuf_base
        placed = {}

        def at(name, shape, dt=F32, start=None):
            off = placed["next"] if start is None else start
            off = (off + 31) // 32 * 32
            size = int(np.prod(shape[1:])) * 4
            assert off + size <= nc.sbuf_usable_end, (name, off + size, nc.sbuf_usable_end)
            placed["next"] = off + size
            return nc.alloc_sbuf_tensor_at(name, shape, dt, offset=off)

        ps = ctx.enter_context(nc.psum_tensor("ps", [P, 8, 512], F32))
        flat = ps[:, :, :].rearrange("p b n -> p (b n)")

        def bank(b, n=1024, rows=slice(0, P)):
            return flat[rows, b * 512:b * 512 + n]

        landed = [sem(f"landed{s}") for s in range(RING)]
        hi_ready = sem("hi_ready")
        lo_ready = sem("lo_ready")
        chunk_done = sem("chunk_done")
        evicted = [sem(f"evicted{s}") for s in range(2)]
        dve_own, act_own, pool_own = sem("dve_own"), sem("act_own"), sem("pool_own")
        dve_chain, act_chain, pool_chain = Chain(dve_own), Chain(act_own), Chain(pool_own)
        loaded = sem("loaded")
        x_landed = [sem(f"x_landed{n}") for n in range(4)]

        def tiles_out(eng, tile):
            for s in range(2):
                wait(eng, evicted[s], (tile - s + 1) // 2)

        def stream_weights(sp):
            def body(g):
                s = g.mod(RING)
                if not g.stride and g.start == 1:
                    sp.wait_ge(x_landed[3], 16)
                wait(sp, lo_ready, g.at(plus=1 - RING))
                src = weights[one(g), :, :].rearrange("g p n -> p (g n)")
                sp.dma_start(raw[:, s, :, :].rearrange("p k n -> p (k n)"), src).then_inc(landed[s], 16)
            loop(sp, TOTAL_CHUNKS, RING, body, peel=1)

        def split_hi(act, g):
            if not g.stride and g.start >= TOTAL_CHUNKS:
                return
            s = g.mod(RING)
            act.wait_ge(landed[s], g.over(RING).at(16, 16))
            wait(act, chunk_done, g.at(plus=1 - RING))
            nc.scalar.activation(w_hi[:, s], raw[:, s], ACT.Copy).then_inc(hi_ready, 1)

        def split_lo(dve, g):
            if not g.stride and g.start >= TOTAL_CHUNKS:
                return
            s = g.mod(RING)
            dve.wait_ge(hi_ready, g.at(plus=1))
            nc.vector.tensor_tensor(w_lo[:, s], raw[:, s], w_hi[:, s], ALU.subtract).then_inc(lo_ready, 1)

        def tile_out(tile, wide):
            s = tile.mod(2)
            return ps[:, 2 * s:2 * s + 2, 0:HALF] if wide else ps[:, 2 * s:2 * s + 1, 0:SEQ]

        def halves(ap, wide):
            return ap[:, 0:T].rearrange("p (h n) -> p h n", h=2) if wide else ap[:, META:T].rearrange("p (h n) -> p h n", h=1)

        def chunk_products(pe, name, t, act_hi, act_lo, wide, nk=8, k0=0, start=True, stop=True, ready=None):
            kg = KGROUPS.get(name, 1)
            g = t.plus(FIRST_CHUNK[name])
            tile = t.over(kg).plus(FIRST_TILE[name])
            s = g.mod(RING)
            pe.wait_ge(lo_ready, g.at(plus=1))
            if start:
                wait(pe, evicted[tile.mod(2)], tile.over(2).at())
            o = tile_out(tile, wide)
            parts = [(h, slice(h * HALF, (h + 1) * HALF)) for h in range(2)] if wide else [(0, slice(META, T))]
            for k in range(nk):
                if ready:
                    pe.wait_ge(ready[0], ready[1] + k0 + k + 1)
                for n, (w, a) in enumerate(((w_hi, act_hi), (w_hi, act_lo), (w_lo, act_hi))):
                    for h, cols in parts:
                        last = nc.tensor.matmul(o[:, h, :], w[:, s, k], a[:, k0 + k, cols],
                                                start=start and k == 0 and n == 0, stop=stop and k == nk - 1 and n == 2)
            last.then_inc(chunk_done, 1)

        def pe_stage(pe, name, act_hi, act_lo, wide, ready=None, after=None):
            kg = KGROUPS.get(name, 1)

            def body(t):
                c = t.mod(kg) if kg > 1 else 0
                first = not t.stride and t.start < kg
                chunk_products(pe, name, t, act_hi, act_lo, wide, k0=8 * c, start=c == 0, stop=c == kg - 1,
                               ready=ready if first else None)
                if after and c == kg - 1:
                    after(t.over(kg).plus(-1))
            loop(pe, CHUNKS[name], 4, body, peel=1 if ready or after or FIRST_CHUNK[name] == 0 else 0)

        def side_stage(eng, split, name, evict, chains=(), peel=0, unroll=4):
            kg = KGROUPS.get(name, 1)
            last = FIRST_CHUNK[name] + CHUNKS[name] + AHEAD > TOTAL_CHUNKS

            def body(t):
                split(eng, t.plus(FIRST_CHUNK[name] + AHEAD))
                if t.mod(kg) == kg - 1 and evict:
                    evict(t.over(kg), t.plus(FIRST_CHUNK[name]).at(plus=1))
            loop(eng, CHUNKS[name], unroll, body, peel=max(peel, FIRST_CHUNK[name] == 0), tail=1 if last else 0,
                 chains=chains)

        placed["next"] = shared
        qk = at("qk", [P, 16, T])
        vt = at("vt", [P, 5, D])
        diff_o = at("diff_o", [P, DIFF_HEADS, T])
        alibi = at("alibi", [P, DIFF_HEADS, T])
        causal = at("causal", [P, P])
        cum_tok = at("cum_tok", [P, 5, FOX_HEADS])
        key_cum = at("key_cum", [P, 2, T])
        gate_bias = at("gate_bias", [P, 2, T])
        work = placed["next"]
        v_slot = at("v_slot", [P, 2, T])
        f_row = at("f_row", [FOX_HEADS, 4, T])
        neg_cum = f_row[:, 0]
        cum_f = f_row[:, 1]
        s_buf = at("s_buf", [P, 4, T], start=work)
        p_norm = at("p_norm", [P, 3, T])
        p_turn = at("p_turn", [P, 2, 5, P])
        stat = at("stat", [P, 4, 64])
        lam_row = at("lam_row", [P, 4, 64])
        even_end = placed["next"]

        products = [("a", h, j) for h in range(DIFF_HEADS) for j in range(5)]
        products += [("b", h, j) for h in range(FOX_HEADS) for j in range(5)]
        maps = {}
        for p, (kind, h, j) in enumerate(products):
            n = sum(len(m) for m in maps.values())
            maps[p] = [n, n + 1] if kind == "a" else [n]
        NPROD = len(products)
        product_of = {u: p for p in maps for u in maps[p]}
        v_turned, v_stored = sem("v_turned"), sem("v_stored")
        scored, masked, expd, normed = sem("scored"), sem("masked"), sem("expd"), sem("normed")
        turned, turn_kept, weighed = sem("turned"), sem("turn_kept"), sem("weighed")
        head_hi, head_lo = sem("head_hi"), sem("head_lo")
        forget_in, forget_ready, lam_ready = sem("forget_in"), sem("forget_ready"), sem("lam_ready")

        def q_rows(j):
            return (0, META) if j == 0 else (META + (j - 1) * P, P)

        def keys_of(j):
            return META if j == 0 else META + j * P

        def even_loads(pool):
            for dst, src in ((par[:], params), (ident[:], tables[:, 0:P]),
                             (alibi[:].rearrange("p h n -> p (h n)"), tables[:, TABLE["alibi"]:TABLE["alibi"] + 4 * T]),
                             (causal[:], tables[:, TABLE["causal"]:TABLE["causal"] + P]),
                             (lam_row[:].rearrange("p a n -> p (a n)"), lam_in)):
                pool.dma_start(dst, src).then_inc(loaded, 16)
            nc.gpsimd.memset(ones_d[:], 1.0 / D).then_inc(forget_in, 1)
            nc.gpsimd.memset(ones_h[:], 1.0 / P).then_inc(forget_in, 1)
            nc.gpsimd.memset(ones_g[:], 1.0 / 512).then_inc(forget_in, 1)
            nc.gpsimd.memset(f_row[:, 3, :], 1.0).then_inc(forget_in, 1)
            nc.gpsimd.memset(small[:, 12:13], LN_EPS).then_inc(forget_in, 1)
            nc.gpsimd.memset(small[:, 13:14], RMS_EPS).then_inc(forget_in, 1)
            pool.wait_ge(forget_ready, 1)
            pool.dma_start(cum_dram, neg_cum).then_inc(cum_out, 16)
            pool.wait_ge(cum_out, 16)
            for h in range(FOX_HEADS):
                if h >= 2:
                    pool.wait_ge(bias_made, 5 * (h - 1))
                src = bass.AP(tensor=cum_dram.tensor, offset=h * T, ap=[[0, P], [1, T]])
                pool.dma_start(key_cum[:, h % 2], src).then_inc(cum_in[h % 2], 16)

        LOADS = 5 * 16
        cum_out, cum_turned, cum_kept, bias_made, bias_ready = (
            sem(n) for n in ("cum_out", "cum_turned", "cum_kept", "bias_made", "bias_ready"))
        cum_in = [sem(f"cum_in{n}") for n in range(2)]
        x_split_hi, x_split_lo = sem("x_split_hi"), sem("x_split_lo")

        def even_act_start(act):
            for n in range(4):
                act.dma_start(x32[:, 2 * n:2 * n + 2], x_in[:, 2 * n:2 * n + 2]).then_inc(x_landed[n], 16)
            for k in range(KT):
                act.wait_ge(x_landed[k // 2], 16)
                nc.scalar.activation(x_hi[:, k], x32[:, k], ACT.Copy).then_inc(x_split_hi, 1)
            for g in range(AHEAD):
                split_hi(act, Step(g))

        def even_dve_start(dve):
            for k in range(KT):
                dve.wait_ge(x_split_hi, k + 1)
                nc.vector.tensor_tensor(x_lo[:, k], x32[:, k], x_hi[:, k], ALU.subtract).then_inc(x_split_lo, 1)
            for g in range(AHEAD):
                split_lo(dve, Step(g))

        def qk_act(act):
            def keep(tile, done):
                act.wait_ge(chunk_done, done)
                nc.scalar.activation(halves(qk[:, one(tile)].rearrange("p a n -> p (a n)"), True),
                                     tile_out(tile.plus(FIRST_TILE["qk"]), True), ACT.Copy,
                                     scale=0.125 if tile.mod(8) < 4 else 1.0) \
                    .then_inc(evicted[tile.mod(2)], 1)
            side_stage(act, split_hi, "qk", keep, unroll=8, peel=0)

        def forget_act(act):
            tile = Step(FIRST_TILE["forget"])
            split_hi(act, Step(FIRST_CHUNK["forget"] + AHEAD))
            act.wait_ge(chunk_done, FIRST_CHUNK["forget"] + 1)
            act.wait_ge(loaded, LOADS)
            bias = par[0:8, PARAM["f_bias"]:PARAM["f_bias"] + 1]
            act_chain.mark(nc.scalar.activation(halves(f_row[:, 0], True), tile_out(tile, True)[0:8], ACT.Identity, bias=bias))
            act_chain.settle(act)
            nc.scalar.activation(f_row[:, 1], f_row[:, 0], ACT.Abs).then_inc(evicted[tile.mod(2)], 1)
            act.wait_ge(evicted[tile.mod(2)], tile.start // 2 + 1)
            act_chain.mark(nc.scalar.activation(f_row[:, 1], f_row[:, 1], ACT.Exp, scale=-1.0))
            act_chain.settle(act)
            nc.scalar.activation(f_row[:, 2], f_row[:, 1], ACT.Ln, bias=1.0).then_inc(forget_in, 1)

        def forget_dve(dve):
            split_lo(dve, Step(FIRST_CHUNK["forget"] + AHEAD))
            dve.wait_ge(forget_in, 7)
            dve_chain.mark(nc.vector.tensor_scalar(f_row[:, 1], f_row[:, 0], 0.0, None, ALU.min))
            dve_chain.settle(dve)
            dve_chain.mark(nc.vector.tensor_tensor(f_row[:, 2], f_row[:, 1], f_row[:, 2], ALU.subtract))
            dve_chain.settle(dve)
            dve_chain.mark(nc.vector.tensor_tensor_scan(cum_f, f_row[:, 3], f_row[:, 2], 0.0, ALU.mult, ALU.add))
            dve_chain.settle(dve)
            nc.vector.tensor_scalar(neg_cum, cum_f, -1.0, None, ALU.mult).then_inc(forget_ready, 1)

        def v_act(act):
            def keep(tile, done):
                act.wait_ge(chunk_done, done)
                wait(act, v_turned, tile.at(plus=-1))
                nc.scalar.activation(halves(v_slot[:, tile.mod(2)], True), tile_out(tile.plus(FIRST_TILE["v"]), True),
                                     ACT.Copy).then_inc(evicted[tile.plus(FIRST_TILE["v"]).mod(2)], 1)
            side_stage(act, split_hi, "v", keep, peel=1)

        def v_pe(pe):
            def turn(t):
                tile = FIRST_TILE["v"] + t
                pe.wait_ge(evicted[tile % 2], tile // 2 + 1)
                wait(pe, v_stored, t)
                for b in range(5):
                    c, n = q_rows(b)
                    o = 2048 + (512 if b == 0 else (b - 1) * P)
                    last = nc.tensor.transpose(flat[0:n, o:o + P], v_slot[:, t % 2, c:c + n], ident[:, :])
                last.then_inc(v_turned, 1)
            pe.wait_ge(loaded, LOADS)
            for t in range(8):
                chunk_products(pe, "v", Step(t), x_hi, x_lo, True)
                if t:
                    turn(t - 1)
            turn(7)

        def v_dve(dve):
            for t in range(8):
                split_lo(dve, Step(FIRST_CHUNK["v"] + t + AHEAD))
                dve.wait_ge(v_turned, t + 1)
                nc.vector.tensor_copy(vt[:, 1:5, t * P:(t + 1) * P], bank(4, 512).rearrange("p (b n) -> p b n", b=4))
                nc.vector.tensor_copy(vt[0:META, 0, t * P:(t + 1) * P], flat[0:META, 2560:2560 + P]).then_inc(v_stored, 1)

        def lam_dve(dve):
            for m in range(2):
                dve_chain.mark(nc.vector.tensor_tensor_reduce(lam_row[:, 2 * m], lam_row[:, 2 * m], lam_row[:, 2 * m + 1], 1.0, 0.0,
                                                              ALU.mult, ALU.add, small[:, m:m + 1]))
            dve_chain.settle(dve)
            nc.vector.tensor_scalar(small[:, 8:10], small[:, 0:2], 1.0, None, ALU.mult).then_inc(lam_ready, 1)
            dve.wait_ge(lam_ready, 2)
            dve_chain.mark(nc.vector.tensor_tensor(small[:, 4:5], small[:, 3:4], small[:, 2:3], ALU.subtract))
            dve_chain.settle(dve)
            dve_chain.mark(nc.vector.tensor_scalar(small[:, 4:5], small[:, 4:5], -LAM_INIT, None, ALU.add))
            g = PARAM["subln_g"]
            dve_chain.mark(nc.vector.tensor_scalar(small[:, 5:6], par[:, g:g + 1], 1.0 - LAM_INIT, None, ALU.mult))
            dve_chain.settle(dve)

        def lam_act(act):
            act.wait_ge(lam_ready, 1)
            nc.scalar.activation(small[:, 2:4], small[:, 8:10], ACT.Exp).then_inc(lam_ready, 1)

        def even_scores(pe, p):
            kind, h, j = products[p]
            (c, n), keys = q_rows(j), keys_of(j)
            for m, u in enumerate(maps[p]):
                if u >= 2:
                    pe.wait_ge(masked, u - 1)
                o = (u % 2) * 1024
                if kind == "a":
                    rows, qt, kt_ = slice(64 * m, 64 * m + 64), h, 4 + h
                else:
                    rows, qt, kt_ = slice(64 * (h % 2), 64 * (h % 2) + 64), 8 + h // 2, 12 + h // 2
                for a in range(0, keys, 512):
                    b = min(keys, a + 512)
                    last = nc.tensor.matmul(flat[0:n, o + a:o + b], qk[rows, qt, c:c + n], qk[rows, kt_, a:b], start=True, stop=True)
                last.then_inc(scored, 1)

        def even_mask(dve, p):
            kind, h, j = products[p]
            (c, n), keys = q_rows(j), keys_of(j)
            f0 = 400 if j == 0 else 528 - keys
            if kind == "b":
                dve.wait_ge(bias_ready, fox_before(p) + 1)
            for u in maps[p]:
                bias = alibi[0:n, h, f0:f0 + keys] if kind == "a" else gate_bias[0:n, p % 2, 0:keys]
                dve.wait_ge(scored, u + 1)
                if u >= 4:
                    dve.wait_ge(normed, product_of[u - 4] + 1)
                nc.vector.tensor_tensor_reduce(s_buf[0:n, u % 4, 0:keys], bank((u % 2) * 2, keys, slice(0, n)), bias, -1.0,
                                               FIRST_MIN, ALU.add, ALU.min, stat[0:n, 0, u % 64:u % 64 + 1]).then_inc(masked, 1)

        def fox_before(p):
            return max(p - 5 * DIFF_HEADS, 0)

        def even_bias(act, p):
            kind, h, j = products[p]
            if kind == "a":
                return
            n, keys = q_rows(j)[1], keys_of(j)
            act.wait_ge(cum_in[h % 2], 16 * (h // 2 + 1))
            act.wait_ge(cum_kept, 1)
            act.wait_ge(masked, maps[p - 2][-1] + 1)
            nc.scalar.activation(gate_bias[0:n, p % 2, 0:keys], key_cum[0:n, h % 2, 0:keys], ACT.Identity,
                                 bias=cum_tok[0:n, j, h:h + 1]).then_inc(bias_made, 1)

        def bias_mask(dve, p):
            kind, h, j = products[p]
            if kind == "a":
                return
            n, keys = q_rows(j)[1], keys_of(j)
            dve.wait_ge(bias_made, fox_before(p) + 1)
            d = gate_bias[0:n, p % 2, keys - n:keys]
            nc.vector.tensor_tensor(d, d, causal[0:n, 0:n], ALU.add).then_inc(bias_ready, 1)

        def even_exp(act, p):
            kind, h, j = products[p]
            n, keys = q_rows(j)[1], keys_of(j)
            for u in maps[p]:
                act.wait_ge(masked, u + 1)
                s = s_buf[0:n, u % 4, 0:keys]
                nc.scalar.activation(s, s, ACT.Exp, scale=-1.0, bias=stat[0:n, 0, u % 64:u % 64 + 1],
                                     accum_out=stat[0:n, 1, u % 64:u % 64 + 1]).then_inc(expd, 1)

        def even_norm(dve, p):
            kind, h, j = products[p]
            n, keys = q_rows(j)[1], keys_of(j)
            dve.wait_ge(expd, maps[p][-1] + 1)
            for u in maps[p]:
                q = u % 64
                dve_chain.mark(nc.vector.reciprocal(stat[0:n, 2, q:q + 1], stat[0:n, 1, q:q + 1]))
            dve_chain.settle(dve)
            if p >= 3:
                dve.wait_ge(turned, p - 2)
            q = maps[p][0] % 64
            o = p_norm[0:n, p % 3, 0:keys]
            ins = nc.vector.tensor_scalar(o, s_buf[0:n, maps[p][0] % 4, 0:keys], stat[0:n, 2, q:q + 1], None, ALU.mult)
            if kind == "a":
                dve_chain.mark(ins)
                dve_chain.mark(nc.vector.tensor_scalar(stat[0:n, 3, q:q + 1], stat[0:n, 2, q + 1:q + 2], small[0:n, 4:5], None, ALU.mult))
                dve_chain.settle(dve)
                ins = nc.vector.scalar_tensor_tensor(o, s_buf[0:n, maps[p][1] % 4, 0:keys], stat[0:n, 3, q:q + 1], o, ALU.mult, ALU.add)
            ins.then_inc(normed, 1)

        def even_turn(pe, p):
            n, j = q_rows(products[p][2])[1], products[p][2]
            pe.wait_ge(normed, p + 1)
            if p:
                pe.wait_ge(turn_kept, p)
            for b in range(j + 1):
                c, k = q_rows(b)
                o = 2048 + (512 if b == 0 else (b - 1) * P)
                last = nc.tensor.transpose(flat[0:k, o:o + n], p_norm[0:n, p % 3, c:c + k], ident[0:n, 0:n])
            last.then_inc(turned, 1)

        def even_keep_turned(act, p):
            n, j = q_rows(products[p][2])[1], products[p][2]
            act.wait_ge(turned, p + 1)
            if p >= 2:
                act.wait_ge(weighed, p - 1)
            if j:
                nc.scalar.activation(p_turn[:, p % 2, 0:j, :], bank(4, j * P).rearrange("p (b n) -> p b n", b=j), ACT.Copy)
            nc.scalar.activation(p_turn[0:META, p % 2, 4, 0:n], flat[0:META, 2560:2560 + n], ACT.Copy).then_inc(turn_kept, 1)

        def groups_before(p):
            return sum(1 for q in range(p) if ends_group(q))

        def ends_group(p):
            kind, h, j = products[p]
            return j == 4 and (kind == "a" or h % 2 == 1)

        def even_values(pe, p):
            kind, h, j = products[p]
            c, n = q_rows(j)
            pe.wait_ge(turn_kept, p + 1)
            done = groups_before(p)
            if done and (p == 0 or ends_group(p - 1)):
                pe.wait_ge(head_hi, done)
                wait(pe, head_lo, done - DIFF_HEADS)
            rows = slice(0, P) if kind == "a" else slice(64 * (h % 2), 64 * (h % 2) + 64)
            col = h * P if kind == "a" else 512 + h * 64
            wide = P if kind == "a" else 64
            o = 3072 + (512 if j == 0 else (j - 1) * P)
            for b in range(j + 1):
                k = q_rows(b)[1]
                last = nc.tensor.matmul(flat[rows, o:o + n], vt[0:k, b, col:col + wide],
                                        p_turn[0:k, p % 2, 4 if b == 0 else b - 1, 0:n], start=b == 0, stop=b == j)
            last.then_inc(weighed, 1)

        def even_keep_head(act, p):
            kind, h, j = products[p]
            if not ends_group(p):
                return
            act.wait_ge(weighed, p + 1)
            dst = diff_o[:, h] if kind == "a" else x_hi[:, 4 + h // 2]
            nc.scalar.activation(dst[:, META:T], bank(6, 512), ACT.Copy)
            nc.scalar.activation(dst[:, 0:META], bank(7, META), ACT.Copy).then_inc(head_hi, 1)

        def even_head_lo(dve, p):
            kind, h, j = products[p]
            if not ends_group(p) or kind == "a":
                return
            k = 4 + h // 2
            dve.wait_ge(head_hi, groups_before(p) + 1)
            nc.vector.tensor_tensor(x_lo[:, k, META:T], bank(6, 512), x_hi[:, k, META:T], ALU.subtract)
            nc.vector.tensor_tensor(x_lo[:, k, 0:META], bank(7, META), x_hi[:, k, 0:META], ALU.subtract).then_inc(head_lo, 1)

        def even_attention_pe(pe):
            pe.wait_ge(forget_ready, 1)
            pe.wait_ge(v_stored, 8)
            tiles_out(pe, FIRST_TILE["even_out"])
            for j in range(5):
                c, n = q_rows(j)
                last = nc.tensor.transpose(flat[0:n, 3072 + 8 * j:3080 + 8 * j], cum_f[:, c:c + n], ident[0:8, 0:8])
            last.then_inc(cum_turned, 1)
            pe.wait_ge(cum_kept, 1)
            for p in range(NPROD + 3):
                if p in MEANS:
                    head_means_pe(pe, p)
                if p < NPROD:
                    even_scores(pe, p)
                if 2 <= p < NPROD + 2:
                    even_turn(pe, p - 2)
                if 3 <= p:
                    even_values(pe, p - 3)

        MEANS = {26: (0, 1), 31: (2, 3)}

        def head_means_pe(pe, p):
            pe.wait_ge(masked, maps[p - 1][-1] + 1)
            for h in MEANS[p]:
                o = 2048 * (h % 2) // 2
                pe.wait_ge(head_sq, h + 1)
                nc.tensor.matmul(flat[:, o:o + 512], ones_h[:], diff_rt[:, h, META:T], start=True, stop=True)
                nc.tensor.matmul(flat[:, o + 512:o + 512 + META], ones_h[:], diff_rt[:, h, 0:META], start=True, stop=True).then_inc(head_mean, 1)
            pe.wait_ge(head_var, MEANS[p][1] + 1)

        def head_means_act(act, p):
            for h in MEANS[p]:
                o = 2048 * (h % 2) // 2
                act.wait_ge(head_mean, h + 1)
                nc.scalar.activation(diff_rt[:, h, META:T], flat[:, o:o + 512], ACT.Ln, bias=small[:, 13:14])
                nc.scalar.activation(diff_rt[:, h, 0:META], flat[:, o + 512:o + 512 + META], ACT.Ln, bias=small[:, 13:14]).then_inc(head_var, 1)

        head_sq, head_mean, head_var, head_root, head_t, diff_hi_s, diff_lo_s = (
            sem(n) for n in ("head_sq", "head_mean", "head_var", "head_root", "head_t", "diff_hi", "diff_lo"))
        diff_rt = alibi

        def even_attention_act(act):
            lam_act(act)
            for p in range(NPROD + 4):
                if 4 <= p:
                    even_keep_head(act, p - 4)
                if 3 <= p < NPROD + 3:
                    even_keep_turned(act, p - 3)
                if p in MEANS:
                    head_means_act(act, p)
                if p < NPROD - 1:
                    even_bias(act, p + 1)
                if p < NPROD:
                    even_exp(act, p)
                if p in (24, 25):
                    act.wait_ge(head_hi, DIFF_HEADS)
                    act.wait_ge(masked, 2 * 5 * DIFF_HEADS)
                    for h in (2 * (p - 24), 2 * (p - 24) + 1):
                        nc.scalar.activation(diff_rt[:, h], diff_o[:, h], ACT.Square).then_inc(head_sq, 1)
                if p == 33:
                    act.wait_ge(head_var, DIFF_HEADS)
                    for h in range(DIFF_HEADS):
                        nc.scalar.activation(diff_rt[:, h], diff_rt[:, h], ACT.Exp, scale=-0.5).then_inc(head_root, 1)
                if 36 <= p < 36 + DIFF_HEADS:
                    act.wait_ge(head_t, p - 35)
                    nc.scalar.activation(x_hi[:, p - 36], diff_o[:, p - 36], ACT.Copy).then_inc(diff_hi_s, 1)

        def even_attention_dve(dve):
            dve.wait_ge(cum_turned, 1)
            nc.vector.tensor_copy(cum_tok[0:META, 0], flat[0:META, 3072:3080])
            nc.vector.tensor_copy(cum_tok[:, 1:5].rearrange("p j h -> p (j h)"), flat[:, 3080:3112]).then_inc(cum_kept, 1)
            dve.wait_ge(loaded, LOADS)
            lam_dve(dve)
            dve.wait_ge(cum_out, 16)
            dve.wait_ge(cum_kept, 1)
            for p in range(NPROD + 4):
                if 4 <= p:
                    even_head_lo(dve, p - 4)
                if p < NPROD:
                    even_mask(dve, p)
                if p < NPROD - 1:
                    bias_mask(dve, p + 1)
                if 1 <= p < NPROD + 1:
                    even_norm(dve, p - 1)
                h = p - 34
                if 0 <= h < DIFF_HEADS:
                    dve.wait_ge(head_root, h + 1)
                    nc.vector.scalar_tensor_tensor(diff_o[:, h], diff_o[:, h], small[:, 5:6], diff_rt[:, h], ALU.mult, ALU.mult).then_inc(head_t, 1)
                if 3 <= h < DIFF_HEADS + 3:
                    dve.wait_ge(diff_hi_s, h - 2)
                    nc.vector.tensor_tensor(x_lo[:, h - 3], diff_o[:, h - 3], x_hi[:, h - 3], ALU.subtract).then_inc(diff_lo_s, 1)

        def residual_dve(dve, name, wide, factor):
            def add(tile, done):
                dve.wait_ge(chunk_done, done)
                o = halves(x32[:, one(tile)].rearrange("p a n -> p (a n)"), wide)
                u = tile.plus(FIRST_TILE[name])
                nc.vector.scalar_tensor_tensor(o, o, factor, tile_out(u, wide), ALU.mult, ALU.add).then_inc(evicted[u.mod(2)], 1)
            side_stage(dve, split_lo, name, add)

        def only_split(eng, split, name):
            side_stage(eng, split, name, None)

        norms = {"all": 0, "layer": 0, "split": 0}
        norm_mean, norm_less, norm_squared, norm_var, norm_root, norm_scaled, norm_y, norm_hi, norm_lo = (
            sem(f"norm_{n}") for n in ("mean", "less", "squared", "var", "root", "scaled", "y", "hi", "lo"))
        mlp_squared, mlp_hi, mlp_lo = (sem(f"mlp_{n}") for n in ("squared", "hi", "lo"))

        def inverse_root(act, parts, out, done, eps=RMS_EPS):
            e = 12 if eps == LN_EPS else 13
            for o, i in parts:
                ins = nc.scalar.activation(o, i, ACT.Ln, bias=small[:, e:e + 1])
            act_chain.mark(ins)
            act_chain.settle(act)
            nc.scalar.activation(out, out, ACT.Exp, scale=-0.5).then_inc(done, 1)

        class Norm:

            def __init__(self, name, tile, wide, g, b=None, eps=LN_EPS, start=None, last=False):
                self.last = last
                split = norms["split"]
                norms["split"] += not last
                self.name, self.tile, self.wide, self.g, self.b, self.eps = name, tile, wide, g, b, eps
                self.c0 = 0 if wide else META
                placed["next"] = shared if start is None else start
                self.xc = at(name + "_xc", [P, KT, T])
                self.sq = at(name + "_sq", [P, KT, T])
                self.rt = at(name + "_rt", [P, T])
                self.n = norms["all"]
                self.nl = norms["layer"]
                norms["all"] += 1
                norms["layer"] += b is not None
                self.hi_before = KT * split
                self.ready = (norm_lo, KT * split)
                self.lo_at = KT * (split + 1)
                self.y = x32 if b is not None else self.xc

            def cols(self):
                return [(META, T, 0)] + ([(0, META, 512)] if self.wide else [])

            def add_mean(self, pe, k):
                if not k.stride and k.start < 0:
                    return
                u = k.plus(self.tile - KT)
                pe.wait_ge(evicted[u.mod(2)], u.over(2).at(plus=1))
                for a, b, o in self.cols():
                    last = nc.tensor.matmul(flat[:, 2048 + o:2048 + o + b - a], ones_d[:],
                                            x32[:, one(k), a:b].rearrange("p k n -> p (k n)"),
                                            start=not k.stride and k.start == 0, stop=not k.stride and k.start == KT - 1,
                                            skip_group_check=True)
                return last

            def pe(self, pe):
                if self.b is not None:
                    self.add_mean(pe, Step(KT - 1)).then_inc(norm_mean, 1)
                for k in range(KT):
                    pe.wait_ge(norm_squared, KT * self.n + k + 1)
                    for a, b, o in self.cols():
                        last = nc.tensor.matmul(flat[:, 3072 + o:3072 + o + b - a], ones_d[:], self.sq[:, k, a:b],
                                                start=k == 0, stop=k == KT - 1)
                last.then_inc(norm_var, 1)

            def dve(self, dve):
                xc = self.xc if self.b is not None else x32
                if self.b is not None:
                    dve.wait_ge(norm_mean, self.nl + 1)
                    for k in range(KT):
                        for a, b, o in self.cols():
                            last = nc.vector.tensor_tensor(xc[:, k, a:b], x32[:, k, a:b], flat[:, 2048 + o:2048 + o + b - a], ALU.subtract)
                        last.then_inc(norm_less, 1)
                dve.wait_ge(norm_root, self.n + 1)
                for k in range(KT + 2):
                    if k < KT:
                        o, i = self.xc[:, k, self.c0:T], xc[:, k, self.c0:T]
                        if self.b is not None:
                            ins = nc.vector.tensor_tensor(o, i, self.rt[:, self.c0:T], ALU.mult)
                        else:
                            ins = nc.vector.scalar_tensor_tensor(o, i, par[:, self.g + k:self.g + k + 1], self.rt[:, self.c0:T],
                                                                 ALU.mult, ALU.mult)
                        ins.then_inc(norm_scaled, 1)
                    if k >= 2 and not self.last:
                        j = k - 2
                        dve.wait_ge(norm_hi, self.hi_before + j + 1)
                        nc.vector.tensor_tensor(x_lo[:, j, self.c0:T], self.y[:, j, self.c0:T], x_hi[:, j, self.c0:T], ALU.subtract).then_inc(norm_lo, 1)

            def act(self, act, follow=None, squared=False):
                src = self.xc if self.b is not None else x32
                if self.b is None:
                    tiles_out(act, self.tile)
                    wait(act, norm_y, KT * self.nl)
                for k in range(0 if squared is False else KT, KT):
                    if self.b is not None:
                        act.wait_ge(norm_less, KT * self.nl + k + 1)
                    nc.scalar.activation(self.sq[:, k, self.c0:T], src[:, k, self.c0:T], ACT.Square).then_inc(norm_squared, 1)
                act.wait_ge(norm_var, self.n + 1)
                inverse_root(act, [(self.rt[:, a:b], flat[:, 3072 + o:3072 + o + b - a]) for a, b, o in self.cols()],
                             self.rt[:, self.c0:T], norm_root, self.eps)
                for k in range(KT):
                    act.wait_ge(norm_scaled, KT * self.n + k + 1)
                    o, i = self.y[:, k, self.c0:T], self.xc[:, k, self.c0:T]
                    if self.b is not None:
                        nc.scalar.activation(o, i, ACT.Identity, scale=par[:, self.g + k:self.g + k + 1],
                                             bias=par[:, self.b + k:self.b + k + 1]).then_inc(norm_y, 1)
                        act.wait_ge(norm_y, KT * self.nl + k + 1)
                    if follow:
                        nc.scalar.activation(follow.sq[:, k, follow.c0:T], o, ACT.Square).then_inc(norm_squared, 1)
                    if not self.last:
                        nc.scalar.activation(x_hi[:, k, self.c0:T], o, ACT.Copy).then_inc(norm_hi, 1)

        class Mlp:

            def __init__(self, layer, wide):
                self.layer, self.wide = layer, wide
                placed["next"] = shared
                self.h_hi = at(f"h_hi{layer}", [P, 16, T], F32R)
                self.h_lo = at(f"h_lo{layer}", [P, 16, T], F32R)
                self.pos = at(f"h_pos{layer}", [P, 2, T])
                self.sq = at(f"h_sq{layer}", [P, 2, T])

            def pe(self, pe, norm, next_norm):
                for half, hn in enumerate("ab"):
                    pe_stage(pe, f"up{self.layer}{hn}", x_hi, x_lo, self.wide, ready=None if half else norm.ready)
                    pe_stage(pe, f"down{self.layer}{hn}", self.h_hi, self.h_lo, self.wide,
                             ready=(mlp_lo, 32 * self.layer + 16 * half),
                             after=(lambda k: next_norm.add_mean(pe, k)) if half else None)

            def act(self, act):
                for half, hn in enumerate("ab"):
                    name = f"up{self.layer}{hn}"

                    def keep(tile, done):
                        u = tile.plus(FIRST_TILE[name])
                        act.wait_ge(chunk_done, done)
                        wait(act, mlp_squared, tile.at(plus=32 * self.layer + 16 * half - 1))
                        nc.scalar.activation(halves(self.pos[:, tile.mod(2)], self.wide), tile_out(u, self.wide), ACT.Relu) \
                            .then_inc(evicted[u.mod(2)], 1)
                        act.wait_ge(mlp_squared, tile.at(plus=32 * self.layer + 16 * half + 1))
                        nc.scalar.activation(halves(self.h_hi[:, one(tile)].rearrange("p a n -> p (a n)"), self.wide),
                                             halves(self.sq[:, tile.mod(2)], self.wide), ACT.Copy).then_inc(mlp_hi, 1)
                    side_stage(act, split_hi, name, keep, peel=int(self.layer == half == 0))
                    only_split(act, split_hi, f"down{self.layer}{hn}")

            def dve(self, dve):
                for half, hn in enumerate("ab"):
                    name = f"up{self.layer}{hn}"

                    def keep(tile, done):
                        u = tile.plus(FIRST_TILE[name])
                        dve.wait_ge(evicted[u.mod(2)], u.over(2).at(plus=1))
                        pos = halves(self.pos[:, tile.mod(2)], self.wide)
                        sq = halves(self.sq[:, tile.mod(2)], self.wide)
                        nc.vector.tensor_tensor(sq, pos, pos, ALU.mult).then_inc(mlp_squared, 1)
                        dve.wait_ge(mlp_hi, tile.at(plus=32 * self.layer + 16 * half + 1))
                        row = one(tile)
                        nc.vector.tensor_tensor(halves(self.h_lo[:, row].rearrange("p a n -> p (a n)"), self.wide), sq,
                                                halves(self.h_hi[:, row].rearrange("p a n -> p (a n)"), self.wide), ALU.subtract) \
                            .then_inc(mlp_lo, 1)
                    side_stage(dve, split_lo, name, keep)
                    residual_dve(dve, f"down{self.layer}{hn}", self.wide, ALPHA if half == 0 else 1.0)

        ln00 = Norm("ln00", FIRST_TILE["up0a"], True, PARAM["ln_g"], PARAM["ln_b"])
        mlp0 = Mlp(0, True)
        ln01 = Norm("ln01", FIRST_TILE["ret0"], True, PARAM["ln_g"] + 8, PARAM["ln_b"] + 8)

        placed["next"] = shared
        ret_hi = at("ret_hi", [P, 8, T], F32R)
        ret_lo = at("ret_lo", [P, 8, T], F32R)
        rq = at("rq", [P, 2, T])
        rk = at("rk", [P, 2, T])
        rv_slot = at("rv_slot", [P, 2, T])
        rv = at("rv", [P, 5, 512])
        decayed = at("decayed", [P, 5, SEQ])
        ro = at("ro", [P, 4, SEQ])
        rg = at("rg", [P, 4, SEQ])
        rsq = at("rsq", [P, 4, SEQ])
        decay = at("decay", [P, SEQ])
        decay_meta = at("decay_meta", [META, SEQ])
        ret_rt = at("ret_rt", [P, SEQ])
        (decay_in, rv_turned, rv_stored, ret_scored, ret_decayed, ret_weighed, ret_squared, ret_copied, ret_var,
         ret_root, ret_gated, ret_hi_s, ret_lo_s) = (
            sem(n) for n in ("decay_in", "rv_turned", "rv_stored", "ret_scored", "ret_decayed", "ret_weighed", "ret_squared",
                             "ret_copied", "ret_var", "ret_root", "ret_gated", "ret_hi_s", "ret_lo_s"))

        def ret_loads(pool):
            for h in range(RET_HEADS):
                if h == 0:
                    pool.wait_ge(norm_lo, ln01.lo_at)
                else:
                    pool.wait_ge(ret_decayed, 5 * h)
                a, b = TABLE["decay"] + h * SEQ, TABLE["decay_meta"] + h * SEQ
                pool.dma_start(decay[:], tables[:, a:a + SEQ]).then_inc(decay_in, 16)
                pool.dma_start(decay_meta[:], tables[0:META, b:b + SEQ]).then_inc(decay_in, 16)

        def ret_pe(pe, h):
            name = f"ret{h}"
            for c in range(12):
                chunk_products(pe, name, Step(c), x_hi, x_lo, 2 <= c < 8, ready=ln01.ready if h == c == 0 else None)
                if h and c == 0:
                    ret_squares_pe(pe, h - 1)
                if 5 <= c < 9:
                    t = c - 5
                    u = FIRST_TILE[name] + 4 + t
                    pe.wait_ge(evicted[u % 2], u // 2 + 1)
                    wait(pe, rv_stored, 4 * h + t)
                    if t == 0:
                        wait(pe, ret_decayed, 5 * h)
                        wait(pe, ret_root, h)
                    for b in range(5):
                        c0, n = q_rows(b)
                        o = 2048 + (512 if b == 0 else (b - 1) * P)
                        last = nc.tensor.transpose(flat[0:n, o:o + P], rv_slot[:, t % 2, c0:c0 + n], ident[:, :])
                    last.then_inc(rv_turned, 1)
            if h == 2:
                pe.wait_ge(ret_lo_s, 8)
                pe_stage(pe, "ret_out0", ret_hi, ret_lo, False)
            pe.wait_ge(rv_stored, 4 * h + 4)
            for i, b in enumerate((1, 2, 3, 4, 0)):
                c0, n = q_rows(b)
                w = SEQ if b == 0 else SEQ - (b - 1) * P
                if i >= 2:
                    pe.wait_ge(ret_decayed, 5 * h + i - 1)
                for k in range(2):
                    last = nc.tensor.matmul(flat[0:n, 2048 + (i % 2) * 512:2048 + (i % 2) * 512 + w], rk[:, k, c0:c0 + n],
                                            rq[:, k, T - w:T], start=k == 0, stop=k == 1)
                last.then_inc(ret_scored, 1)
            for e in range(4):
                n0 = 4 * h + e
                if e == 0:
                    pe.wait_ge(ret_decayed, 5 * h + 5)
                wait(pe, ret_copied, n0 - 1)
                o = (6 + e % 2) * 512
                for i, b in enumerate((1, 2, 3, 4, 0)):
                    n = q_rows(b)[1]
                    w = SEQ if b == 0 else SEQ - (b - 1) * P
                    last = nc.tensor.matmul(flat[:, o + SEQ - w:o + SEQ], rv[0:n, b, e * P:(e + 1) * P],
                                            decayed[0:n, b, SEQ - w:SEQ], start=i == 0, stop=i == 4)
                last.then_inc(ret_weighed, 1)

        def ret_squares_pe(pe, h):
            for e in range(4):
                pe.wait_ge(ret_squared, 4 * h + e + 1)
                last = nc.tensor.matmul(bank(4, SEQ), ones_g[:], rsq[:, e], start=e == 0, stop=e == 3)
            last.then_inc(ret_var, 1)

        def ret_act(act, h):
            name = f"ret{h}"
            for c in range(12):
                u = Step(FIRST_TILE[name] + c)
                split_hi(act, Step(FIRST_CHUNK[name] + c + AHEAD))
                if h and c < 3:
                    (ret_squares_act, ret_root_act, ret_hi_act)[c](act, h - 1)
                act.wait_ge(chunk_done, FIRST_CHUNK[name] + c + 1)
                wide = 2 <= c < 8
                src = tile_out(u, wide)
                if c < 2:
                    if c == 0:
                        wait(act, ret_scored, 5 * h)
                    nc.scalar.activation(halves(rq[:, c], wide), src, ACT.Copy).then_inc(evicted[u.mod(2)], 1)
                elif c < 4:
                    nc.scalar.activation(halves(rk[:, c - 2], wide), src, ACT.Copy, scale=1.0 / 16).then_inc(evicted[u.mod(2)], 1)
                elif c < 8:
                    wait(act, rv_turned, 4 * h + c - 4 - 1)
                    nc.scalar.activation(halves(rv_slot[:, c % 2], wide), src, ACT.Copy).then_inc(evicted[u.mod(2)], 1)
                else:
                    if c == 8:
                        wait(act, ret_gated, 4 * h)
                    nc.scalar.activation(rg[:, c - 8:c - 7], src, ACT.Silu).then_inc(evicted[u.mod(2)], 1)
            if h == 2:
                only_split(act, split_hi, "ret_out0")

        def ret_squares_act(act, h):
            for e in range(4):
                act.wait_ge(ret_copied, 4 * h + e + 1)
                if e == 0:
                    wait(act, ret_var, h)
                nc.scalar.activation(rsq[:, e], ro[:, e], ACT.Square).then_inc(ret_squared, 1)

        def ret_root_act(act, h):
            act.wait_ge(ret_var, h + 1)
            inverse_root(act, [(ret_rt[:], bank(4, SEQ))], ret_rt[:], ret_root)

        def ret_hi_act(act, h):
            for e in range(4):
                act.wait_ge(ret_gated, 4 * h + e + 1)
                if e == 0 and h == 2:
                    act.wait_ge(chunk_done, FIRST_CHUNK["ret_out0"] + 8)
                nc.scalar.activation(ret_hi[:, 4 * (h % 2) + e, META:T], ro[:, e], ACT.Copy).then_inc(ret_hi_s, 1)

        def ret_dve(dve, h):
            name = f"ret{h}"
            for c in range(12):
                split_lo(dve, Step(FIRST_CHUNK[name] + c + AHEAD))
                if h and c == 1:
                    ret_gate_dve(dve, h - 1)
                if h and c == 2:
                    ret_lo_dve(dve, h - 1)
                if 5 <= c < 9:
                    t = c - 5
                    dve.wait_ge(rv_turned, 4 * h + t + 1)
                    if t == 0:
                        wait(dve, ret_weighed, 4 * h)
                    nc.vector.tensor_copy(rv[:, 1:5, t * P:(t + 1) * P], bank(4, 512).rearrange("p (b n) -> p b n", b=4))
                    nc.vector.tensor_copy(rv[0:META, 0, t * P:(t + 1) * P], flat[0:META, 2560:2560 + P]).then_inc(rv_stored, 1)
            if h == 2:
                residual_dve(dve, "ret_out0", False, ALPHA)
            dve.wait_ge(decay_in, 32 * (h + 1))
            for i, b in enumerate((1, 2, 3, 4, 0)):
                n = q_rows(b)[1]
                w = SEQ if b == 0 else SEQ - (b - 1) * P
                dve.wait_ge(ret_scored, 5 * h + i + 1)
                d = decay_meta[:, 0:w] if b == 0 else decay[:, 0:w]
                o = 2048 + (i % 2) * 512
                nc.vector.tensor_tensor(decayed[0:n, b, SEQ - w:SEQ], flat[0:n, o:o + w], d, ALU.mult).then_inc(ret_decayed, 1)
            for e in range(4):
                dve.wait_ge(ret_weighed, 4 * h + e + 1)
                if e == 0:
                    wait(dve, ret_hi_s, 4 * h)
                    wait(dve, ret_lo_s, 4 * h)
                nc.vector.tensor_copy(ro[:, e], bank(6 + e % 2, SEQ)).then_inc(ret_copied, 1)

        def ret_gate_dve(dve, h):
            dve.wait_ge(ret_root, h + 1)
            for e in range(4):
                dve_chain.mark(nc.vector.tensor_tensor(ro[:, e], ro[:, e], ret_rt[:], ALU.mult))
            dve_chain.settle(dve)
            for e in range(4):
                nc.vector.tensor_tensor(ro[:, e], ro[:, e], rg[:, e], ALU.mult).then_inc(ret_gated, 1)

        def ret_lo_dve(dve, h):
            for e in range(4):
                dve.wait_ge(ret_hi_s, 4 * h + e + 1)
                nc.vector.tensor_tensor(ret_lo[:, 4 * (h % 2) + e, META:T], ro[:, e], ret_hi[:, 4 * (h % 2) + e, META:T],
                                        ALU.subtract).then_inc(ret_lo_s, 1)

        LAST_HEAD = RET_HEADS - 1

        def retention_pe(pe):
            for h in range(RET_HEADS):
                ret_pe(pe, h)
            ret_squares_pe(pe, LAST_HEAD)
            pe.wait_ge(ret_lo_s, 4 * RET_HEADS)
            pe_stage(pe, "ret_out1", ret_hi, ret_lo, False, after=lambda k: ln10.add_mean(pe, k))

        def retention_act(act):
            for h in range(RET_HEADS):
                ret_act(act, h)
            ret_squares_act(act, LAST_HEAD)
            ret_root_act(act, LAST_HEAD)
            ret_hi_act(act, LAST_HEAD)
            only_split(act, split_hi, "ret_out1")

        def retention_dve(dve):
            for h in range(RET_HEADS):
                ret_dve(dve, h)
            ret_gate_dve(dve, LAST_HEAD)
            ret_lo_dve(dve, LAST_HEAD)
            residual_dve(dve, "ret_out1", False, 1.0)

        ln10 = Norm("ln10", FIRST_TILE["up1a"], False, PARAM["ln_g"] + 16, PARAM["ln_b"] + 16)
        mlp1 = Mlp(1, False)
        ln11 = Norm("ln11", FIRST_TILE["latq"], False, PARAM["ln_g"] + 24, PARAM["ln_b"] + 24, last=True)

        rms_mix = Norm("rms_mix", FIRST_TILE["latq"], False, PARAM["norm_mix"], eps=RMS_EPS)
        placed["next"] = shared
        merged = at("merged", [P, KT, SEQ])
        after_merged = placed["next"]
        lq = nc.alloc_sbuf_tensor_at("lq", [P, KT, SEQ], F32, offset=shared)
        key_row = at("key_row", [P, SEQ])
        key_tok = at("key_tok", [P, QT, P])
        wuk = at("wuk", [P, 8, P])
        wuv = at("wuv", [P, 8, P])
        select = at("select", [P, 1280])
        att_hi = at("att_hi", [P, KT, T], F32R)
        att_lo = at("att_lo", [P, KT, T], F32R)
        kept = at("kept", [P, 2, SEQ])
        dsa_work = placed["next"]
        bias_near = at("bias_near", [P, 2, 2 * P])
        q_lat = at("q_lat", [P, 2, SEQ])
        d_buf = at("d_buf", [P, 4, SEQ])
        d_norm = at("d_norm", [P, 3, SEQ])
        d_turn = at("d_turn", [P, 2, SEQ])
        att_lat = at("att_lat", [P, 2, SEQ])
        d_stat = at("d_stat", [P, 3, 64])
        dsa_causal = at("dsa_causal", [P, P])
        gate_made = nc.alloc_sbuf_tensor_at("gate_made", [P, KT, SEQ], F32, offset=dsa_work - 4 * (2 * SEQ + KT * T))
        gate = nc.alloc_sbuf_tensor_at("gate", [P, KT, SEQ], F32, offset=dsa_work)
        key_raw = at("key_raw", [P, SEQ], start=dsa_work)
        key_sq = at("key_sq", [P, SEQ])
        key_rt = at("key_rt", [P, SEQ])
        iq = at("iq", [P, 4, SEQ])
        ik = at("ik", [P, SEQ])
        iw_row = at("iw_row", [IDX_HEADS, SEQ])
        iw = at("iw", [P, QT, IDX_HEADS])
        i_relu = at("i_relu", [P, 2, SEQ])
        top = at("top", [P, 3, 8])
        bucket = at("bucket", [32, 640])
        rel_sb = at("rel_sb", [32, ATT_HEADS])
        line_sb = at("line_sb", [ATT_HEADS, 640])

        (dsa_loaded, line_done, line_kept, line_out, key_squared, key_mean, key_root, key_ready,
         key_turned, key_kept, idx_turned, idx_kept, idx_scored, idx_relu, idx_added, selected) = (
            sem(n) for n in ("dsa_loaded", "line_done", "line_kept", "line_out", "key_squared", "key_mean",
                             "key_root", "key_ready", "key_turned", "key_kept", "idx_turned", "idx_kept", "idx_scored", "idx_relu",
                             "idx_added", "selected"))
        (ql_done, ql_kept, d_scored, d_biased, d_expd, d_normed, d_turned, d_kept, d_weighed, lat_kept, att_done, att_hi_s,
         att_lo_s, gate_done) = (
            sem(n) for n in ("ql_done", "ql_kept", "d_scored", "d_biased", "d_expd", "d_normed", "d_turned", "d_kept",
                             "d_weighed", "lat_kept", "att_done", "att_hi_s", "att_lo_s", "gate_done"))

        skew_out = sem("skew_out")
        near_in = [sem(f"near_in{n}") for n in range(2)]
        gate_out, gate_in, gate_dve_done = sem("gate_out"), sem("gate_in"), sem("gate_dve_done")
        kept_out = [sem(f"kept_out{n}") for n in range(2)]

        def sel_cols(i):
            a = P * i * (i + 1) // 2
            return slice(a, a + P * (i + 1))

        def dsa_loads(pool):
            pool.wait_ge(norm_lo, rms_mix.lo_at)
            for dst, src in ((bucket[:], tables[0:32, TABLE["bucket"]:TABLE["bucket"] + 640]), (rel_sb[:], rel),
                             (wuk[:], w_uk), (wuv[:].rearrange("p a n -> p (a n)"), w_uv),
                             (dsa_causal[:], tables[:, TABLE["causal"]:TABLE["causal"] + P])):
                pool.dma_start(dst, src).then_inc(dsa_loaded, 16)
            pool.wait_ge(line_kept, 1)
            pool.dma_start(line, line_sb[:]).then_inc(line_out, 16)
            pool.wait_ge(line_out, 16)
            for h in range(ATT_HEADS):
                src = bass.AP(tensor=line.tensor, offset=h * 640 + 256, ap=[[0, P], [1, 384]])
                dst = bass.AP(tensor=skewed.tensor, offset=h * SKEW + 256, ap=[[641, P], [1, 384]])
                pool.dma_start(dst, src).then_inc(skew_out, 16)
            pool.wait_ge(skew_out, 16 * ATT_HEADS)
            pool.wait_ge(selected, 1)
            for h in range(ATT_HEADS):
                if h >= 2:
                    pool.wait_ge(d_biased, 4 * (h - 1))
                src = bass.AP(tensor=skewed.tensor, offset=h * SKEW + 383, ap=[[640, P], [1, 2 * P]])
                pool.dma_start(bias_near[:, h % 2], src).then_inc(near_in[h % 2], 16)
            pool.wait_ge(att_lo_s, KT)
            pool.wait_ge(gate_out, 16)
            pool.dma_start(gate[:].rearrange("p k n -> p (k n)"), gate_dram).then_inc(gate_in, 16)

        def single(eng, split, name):
            split(eng, Step(FIRST_CHUNK[name] + AHEAD))

        def keep_tiles(act, name, dst, func=ACT.Copy, scale=1.0, rows=P, n=None):
            def keep(tile, done):
                act.wait_ge(chunk_done, done)
                u = tile.plus(FIRST_TILE[name])
                o = dst[0:rows, one(tile), 0:SEQ] if len(dst.shape) == 3 else dst[0:rows, :].rearrange("p (a n) -> p a n", a=1)
                nc.scalar.activation(o, tile_out(u, False)[0:rows], func, scale=scale).then_inc(evicted[u.mod(2)], 1)
            side_stage(act, split_hi, name, keep)

        def tile_kept(eng, name, n=1):
            tiles_out(eng, FIRST_TILE[name] + n)

        KEPT_CHUNK, KEPT_TILE = FIRST_CHUNK[KEPT[0][0]], FIRST_TILE[KEPT[0][0]]
        ND = ATT_HEADS * QT
        later = len(KEPT) - KEPT_EARLY
        fill_step = {(KEPT_EARLY + n, k): 1 + (8 * n + k) * (ND - 2) // (8 * later) for n in range(later) for k in range(KT)}

        def kept_pe(pe, n, k):
            ck, u = KEPT_CHUNK + n, KEPT_TILE + n
            if k == 0:
                pe.wait_ge(lo_ready, ck + 1)
                pe.wait_ge(evicted[u % 2], u // 2)
            for i, (w, a) in enumerate(((w_hi, x_hi), (w_hi, x_lo), (w_lo, x_hi))):
                last = nc.tensor.matmul(ps[:, 2 * (u % 2), 0:SEQ], w[:, ck % RING, k], a[:, k, META:T],
                                        start=k == 0 and i == 0, stop=k == KT - 1 and i == 2)
            if k == KT - 1:
                last.then_inc(chunk_done, 1)

        def kept_split(eng, n, split):
            split(eng, Step(KEPT_CHUNK + n + AHEAD))

        def kept_act(act, n):
            u = KEPT_TILE + n
            act.wait_ge(chunk_done, KEPT_CHUNK + n + 1)
            wait(act, kept_out[n % 2], 16 * (n // 2))
            nc.scalar.activation(kept[:, n % 2:n % 2 + 1], tile_out(Step(u), False), ACT.Copy).then_inc(evicted[u % 2], 1)
            act.wait_ge(evicted[u % 2], u // 2 + 1)
            act.dma_start(kept_dram[n], kept[:, n % 2]).then_inc(kept_out[n % 2], 16)

        def select_pe(pe):
            pe_stage(pe, "latq", x_hi, x_lo, False, ready=rms_mix.ready)
            pe_stage(pe, "latc", x_hi, x_lo, False)
            pe_stage(pe, "idxq", x_hi, x_lo, False)
            pe_stage(pe, "idxk", x_hi, x_lo, False)
            pe_stage(pe, "idxw", x_hi, x_lo, False)
            pe.wait_ge(dsa_loaded, 5 * 16)
            nc.tensor.matmul(flat[0:ATT_HEADS, 3072:3584], rel_sb[:], bucket[:, 0:512], start=True, stop=True)
            nc.tensor.matmul(flat[0:ATT_HEADS, 3584:3712], rel_sb[:], bucket[:, 512:640], start=True, stop=True).then_inc(line_done, 1)
            pe.wait_ge(key_squared, 1)
            nc.tensor.matmul(bank(4, SEQ), ones_h[:], key_sq[:], start=True, stop=True).then_inc(key_mean, 1)
            tiles_out(pe, FIRST_TILE["gate_att"])
            for j in range(QT):
                last = nc.tensor.transpose(flat[:, 1024 + 8 * j:1024 + 8 * j + 8], iw_row[:, j * P:(j + 1) * P], ident[0:8, 0:8])
            last.then_inc(idx_turned, 1)
            for n in range(3 * IDX_HEADS):
                i, h = 1 + n // IDX_HEADS, n % IDX_HEADS
                rows = slice(64 * (h % 2), 64 * (h % 2) + 64)
                if n < 2:
                    pe.wait_ge(idx_kept, 1)
                else:
                    pe.wait_ge(idx_relu, n - 1)
                nc.tensor.matmul(bank(2 + n % 2, P * (i + 1)), iq[rows, h // 2, i * P:(i + 1) * P], ik[rows, 0:P * (i + 1)],
                                 start=True, stop=True).then_inc(idx_scored, 1)
            pe.wait_ge(key_ready, 1)
            for j in range(QT):
                last = nc.tensor.transpose(flat[:, 2560 + j * P:2560 + (j + 1) * P], key_row[:, j * P:(j + 1) * P], ident[:])
            last.then_inc(key_turned, 1)
            pe.wait_ge(idx_relu, 3 * IDX_HEADS)
            for t in range(KT):
                chunk_products(pe, "gate_att", Step(t), x_hi, x_lo, False)
            for n in range(KEPT_EARLY):
                for k in range(KT):
                    kept_pe(pe, n, k)

        def select_act(act):
            keep_tiles(act, "latq", lq, scale=0.125)
            keep_tiles(act, "latc", key_raw)
            keep_tiles(act, "idxq", iq)
            keep_tiles(act, "idxk", ik)
            keep_tiles(act, "idxw", iw_row, rows=IDX_HEADS)
            tile_kept(act, "latc")
            nc.scalar.activation(key_sq[:], key_raw[:], ACT.Square).then_inc(key_squared, 1)
            act.wait_ge(line_done, 1)
            nc.scalar.activation(line_sb[:], flat[0:ATT_HEADS, 3072:3712], ACT.Copy).then_inc(line_kept, 1)
            act.wait_ge(key_mean, 1)
            inverse_root(act, [(key_rt[:], bank(4, SEQ))], key_rt[:], key_root)
            for n in range(3 * IDX_HEADS):
                i = 1 + n // IDX_HEADS
                act.wait_ge(idx_scored, n + 1)
                if n >= 2:
                    act.wait_ge(idx_added, n - 1)
                nc.scalar.activation(i_relu[:, n % 2, 0:P * (i + 1)], bank(2 + n % 2, P * (i + 1)), ACT.Relu).then_inc(idx_relu, 1)
            for t in range(KT):
                u = FIRST_TILE["gate_att"] + t
                split_hi(act, Step(FIRST_CHUNK["gate_att"] + t + AHEAD))
                act.wait_ge(chunk_done, FIRST_CHUNK["gate_att"] + t + 1)
                nc.scalar.activation(gate_made[:, t:t + 1], tile_out(Step(u), False), ACT.Sigmoid).then_inc(evicted[u % 2], 1)
            tiles_out(act, FIRST_TILE["gate_att"] + KT)
            act.dma_start(gate_dram, gate_made[:].rearrange("p k n -> p (k n)")).then_inc(gate_out, 16)
            for n in range(KEPT_EARLY):
                kept_split(act, n, split_hi)
                kept_act(act, n)

        def select_dve(dve):
            for name in ("latq", "latc", "idxq", "idxk", "idxw"):
                only_split(dve, split_lo, name)
            dve.wait_ge(key_root, 1)
            g = par[:, PARAM["kv_norm"]:PARAM["kv_norm"] + 1]
            nc.vector.scalar_tensor_tensor(key_row[:], key_raw[:], g, key_rt[:], ALU.mult, ALU.mult).then_inc(key_ready, 1)
            dve.wait_ge(idx_turned, 1)
            nc.vector.tensor_copy(iw[:].rearrange("p a n -> p (a n)"), flat[:, 1024:1056]).then_inc(idx_kept, 1)
            dve.wait_ge(idx_kept, 1)
            dve.wait_ge(dsa_loaded, 5 * 16)
            nc.vector.tensor_copy(select[:, 0:P], dsa_causal[:])
            for n in range(3 * IDX_HEADS):
                i, h = 1 + n // IDX_HEADS, n % IDX_HEADS
                w = iw[:, i, h:h + 1]
                s = select[:, sel_cols(i)]
                r = i_relu[:, n % 2, 0:P * (i + 1)]
                dve.wait_ge(idx_relu, n + 1)
                if h == 0:
                    nc.vector.tensor_scalar(s, r, w, None, ALU.mult).then_inc(idx_added, 1)
                else:
                    dve.wait_ge(idx_added, n)
                    nc.vector.scalar_tensor_tensor(s, r, w, s, ALU.mult, ALU.add).then_inc(idx_added, 1)
                if h == IDX_HEADS - 1:
                    dve.wait_ge(idx_added, n + 1)
                    d = select[:, sel_cols(i).stop - P:sel_cols(i).stop]
                    dve_chain.mark(nc.vector.tensor_tensor(d, d, dsa_causal[:], ALU.add))
            split_after = {1: 0, 2: 1, 4: 2, 5: 3, 7: 4, 8: 5, 9: 6, 11: 7, 12: 8, 13: 9, 14: 10}
            assert len(split_after) == KT + KEPT_EARLY
            for turn in range(16):
                dve_chain.settle(dve)
                for i in range(1, QT):
                    dve_chain.mark(nc.vector.max(top[:, i - 1], select[:, sel_cols(i)]))
                dve_chain.settle(dve)
                for i in range(1, QT):
                    s = select[:, sel_cols(i)]
                    dve_chain.mark(nc.vector.match_replace(s, top[:, i - 1], s, FILL))
                if turn in split_after:
                    split_lo(dve, Step(FIRST_CHUNK["gate_att"] + split_after[turn] + AHEAD))
            dve_chain.settle(dve)
            s = select[:, P:1280]
            dve_chain.mark(nc.vector.tensor_scalar(s, s, FILL, 1.0, ALU.is_equal, ALU.subtract))
            dve_chain.settle(dve)
            dve_chain.mark(nc.vector.tensor_scalar(s, s, -NEG, None, ALU.mult))
            dve_chain.settle(dve)
            dve.wait_ge(key_turned, 1)
            nc.vector.tensor_copy(key_tok[:].rearrange("p a n -> p (a n)"), bank(5, SEQ)).then_inc(selected, 1)

        def d_query(pe, h):
            rows = slice(64 * (h % 2), 64 * (h % 2) + 64)
            wait(pe, ql_kept, h)
            nc.tensor.matmul(bank(3, SEQ), wuk[rows, h // 2, :], lq[rows, h // 2, :], start=True, stop=True).then_inc(ql_done, 1)

        def d_scores(pe, p):
            h, i = divmod(p, QT)
            if i == 0:
                pe.wait_ge(ql_kept, h + 1)
            if p >= 2:
                pe.wait_ge(d_biased, p - 1)
            nc.tensor.matmul(bank(4 + p % 2, P * (i + 1)), q_lat[:, h % 2, i * P:(i + 1) * P], key_row[:, 0:P * (i + 1)],
                             start=True, stop=True).then_inc(d_scored, 1)

        def d_bias(dve, p):
            h, i = divmod(p, QT)
            w = P * (i + 1)
            near = min(w, 2 * P)
            s = d_buf[:, p % 4]
            dve.wait_ge(d_scored, p + 1)
            dve.wait_ge(near_in[h % 2], 16 * (h // 2 + 1))
            if p >= 4:
                dve.wait_ge(d_normed, p - 3)
            dve_chain.mark(nc.vector.tensor_tensor(s[:, w - near:w], bank(4 + p % 2, w)[:, w - near:w], bias_near[:, h % 2, 2 * P - near:2 * P], ALU.add))
            if w > near:
                far = par[:, PARAM["rel_far"] + h:PARAM["rel_far"] + h + 1]
                dve_chain.mark(nc.vector.tensor_scalar(s[:, 0:w - near], bank(4 + p % 2, w - near), far, None, ALU.add))
            dve_chain.settle(dve)
            nc.vector.tensor_tensor_reduce(s[:, 0:w], s[:, 0:w], select[:, sel_cols(i)], -1.0, FIRST_MIN, ALU.add, ALU.min,
                                           d_stat[:, 0, p:p + 1]).then_inc(d_biased, 1)

        def d_exp(act, p):
            w = P * (p % QT + 1)
            s = d_buf[:, p % 4, 0:w]
            act.wait_ge(d_biased, p + 1)
            nc.scalar.activation(s, s, ACT.Exp, scale=-1.0, bias=d_stat[:, 0, p:p + 1], accum_out=d_stat[:, 1, p:p + 1]).then_inc(d_expd, 1)

        def d_divide(dve, p):
            w = P * (p % QT + 1)
            dve.wait_ge(d_expd, p + 1)
            dve_chain.mark(nc.vector.reciprocal(d_stat[:, 2, p:p + 1], d_stat[:, 1, p:p + 1]))
            if p >= 3:
                dve.wait_ge(d_turned, p - 2)
            dve_chain.settle(dve)
            nc.vector.tensor_scalar(d_norm[:, p % 3, 0:w], d_buf[:, p % 4, 0:w], d_stat[:, 2, p:p + 1], None, ALU.mult).then_inc(d_normed, 1)

        def d_turn_pe(pe, p):
            pe.wait_ge(d_normed, p + 1)
            if p:
                pe.wait_ge(d_kept, p)
            for b in range(p % QT + 1):
                last = nc.tensor.transpose(flat[:, 3072 + b * P:3072 + (b + 1) * P], d_norm[:, p % 3, b * P:(b + 1) * P], ident[:])
            last.then_inc(d_turned, 1)

        def d_keep(act, p):
            w = P * (p % QT + 1)
            act.wait_ge(d_turned, p + 1)
            if p >= 2:
                act.wait_ge(d_weighed, p - 1)
            nc.scalar.activation(d_turn[:, p % 2, 0:w], bank(6, w), ACT.Copy).then_inc(d_kept, 1)

        def d_values(pe, p):
            h, i = divmod(p, QT)
            pe.wait_ge(d_kept, p + 1)
            if i == 0:
                wait(pe, lat_kept, h)
            for b in range(i + 1):
                last = nc.tensor.matmul(flat[:, 3584 + i * P:3584 + (i + 1) * P], key_tok[:, b, :], d_turn[:, p % 2, b * P:(b + 1) * P],
                                        start=b == 0, stop=b == i)
            last.then_inc(d_weighed, 1)

        def d_out(pe, h):
            rows = slice(64 * (h % 2), 64 * (h % 2) + 64)
            pe.wait_ge(lat_kept, h + 1)
            if h % 2 == 0:
                wait(pe, att_lo_s, h // 2)
            nc.tensor.matmul(bank(1, SEQ, rows), wuv[:, h // 2, 64 * (h % 2):64 * (h % 2) + 64], att_lat[:, h % 2],
                             start=True, stop=True).then_inc(att_done, 1)

        def sparse_pe(pe):
            pe.wait_ge(selected, 1)
            d_query(pe, 0)
            d_query(pe, 1)
            for s in range(ND + 5):
                if s < ND:
                    d_scores(pe, s)
                if s % QT == 2 and 2 <= s // QT + 2 < ATT_HEADS and s < ND:
                    d_query(pe, s // QT + 2)
                for (n, k), at_step in fill_step.items():
                    if at_step == s:
                        kept_pe(pe, n, k)
                if 3 <= s < ND + 3:
                    d_turn_pe(pe, s - 3)
                if 4 <= s < ND + 4:
                    d_values(pe, s - 4)
                if s >= 5 and (s - 5) % QT == QT - 1:
                    d_out(pe, (s - 5) // QT)

        def sparse_act(act):
            act.wait_ge(selected, 1)

            def query(h):
                act.wait_ge(ql_done, h + 1)
                if h >= 2:
                    act.wait_ge(d_scored, QT * (h - 1))
                nc.scalar.activation(q_lat[:, h % 2], bank(3, SEQ), ACT.Copy).then_inc(ql_kept, 1)
            query(0)
            query(1)
            for s in range(ND + 6):
                if s >= 5 and (s - 5) % QT == QT - 1 and s - 5 < ND:
                    h = (s - 5) // QT
                    act.wait_ge(d_weighed, QT * (h + 1))
                    if h >= 2:
                        act.wait_ge(att_done, h - 1)
                    nc.scalar.activation(att_lat[:, h % 2], bank(7, SEQ), ACT.Copy).then_inc(lat_kept, 1)
                if s >= 6 and (s - 6) % (2 * QT) == 2 * QT - 1:
                    k = (s - 6) // (2 * QT)
                    act.wait_ge(att_done, 2 * k + 2)
                    nc.scalar.activation(att_hi[:, k, META:T], bank(1, SEQ), ACT.Copy).then_inc(att_hi_s, 1)
                if 4 <= s < ND + 4:
                    d_keep(act, s - 4)
                if s < ND:
                    d_exp(act, s)
                if s % QT == 3 and s // QT + 2 < ATT_HEADS:
                    query(s // QT + 2)
                for n in range(KEPT_EARLY, len(KEPT)):
                    if fill_step[n, 0] + 1 == s:
                        kept_split(act, n, split_hi)
                    if fill_step[n, KT - 1] + 1 == s:
                        kept_act(act, n)

        def sparse_dve(dve):
            for s in range(ND + 7):
                if s >= 7 and (s - 7) % (2 * QT) == 2 * QT - 1:
                    k = (s - 7) // (2 * QT)
                    if k == 0:
                        dve.wait_ge(gate_out, 16)
                    dve.wait_ge(att_hi_s, k + 1)
                    nc.vector.tensor_tensor(att_lo[:, k, META:T], bank(1, SEQ), att_hi[:, k, META:T], ALU.subtract).then_inc(att_lo_s, 1)
                if s < ND:
                    d_bias(dve, s)
                if 1 <= s < ND + 1:
                    d_divide(dve, s - 1)
                for n in range(KEPT_EARLY, len(KEPT)):
                    if fill_step[n, 0] + 1 == s:
                        kept_split(dve, n, split_lo)

        def att_merge_pe(pe):
            pe_stage(pe, "att_out", att_hi, att_lo, False, ready=(att_lo_s, 0))

        def att_merge_dve(dve):
            def gated(tile, done):
                dve.wait_ge(chunk_done, done)
                if not tile.stride and tile.start == 0:
                    dve.wait_ge(gate_in, 16)
                    for n in range(2):
                        dve.wait_ge(kept_out[n], 16 * len(KEPT) // 2)
                u = tile.plus(FIRST_TILE["att_out"])
                nc.vector.tensor_tensor(merged[:, one(tile)], tile_out(u, False), gate[:, one(tile)], ALU.mult) \
                    .then_inc(evicted[u.mod(2)], 1)
            side_stage(dve, split_lo, "att_out", gated, peel=1)

        CH = QT
        placed["next"] = after_merged
        y_ssm = at("y_ssm", [P, KT, SEQ])
        u_hi = at("u_hi", [P, 4, T], F32R)
        u_lo = at("u_lo", [P, 4, T], F32R)
        ssm_work = placed["next"]
        xs, b_row, c_row = ([at(f"{n}0", shape)] for n, shape in (("xs", [P, 4, SEQ]), ("b_row", [P, SEQ]), ("c_row", [P, SEQ])))
        conv_in = at("conv_in", [P, 2, SEQ + 4])
        ssm_work2 = placed["next"]
        placed["next"] = shared
        for bufs, n, shape in ((xs, "xs1", [P, 4, SEQ]), (b_row, "b_row1", [P, SEQ]), (c_row, "c_row1", [P, SEQ])):
            bufs.append(at(n, shape))
        assert placed["next"] <= after_merged
        placed["next"] = ssm_work2
        z_buf = at("z_buf", [P, 4, SEQ])
        steps_abc = at("steps_abc", [P, 2, 8, P])
        seg_start = placed["next"] = (placed["next"] + 31) // 32 * 32
        seg = at("seg", [P, 8, P])
        c_dec = at("c_dec", [P, 8, P])
        x_dt = at("x_dt", [P, 2, SEQ])
        x_dec = at("x_dec", [P, SEQ])
        b_tok = at("b_tok", [P, P])
        cb = at("cb", [P, P])
        tri = at("tri", [P, P])
        state = at("state", [P, SEQ])
        dec_end = at("dec_end", [P, 2, 8])
        dt_tok = at("dt_tok", [P, CH, 32])
        acum_tok = at("acum_tok", [P, CH, 32])
        a_col = at("a_col", [32, 1])
        g_rt = z_buf[:, 0]
        gates = nc.alloc_sbuf_tensor_at("gates", [P, KT, SEQ], F32, offset=ssm_work)
        dt_row = nc.alloc_sbuf_tensor_at("dt_row", [32, 4, SEQ], F32, offset=ssm_work2)
        dt_one = nc.alloc_sbuf_tensor_at("dt_one", [32, P], F32, offset=seg_start)
        acum_row = nc.alloc_sbuf_tensor_at("acum_row", [32, SEQ], F32, offset=seg_start + P * 4)

        (dt_a, dt_b, acum_ready, acum_out, ssm_loaded, dt_turned, dt_kept, conv_done, conv_silu, ssm_turned, seg_args, dec_args,
         seg_exp, dec_exp, abc_exp, y_ready, end_ready, y_done, state_done, abc_used, z_ready, u_done, u_sq, ssm_var, ssm_root,
         u_norm, u_hi_s, u_lo_s, zeroed, m_sum, m_hi_s, m_lo_s) = (
            sem(n) for n in ("dt_a", "dt_b", "acum_ready", "acum_out", "ssm_loaded", "dt_turned", "dt_kept", "conv_done", "conv_silu",
                             "ssm_turned", "seg_args", "dec_args", "seg_exp", "dec_exp", "abc_exp", "y_ready", "end_ready", "y_done",
                             "state_done", "abc_used", "z_ready", "u_done", "u_sq", "ssm_var", "ssm_root", "u_norm",
                             "u_hi_s", "u_lo_s", "zeroed", "m_sum", "m_hi_s", "m_lo_s"))
        abc_in = [sem(f"abc_in{n}") for n in range(2)]

        def kept_back(pool, dst, n, done):
            pool.dma_start(dst[:, 0:4], kept_dram[n:n + 4].rearrange("t p n -> p t n")).then_inc(done, 16)

        def ssm_loads(pool):
            tiles_out(pool, FIRST_TILE["dt"])
            nc.gpsimd.memset(conv_in[:, :, 0:3], 0.0).then_inc(zeroed, 1)
            nc.gpsimd.memset(dt_one[:], 1.0).then_inc(zeroed, 1)
            pool.dma_start(tri[:], tables[:, TABLE["tri"]:TABLE["tri"] + P]).then_inc(ssm_loaded, 16)
            pool.dma_start(merged_dram, merged[:].rearrange("p k n -> p (k n)")).then_inc(merged_out, 16)
            pool.wait_ge(acum_ready, 1)
            pool.dma_start(acum_dram, acum_row[:]).then_inc(acum_out, 16)
            pool.wait_ge(acum_out, 16)
            for n in range(SSM_GROUPS * CH):
                g, c = divmod(n, CH)
                if n >= 2:
                    pool.wait_ge(abc_used, n - 1)
                src = bass.AP(tensor=acum_dram.tensor, offset=8 * g * SEQ + c * P, ap=[[0, P], [SEQ, 8], [1, P]])
                pool.dma_start(steps_abc[:, n % 2], src).then_inc(abc_in[n % 2], 16)
                if c == 2 and g in (1, 2):
                    pool.wait_ge(u_norm, 4 * g)
                    kept_back(pool, z_buf, 4 * (g - 1), z_in)
                if c == 2 and g == SSM_GROUPS - 1:
                    pool.wait_ge(u_lo_s, 4 * g)
                    kept_back(pool, gates, 8, gates_in)
            pool.wait_ge(merged_out, 16)
            pool.wait_ge(u_hi_s, 4 * SSM_GROUPS)
            pool.wait_ge(u_lo_s, 4 * SSM_GROUPS)
            pool.dma_start(merged[:].rearrange("p k n -> p (k n)"), merged_dram).then_inc(merged_in, 16)

        def dt_pe(pe):
            chunk_products(pe, "dt", Step(0), x_hi, x_lo, False)

        def dt_turn_pe(pe):
            pe.wait_ge(acum_ready, 1)
            for src, o in ((dt_row[:, 3], 2048), (acum_row[:], 2176)):
                for c in range(CH):
                    last = nc.tensor.transpose(flat[:, o + 32 * c:o + 32 * c + 32], src[:, c * P:(c + 1) * P], ident[0:32, 0:32])
            last.then_inc(dt_turned, 1)

        def dt_act(act):
            u = Step(FIRST_TILE["dt"])
            split_hi(act, Step(FIRST_CHUNK["dt"] + AHEAD))
            act.wait_ge(chunk_done, FIRST_CHUNK["dt"] + 1)
            tiles_out(act, FIRST_TILE["dt"])
            act_chain.mark(nc.scalar.activation(dt_row[:, 0:1], tile_out(u, False)[0:32], ACT.Identity,
                                                bias=par[0:32, PARAM["dt_bias"]:PARAM["dt_bias"] + 1]))
            act_chain.settle(act)
            nc.scalar.activation(dt_row[:, 1], dt_row[:, 0], ACT.Abs).then_inc(evicted[u.mod(2)], 1)
            act.wait_ge(evicted[u.mod(2)], u.start // 2 + 1)
            act_chain.mark(nc.scalar.activation(dt_row[:, 1], dt_row[:, 1], ACT.Exp, scale=-1.0))
            nc.scalar.activation(a_col[:], par[0:32, PARAM["a_log"]:PARAM["a_log"] + 1], ACT.Exp).then_inc(dt_a, 1)
            act_chain.settle(act)
            nc.scalar.activation(dt_row[:, 2], dt_row[:, 1], ACT.Ln, bias=1.0).then_inc(dt_a, 1)

        def dt_dve(dve):
            split_lo(dve, Step(FIRST_CHUNK["dt"] + AHEAD))
            dve.wait_ge(dt_a, 2)
            dve_chain.mark(nc.vector.tensor_scalar(dt_row[:, 3], dt_row[:, 0], 0.0, None, ALU.max))
            dve_chain.settle(dve)
            dve_chain.mark(nc.vector.tensor_tensor(dt_row[:, 3], dt_row[:, 3], dt_row[:, 2], ALU.add))
            dve_chain.settle(dve)
            dve_chain.mark(nc.vector.tensor_scalar(dt_row[:, 1], dt_row[:, 3], a_col[:], -1.0, ALU.mult, ALU.mult))
            dve_chain.settle(dve)
            dve.wait_ge(zeroed, 2)
            for c in range(CH):
                cols = slice(c * P, (c + 1) * P)
                ins = nc.vector.tensor_tensor_scan(acum_row[:, cols], dt_one[:], dt_row[:, 1, cols], 0.0, ALU.mult, ALU.add)
            ins.then_inc(acum_ready, 1)

        def dt_turned_dve(dve):
            dve.wait_ge(dt_turned, 1)
            nc.vector.tensor_copy(dt_tok[:].rearrange("p c h -> p (c h)"), flat[:, 2048:2176])
            nc.vector.tensor_copy(acum_tok[:].rearrange("p c h -> p (c h)"), flat[:, 2176:2304]).then_inc(dt_kept, 1)
            dve.wait_ge(dt_kept, 1)
            dve.wait_ge(ssm_loaded, 16)
            dve.wait_ge(acum_out, 16)

        def ssm_turn(pe, g, c):
            n = CH * g + c
            cols = slice(c * P, (c + 1) * P)
            if n:
                pe.wait_ge(y_ready, n)
            for t in range(4):
                nc.tensor.transpose(flat[:, 2048 + t * P:2048 + (t + 1) * P], xs[g % 2][:, t, cols], ident[:])
            nc.tensor.transpose(flat[:, 2560:2560 + P], b_row[g % 2][:, cols], ident[:])
            nc.tensor.matmul(flat[:, 2688:2688 + P], b_row[g % 2][:, cols], c_row[g % 2][:, cols], start=True, stop=True) \
                .then_inc(ssm_turned, 1)

        def ssm_outputs(pe, g, c):
            n = CH * g + c
            pe.wait_ge(y_ready, n + 1)
            if n:
                pe.wait_ge(y_done, n)
            for h in range(HEADS_PER_GROUP):
                rows = slice(64 * (h % 2), 64 * (h % 2) + 64)
                o = flat[rows, 3072 + (h // 2) * P:3072 + (h // 2 + 1) * P]
                last = nc.tensor.matmul(o, x_dt[:, n % 2, 64 * h:64 * h + 64], seg[:, h], start=True, stop=c == 0)
                if c:
                    last = nc.tensor.matmul(o, state[:, 64 * h:64 * h + 64], c_dec[:, h], start=False, stop=True)
            if c == CH - 1:
                last.then_inc(end_ready, 1)
            else:
                nc.tensor.matmul(bank(7, SEQ), b_tok[:], x_dec[:], start=True, stop=True).then_inc(end_ready, 1)

        def group_items(g):
            xs_next, so_last, z_own = ([(kind, h, t) for t in range(n)] for kind, h, n in (("xs", g + 1, 6), ("so", g - 1, 4), ("z", g, 4)))
            gate = [("gate", g, t) for t in range(4)]
            if g == SSM_GROUPS:
                return [gate[1:4]]
            if g == SSM_GROUPS - 1:
                return [z_own[0:2], z_own[2:4] + so_last[0:1], so_last[1:3], so_last[3:4] + gate[0:1]]
            if g == 0:
                return [xs_next[2:4], xs_next[4:6], z_own[0:2], z_own[2:4]]
            return [xs_next[0:3], xs_next[3:5], xs_next[5:6] + so_last[0:2], so_last[2:4]]

        def item_at(item):
            kind, g, t = item
            name = "gate_ssm_b" if kind == "gate" else f"{kind}{g}"
            return name, FIRST_CHUNK[name] + t, FIRST_TILE[name] + (2 * t if kind == "so" else t)

        def so_pe(pe, g, k):
            ck = FIRST_CHUNK[f"so{g}"] + k
            pe.wait_ge(lo_ready, ck + 1)
            pe.wait_ge(u_lo_s, 4 * g + 4)
            for m in range(2):
                u = FIRST_TILE[f"so{g}"] + 2 * k + m
                pe.wait_ge(evicted[u % 2], u // 2 - (1 if k else 0))
                for f in range(4):
                    for w, (a, b) in enumerate(((w_hi, u_hi), (w_hi, u_lo), (w_lo, u_hi))):
                        last = nc.tensor.matmul(ps[:, 2 * (u % 2) + k % 2, 0:SEQ], a[:, ck % RING, 2 * f + m], b[:, f, META:T],
                                                start=f == 0 and w == 0, stop=f == 3 and w == 2)
            last.then_inc(chunk_done, 1)

        def item_pe(pe, item):
            if item[0] == "so":
                so_pe(pe, item[1], item[2])
            else:
                chunk_products(pe, item_at(item)[0], Step(item[2]), x_hi, x_lo, False)

        def squares_pe(pe, g):
            for t in range(4):
                pe.wait_ge(u_sq, 4 * g + t + 1)
                last = nc.tensor.matmul(bank(1, SEQ), ones_g[:], z_buf[:, t], start=t == 0, stop=t == 3)
            last.then_inc(ssm_var, 1)

        def ssm_pe(pe, g):
            if g < SSM_GROUPS:
                pe.wait_ge(conv_silu, 3 * g + 3)
            for c, items in enumerate(group_items(g)):
                if g < SSM_GROUPS:
                    ssm_turn(pe, g, c)
                for i, item in enumerate(items):
                    item_pe(pe, item)
                    if g and c == 0 and i == 0:
                        squares_pe(pe, g - 1)
                if g < SSM_GROUPS:
                    ssm_outputs(pe, g, c)

        FIRST_ITEMS = [("xs", 0, t) for t in range(6)] + [("xs", 1, t) for t in range(2)]

        def first_inputs_pe(pe):
            for i, item in enumerate(FIRST_ITEMS):
                item_pe(pe, item)
                if i == 1:
                    dt_turn_pe(pe)

        def item_split(eng, item, split):
            split(eng, Step(item_at(item)[1] + AHEAD))

        def item_act(act, item):
            kind, g, t = item
            name, chunk, u = item_at(item)
            if kind == "so":
                return
            act.wait_ge(chunk_done, chunk + 1)
            out = tile_out(Step(u), False)
            if kind == "xs":
                wait(act, conv_done, 6 * g + t - 1)
                nc.scalar.activation(conv_in[:, t % 2:t % 2 + 1, 3:3 + SEQ], out, ACT.Copy).then_inc(evicted[u % 2], 1)
            elif kind == "gate":
                nc.scalar.activation(gates[:, t + 4:t + 5], out, ACT.Sigmoid).then_inc(evicted[u % 2], 1)
            else:
                nc.scalar.activation(z_buf[:, t:t + 1], out, ACT.Copy).then_inc(evicted[u % 2], 1)
                if t == 3:
                    tiles_out(act, u + 1)
                    nc.scalar.activation(z_buf[:], z_buf[:], ACT.Silu).then_inc(z_ready, 1)

        def inputs_silu(act, g):
            act.wait_ge(conv_done, 6 * g + 6)
            for buf in (xs, b_row, c_row):
                nc.scalar.activation(buf[g % 2][:], buf[g % 2][:], ACT.Silu).then_inc(conv_silu, 1)

        def first_inputs_act(act):
            act.wait_ge(zeroed, 2)
            for item in FIRST_ITEMS[0:6]:
                item_split(act, item, split_hi)
                item_act(act, item)
            for item in FIRST_ITEMS[6:8]:
                item_split(act, item, split_hi)
            inputs_silu(act, 0)
            for item in FIRST_ITEMS[6:8]:
                item_act(act, item)

        def ssm_act(act, g):
            inputs_here = False
            if g:
                for t in range(4):
                    act.wait_ge(u_done, 4 * (g - 1) + t + 1)
                    nc.scalar.activation(z_buf[:, t], xs[(g - 1) % 2][:, t], ACT.Square).then_inc(u_sq, 1)
            for c, items in enumerate(group_items(g)):
                n = CH * g + c
                if g < SSM_GROUPS:
                    act.wait_ge(dec_args, n + 1)
                    nc.scalar.activation(dec_end[:, n % 2], dec_end[:, n % 2], ACT.Exp).then_inc(dec_exp, 1)
                    act.wait_ge(seg_args, n + 1)
                    nc.scalar.activation(seg[:], seg[:], ACT.Exp).then_inc(seg_exp, 1)
                    nc.scalar.activation(steps_abc[:, n % 2], steps_abc[:, n % 2], ACT.Exp).then_inc(abc_exp, 1)
                if inputs_here:
                    inputs_silu(act, g + 1)
                for i, item in enumerate(items):
                    item_split(act, item, split_hi)
                    if g and c == 0 and i == 0:
                        finish_root_act(act, g - 1)
                    if g and c == 0 and i == (0 if item[0] == "z" else 1):
                        finish_hi_act(act, g - 1)
                    item_act(act, item)
                inputs_here = ("xs", g + 1, 5) in items
            if g in (1, 2):
                act.wait_ge(z_in, 16 * g)
                nc.scalar.activation(z_buf[:], z_buf[:], ACT.Silu).then_inc(z_ready, 1)
            if g == SSM_GROUPS:
                act.wait_ge(gates_in, 16)
                nc.scalar.activation(gates[:, 0:4], gates[:, 0:4], ACT.Sigmoid).then_inc(gates_ready, 1)

        def finish_root_act(act, g):
            act.wait_ge(ssm_var, g + 1)
            inverse_root(act, [(g_rt, bank(1, SEQ))], g_rt, ssm_root)

        def finish_hi_act(act, g):
            for t in range(4):
                act.wait_ge(u_norm, 4 * g + t + 1)
                nc.scalar.activation(u_hi[:, t, META:T], xs[g % 2][:, t], ACT.Copy).then_inc(u_hi_s, 1)

        def convolve(dve, dst, taps, col, src, bias, done):
            for j in reversed(range(taps)):
                w = par[:, col(j)]
                x = src[:, j:j + SEQ]
                if j == taps - 1:
                    dve_chain.mark(nc.vector.tensor_scalar(dst, x, w, par[:, bias], ALU.mult, ALU.add))
                else:
                    dve_chain.settle(dve)
                    ins = nc.vector.scalar_tensor_tensor(dst, x, w, dst, ALU.mult, ALU.add)
                    if j:
                        dve_chain.mark(ins)
            ins.then_inc(done, 1)

        def item_dve(dve, item):
            kind, g, t = item
            name, chunk, u = item_at(item)
            if kind == "xs":
                dve.wait_ge(evicted[u % 2], u // 2 + 1)
                if g == 1 and t == 0:
                    dve.wait_ge(merged_out, 16)
                if g >= 2 and t == 0:
                    dve.wait_ge(u_lo_s, 4 * (g - 1))
                k = 4 * g + t if t < 4 else (16 + g if t == 4 else 20 + g)
                dst = xs[g % 2][:, t] if t < 4 else (b_row[g % 2][:] if t == 4 else c_row[g % 2][:])
                c0, b0 = PARAM["conv_ssm_w"], PARAM["conv_ssm_b"] + k
                convolve(dve, dst, 4, lambda j: slice(c0 + 24 * j + k, c0 + 24 * j + k + 1), conv_in[:, t % 2], slice(b0, b0 + 1), conv_done)
            elif kind == "so":
                dve.wait_ge(chunk_done, chunk + 1)
                for m in range(2):
                    src = ps[:, 2 * ((u + m) % 2) + t % 2, 0:SEQ]
                    y = y_ssm[:, 2 * t + m]
                    ins = nc.vector.tensor_copy(y, src) if g == 0 else nc.vector.tensor_tensor(y, y, src, ALU.add)
                    ins.then_inc(evicted[(u + m) % 2], 1)

        def first_inputs_dve(dve):
            for i, item in enumerate(FIRST_ITEMS):
                item_split(dve, item, split_lo)
                if i < 6:
                    item_dve(dve, item)
                else:
                    waiting.append(item)
                if i == 1:
                    dt_turned_dve(dve)

        def chunk_ready(dve, g, c):
            heads = slice(8 * g, 8 * g + 8)
            n = CH * g + c
            cols = slice(c * P, (c + 1) * P)
            abc = steps_abc[:, n % 2]
            dve.wait_ge(abc_in[n % 2], 16 * (n // 2 + 1))
            if n >= 1:
                dve.wait_ge(x_end_used, n)
            nc.vector.tensor_tensor(dec_end[:, n % 2].unsqueeze(2), abc[:, :, P - 1:P], acum_tok[:, c, heads].unsqueeze(2), ALU.subtract) \
                .then_inc(dec_args, 1)
            wait(dve, end_ready, n)
            for h in range(8):
                ins = nc.vector.tensor_scalar(seg[:, h], abc[:, h], acum_tok[:, c, 8 * g + h:8 * g + h + 1], 0.0, ALU.subtract, ALU.min)
            ins.then_inc(seg_args, 1)
            dve.wait_ge(ssm_turned, n + 1)
            x3 = x_dt[:, n % 2].rearrange("p (h d) -> p h d", h=8)
            dt3 = dt_tok[:, c, heads].unsqueeze(2).broadcast_to([P, 8, 64])
            dve_chain.mark(nc.vector.tensor_tensor(x3, bank(4, SEQ).rearrange("p (h d) -> p h d", h=8), dt3, ALU.mult))
            nc.vector.tensor_copy(b_tok[:], flat[:, 2560:2560 + P])
            dve_chain.mark(nc.vector.tensor_tensor(cb[:], flat[:, 2688:2688 + P], tri[:], ALU.mult))
            dve.wait_ge(dec_exp, n + 1)
            dve_chain.settle(dve)
            nc.vector.tensor_tensor(x_dec[:].rearrange("p (h d) -> p h d", h=8), x3,
                                    dec_end[:, n % 2].unsqueeze(2).broadcast_to([P, 8, 64]), ALU.mult).then_inc(x_end_used, 1)
            dve.wait_ge(seg_exp, n + 1)
            nc.vector.tensor_tensor(seg[:], seg[:], cb[:].unsqueeze(1).broadcast_to([P, 8, P]), ALU.mult)
            dve.wait_ge(abc_exp, n + 1)
            nc.vector.tensor_tensor(c_dec[:], abc, c_row[g % 2][:, cols].unsqueeze(1).broadcast_to([P, 8, P]), ALU.mult).then_inc(y_ready, 1)

        def chunk_end(dve, g, c):
            n = CH * g + c
            cols = slice(c * P, (c + 1) * P)
            dve.wait_ge(end_ready, n + 1)
            if c < CH - 1:
                s3 = state[:].rearrange("p (h d) -> p h d", h=8)
                if c == 0:
                    ins = nc.vector.tensor_copy(state[:], bank(7, SEQ))
                else:
                    dve_chain.mark(nc.vector.tensor_tensor(s3, s3, steps_abc[:, n % 2, :, P - 1:P].broadcast_to([P, 8, 64]), ALU.mult))
                    dve_chain.settle(dve)
                    ins = nc.vector.tensor_tensor(state[:], state[:], bank(7, SEQ), ALU.add)
                dve_chain.mark(ins)
            x = xs[g % 2]
            for t in range(4):
                d = PARAM["d_skip"] + 4 * g + t
                ins = nc.vector.scalar_tensor_tensor(x[:, t, cols], x[:, t, cols], par[:, d:d + 1],
                                                     flat[:, 3072 + t * P:3072 + (t + 1) * P], ALU.mult, ALU.add)
            ins.then_inc(y_done, 1)
            dve_chain.settle(dve)
            nc.vector.tensor_copy(small[:, 16:17], small[:, 4:5]).then_inc(abc_used, 1)

        def finish_norm_dve(dve, g):
            x = xs[g % 2]
            dve.wait_ge(ssm_root, g + 1)
            for t in range(4):
                k = PARAM["ssm_norm"] + 4 * g + t
                nc.vector.scalar_tensor_tensor(x[:, t], x[:, t], par[:, k:k + 1], g_rt, ALU.mult, ALU.mult).then_inc(u_norm, 1)

        def finish_lo_dve(dve, g):
            x = xs[g % 2]
            for t in range(4):
                dve.wait_ge(u_hi_s, 4 * g + t + 1)
                nc.vector.tensor_tensor(u_lo[:, t, META:T], x[:, t], u_hi[:, t, META:T], ALU.subtract).then_inc(u_lo_s, 1)

        waiting = []

        def ssm_dve(dve, g):
            for c, items in enumerate(group_items(g)):
                if g < SSM_GROUPS:
                    chunk_ready(dve, g, c)
                for item in waiting:
                    item_dve(dve, item)
                waiting.clear()
                for i, item in enumerate(items):
                    item_split(dve, item, split_lo)
                    if g and c == 0 and i == 0:
                        finish_norm_dve(dve, g - 1)
                    if g and c == 0 and i == (0 if item[0] == "z" else 1):
                        finish_lo_dve(dve, g - 1)
                        item_dve(dve, items[0])
                    if not (g and c == 0 and i == 0):
                        if item[0] == "xs" and i == len(items) - 1:
                            waiting.append(item)
                        else:
                            item_dve(dve, item)
                if g < SSM_GROUPS:
                    chunk_end(dve, g, c)
            if g < SSM_GROUPS:
                dve.wait_ge(y_done, CH * g + CH)
                dve.wait_ge(z_ready, g + 1)
                for t in range(4):
                    nc.vector.tensor_tensor(xs[g % 2][:, t], xs[g % 2][:, t], z_buf[:, t], ALU.mult).then_inc(u_done, 1)

        x_end_used, merged_out, merged_in, z_in, gates_in, gates_ready = (
            sem(n) for n in ("x_end_used", "merged_out", "merged_in", "z_in", "gates_in", "gates_ready"))

        m_hi = nc.alloc_sbuf_tensor_at("m_hi", [P, KT, T], F32R, offset=ssm_work2)
        m_lo = nc.alloc_sbuf_tensor_at("m_lo", [P, KT, T], F32R, offset=ssm_work2 + KT * T * 4)
        assert ssm_work2 + 2 * KT * T * 4 <= nc.sbuf_usable_end
        LAST = SSM_GROUPS - 1

        def mix_pe(pe):
            for k in range(4):
                so_pe(pe, LAST, k)
            pe_stage(pe, "mix_out", m_hi, m_lo, False, ready=(m_lo_s, 0))

        def mix_act(act):
            act.wait_ge(u_norm, 4 * SSM_GROUPS)
            for k in range(4):
                split_hi(act, Step(FIRST_CHUNK[f"so{LAST}"] + k + AHEAD))
                for f in (2 * k, 2 * k + 1):
                    act.wait_ge(m_sum, f + 1)
                    nc.scalar.activation(m_hi[:, f:f + 1, META:T], merged[:, f:f + 1], ACT.Copy).then_inc(m_hi_s, 1)
            only_split(act, split_hi, "mix_out")

        def mix_dve(dve):
            for k in range(4):
                item_split(dve, ("so", LAST, k), split_lo)
                item_dve(dve, ("so", LAST, k))
                u = FIRST_TILE[f"so{LAST}"] + 2 * k
                tiles_out(dve, u + 2)
                if k == 0:
                    dve.wait_ge(merged_in, 16)
                    dve.wait_ge(gates_ready, 1)
                for f in (2 * k, 2 * k + 1):
                    dve_chain.mark(nc.vector.tensor_tensor(gates[:, f], gates[:, f], y_ssm[:, f], ALU.mult))
                dve_chain.settle(dve)
                for f in (2 * k, 2 * k + 1):
                    nc.vector.tensor_tensor(merged[:, f], merged[:, f], gates[:, f], ALU.add).then_inc(m_sum, 1)
                for f in (2 * k, 2 * k + 1):
                    dve.wait_ge(m_hi_s, f + 1)
                    nc.vector.tensor_tensor(m_lo[:, f, META:T], merged[:, f], m_hi[:, f, META:T], ALU.subtract).then_inc(m_lo_s, 1)
            residual_dve(dve, "mix_out", False, 1.0)

        rms_ffn = Norm("rms_ffn", FIRST_TILE["gv0"], False, PARAM["norm_ffn"], eps=RMS_EPS)
        placed["next"] = shared
        f_hi = at("f_hi", [P, 8, T], F32R)
        f_lo = at("f_lo", [P, 8, T], F32R)
        f_in = at("f_in", [P, 4, SEQ + 4])
        f_conv = at("f_conv", [P, 4, SEQ])
        f_zero, f_conved, f_silu, f_prod, f_hi_s, f_lo_s = (sem(n) for n in ("f_zero", "f_conved", "f_silu", "f_prod", "f_hi_s", "f_lo_s"))
        GROUPS = (8, 8, 6)

        def ffn_pool(pool):
            pool.wait_ge(norm_lo, rms_ffn.lo_at)
            nc.gpsimd.memset(f_in[:, :, 0:2], 0.0).then_inc(f_zero, 1)

        def ffn_pe(pe):
            done = 0
            for g, n in enumerate(GROUPS):
                pe_stage(pe, f"gv{g}", x_hi, x_lo, False, ready=None if g else rms_ffn.ready)
                loop(pe, 8, 4, lambda t: chunk_products(pe, f"fd{g}", t, f_hi, f_lo, False, nk=n,
                                                        ready=(f_lo_s, done) if not t.stride and t.start == 0 else None), peel=1)
                done += n

        def ffn_act(act):
            act.wait_ge(f_zero, 1)
            f0 = 0
            for g, n in enumerate(GROUPS):
                name = f"gv{g}"

                def keep(t, done):
                    pair = t.over(2).plus(f0)
                    slot = 2 * (t.start // 2 % 2) + t.start % 2
                    u = t.plus(FIRST_TILE[name])
                    act.wait_ge(chunk_done, done)
                    wait(act, f_conved, pair.at(2, t.start % 2 - 3))
                    nc.scalar.activation(f_in[:, slot:slot + 1, 2:2 + SEQ], tile_out(u, False), ACT.Copy).then_inc(evicted[u.mod(2)], 1)
                    if t.start % 2:
                        act.wait_ge(f_conved, pair.at(2, 1))
                        nc.scalar.activation(f_conv[:, slot - 1], f_conv[:, slot - 1], ACT.Silu).then_inc(f_silu, 1)
                        act.wait_ge(f_prod, pair.at(1, 1))
                        nc.scalar.activation(f_hi[:, one(t.over(2)), META:T], f_conv[:, slot:slot + 1], ACT.Copy).then_inc(f_hi_s, 1)
                side_stage(act, split_hi, name, keep, peel=1 if g == 0 else 0)
                only_split(act, split_hi, f"fd{g}")
                f0 += n

        def ffn_dve(dve):
            f0 = 0
            for g, n in enumerate(GROUPS):
                name = f"gv{g}"

                def conv(t, done):
                    pair = t.over(2).plus(f0)
                    slot = 2 * (t.start // 2 % 2) + t.start % 2
                    u = t.plus(FIRST_TILE[name])
                    half = FFN2 * (t.start % 2)
                    dve.wait_ge(evicted[u.mod(2)], u.over(2).at(plus=1))
                    wait(dve, f_lo_s, pair.at(1, -1))

                    def col(j):
                        return one(pair.plus(PARAM["conv_ffn_w"] + 44 * j + half))
                    convolve(dve, f_conv[:, slot], 3, col, f_in[:, slot], one(pair.plus(PARAM["conv_ffn_b"] + half)), f_conved)
                    if t.start % 2:
                        dve.wait_ge(f_silu, pair.at(1, 1))
                        dve.wait_ge(f_conved, pair.at(2, 2))
                        o = f_conv[:, slot]
                        nc.vector.tensor_tensor(o, o, f_conv[:, slot - 1], ALU.mult).then_inc(f_prod, 1)
                        dve.wait_ge(f_hi_s, pair.at(1, 1))
                        row = one(t.over(2))
                        nc.vector.tensor_tensor(f_lo[:, row, META:T], f_conv[:, slot:slot + 1], f_hi[:, row, META:T], ALU.subtract).then_inc(f_lo_s, 1)
                side_stage(dve, split_lo, name, conv, peel=1 if g == 0 else 0, chains=[(dve_chain, 2)])
                residual_dve(dve, f"fd{g}", False, 1.0)
                f0 += n

        final = Norm("final", TOTAL_TILES, False, PARAM["norm_final"], eps=RMS_EPS, last=True)

        stored = sem("stored")
        block = ctx.enter_context(nc.Block())

        @block.sync
        def _(sp):
            stream_weights(sp)
            sp.wait_ge(norm_scaled, KT * norms["all"])
            sp.dma_start(out, final.y[:, :, META:T]).then_inc(stored, 16)
            sp.wait_ge(stored, 16)

        @block.gpsimd
        def _(pool):
            even_loads(pool)
            ret_loads(pool)
            dsa_loads(pool)
            ssm_loads(pool)
            ffn_pool(pool)

        @block.tensor
        def _(pe):
            pe_stage(pe, "qk", x_hi, x_lo, True, ready=(x_split_lo, 0))
            chunk_products(pe, "forget", Step(0), x_hi, x_lo, True)
            v_pe(pe)
            even_attention_pe(pe)
            pe.wait_ge(diff_lo_s, DIFF_HEADS)
            pe.wait_ge(head_lo, FOX_HEADS // 2)
            pe_stage(pe, "even_out", x_hi, x_lo, True, after=lambda k: ln00.add_mean(pe, k))
            ln00.pe(pe)
            mlp0.pe(pe, ln00, ln01)
            ln01.pe(pe)
            retention_pe(pe)
            ln10.pe(pe)
            mlp1.pe(pe, ln10, ln11)
            ln11.pe(pe)
            rms_mix.pe(pe)
            select_pe(pe)
            sparse_pe(pe)
            att_merge_pe(pe)
            dt_pe(pe)
            first_inputs_pe(pe)
            for g in range(SSM_GROUPS + 1):
                ssm_pe(pe, g)
            mix_pe(pe)
            rms_ffn.pe(pe)
            ffn_pe(pe)
            final.pe(pe)

        @block.scalar
        def _(act):
            even_act_start(act)
            qk_act(act)
            forget_act(act)
            v_act(act)
            even_attention_act(act)
            only_split(act, split_hi, "even_out")
            ln00.act(act)
            mlp0.act(act)
            ln01.act(act)
            retention_act(act)
            ln10.act(act)
            mlp1.act(act)
            ln11.act(act, follow=rms_mix)
            rms_mix.act(act, squared=True)
            select_act(act)
            sparse_act(act)
            only_split(act, split_hi, "att_out")
            dt_act(act)
            first_inputs_act(act)
            for g in range(SSM_GROUPS + 1):
                ssm_act(act, g)
            mix_act(act)
            rms_ffn.act(act)
            ffn_act(act)
            final.act(act)

        @block.vector
        def _(dve):
            even_dve_start(dve)
            only_split(dve, split_lo, "qk")
            forget_dve(dve)
            v_dve(dve)
            even_attention_dve(dve)
            residual_dve(dve, "even_out", True, ALPHA)
            ln00.dve(dve)
            mlp0.dve(dve)
            ln01.dve(dve)
            retention_dve(dve)
            ln10.dve(dve)
            mlp1.dve(dve)
            ln11.dve(dve)
            rms_mix.dve(dve)
            select_dve(dve)
            sparse_dve(dve)
            att_merge_dve(dve)
            dt_dve(dve)
            first_inputs_dve(dve)
            for g in range(SSM_GROUPS + 1):
                ssm_dve(dve, g)
            mix_dve(dve)
            rms_ffn.dve(dve)
            ffn_dve(dve)
            final.dve(dve)


def pack(w):
    even, eo, r, ro = w["even_w_in"][0], w["even_w_out"][0], w["ret_w_in"][0], w["ret_w_out"][0]
    w2, parts = w["w_in_2"][0], []

    def cols(m, c0, n, rows=(0, 1024)):
        for c in range(n):
            for r0 in range(rows[0], rows[1], 1024):
                chunk = np.zeros((P, 8, P), np.float32)
                block = m[r0:min(r0 + 1024, rows[1]), c0 + c * P:min(c0 + (c + 1) * P, m.shape[1])]
                k = block.shape[0] // P
                chunk[:, 0:k, 0:block.shape[1]] = block.reshape(k, P, -1).transpose(1, 0, 2)
                parts.append(chunk)

    cols(even, 0, 8)
    cols(even, 1536, 8)
    cols(even, 3072, 1)
    cols(even, 1024, 4)
    cols(even, 2560, 4)
    cols(eo, 0, 8)

    def mlp(layer):
        for half in range(2):
            cols(w["ffn_w1"][layer], 2048 * half, 16)
            cols(w["ffn_w2"][layer], 0, 8, (2048 * half, 2048 * half + 2048))
    mlp(0)
    for h in range(RET_HEADS):
        cols(r, 256 * h, 2)
        cols(r, 1024 + 256 * h, 2)
        cols(r, 2048 + 512 * h, 4)
        cols(r, 4096 + 512 * h, 4)
        if h >= 2:
            cols(ro, 0, 8, (1024 * (h - 2), 1024 * (h - 2) + 1024))
    mlp(1)
    cols(w2, 0, 8)
    cols(w2, 1024, 1)
    cols(w2, 1152, 4)
    k_idx = w2[:, 1664:1728]
    cols(np.concatenate([k_idx, k_idx], 1), 0, 1)
    cols(w2[:, 1728:1736], 0, 1)
    def ssm(kind, g):
        if kind == "xs":
            cols(w2, 3784 + 512 * g, 4)
            cols(w2, 3784 + 2048 + 128 * g, 1)
            cols(w2, 3784 + 2560 + 128 * g, 1)
        elif kind == "z":
            cols(w2, 1736 + 512 * g, 4)
        else:
            rows = w["w_ssm_out_2"][0][512 * g:512 * g + 512]
            for c in range(4):
                parts.append(rows[:, 256 * c:256 * c + 256].reshape(4, P, 2 * P).transpose(1, 0, 2).reshape(P, 8, P))
    names = [name for name, _ in STAGES]
    for name in names[names.index("gate_att"):names.index("mix_out")]:
        if name[:-1] in ("xs", "z", "so"):
            ssm(name[:-1], int(name[-1]))
        elif name == "gate_att":
            cols(w2, 6888, 8)
        elif name == "att_out":
            cols(w["w_att_out_2"][0], 0, 8)
        elif name == "dt":
            cols(w2[:, 6856:6888], 0, 1)
        else:
            cols(w2, 6888 + 1024 + 512 * (name == "gate_ssm_b"), 4)
    cols(w["w_out_2"][0], 0, 8)
    up, down, f = w["w_ffn_up_2"][0], w["w_ffn_down_2"][0], 0
    for n in (8, 8, 6):
        for t in range(f, f + n):
            cols(up, t * P, 1)
            cols(up, (FFN2 + t) * P, 1)
        cols(down, 0, 8, (f * P, (f + n) * P))
        f += n
    assert len(parts) == TOTAL_CHUNKS
    return np.stack(parts).reshape(TOTAL_CHUNKS, P, 8 * P)


def pack_params(w):
    out = np.zeros((P, PARAMS), np.float32)

    def put(name, a):
        a = np.asarray(a)
        out[:a.shape[-1], PARAM[name]:PARAM[name] + a.shape[0]] = a.T
    put("ln_g", w["ln_g"].reshape(32, P))
    put("ln_b", w["ln_b"].reshape(32, P))
    put("subln_g", w["diff_subln_g"])
    put("f_bias", w["even_f_bias"])
    put("norm_mix", w["norm_mix_2"].reshape(8, P))
    put("norm_ffn", w["norm_ffn_2"].reshape(8, P))
    put("norm_final", w["norm_final_2"].reshape(8, P))
    put("kv_norm", w["kv_norm_2"])
    put("conv_ssm_w", w["conv_ssm_w_2"][0].reshape(96, P))
    put("conv_ssm_b", w["conv_ssm_b_2"].reshape(24, P))
    put("ssm_norm", w["ssm_norm_2"].reshape(16, P))
    put("d_skip", np.repeat(w["d_skip_2"][0], 64).reshape(16, P))
    put("dt_bias", w["dt_bias_2"])
    put("a_log", w["a_log_2"])
    put("conv_ffn_w", w["conv_ffn_w_2"][0].reshape(132, P))
    put("conv_ffn_b", w["conv_ffn_b_2"].reshape(44, P))
    out[:, PARAM["rel_far"]:PARAM["rel_far"] + 16] = w["rel_bias_2"][31][None]
    return out


def shape_tables():
    out = np.zeros((P, TABLES), np.float32)

    def put(name, a):
        out[:a.shape[0], TABLE[name]:TABLE[name] + a.shape[1]] = a
    r, m = np.arange(P)[:, None], np.arange(P)[None]
    put("ident", np.eye(P))
    put("tri", (m >= r).astype(np.float32))
    put("causal", np.where(m <= r, 0, NEG))
    q, k = META + 384 + np.arange(P)[:, None], np.arange(T)[None]
    seen = (k + 48) // 64 <= (q + 48) // 64
    slopes = 2.0 ** (-8.0 * np.arange(1, 5) / 4)
    put("alibi", np.concatenate([np.where(seen, -s * np.abs(q - k), NEG) for s in slopes], 1))
    gamma = 1 - 2.0 ** (-5.0 - np.arange(RET_HEADS))
    m = np.arange(SEQ)[None]
    put("decay", np.concatenate([np.where(r // 64 <= m // 64, g ** np.abs(m - r), 0) for g in gamma], 1))
    s = np.arange(META)[:, None]
    put("decay_meta", np.concatenate([g ** (META + m - s) for g in gamma], 1))
    dist = 511 - np.arange(640)
    n = np.maximum(dist, 0)
    large = 16 + (np.log(np.maximum(n, 1).astype(np.float32) / 16) / np.float32(math.log(8)) * 16).astype(np.int32)
    bucket = np.where(n < 16, n, np.minimum(large, 31))
    put("bucket", (np.arange(32)[:, None] == bucket[None]).astype(np.float32))
    return out


def kernel(**inputs):
    import concourse.bacc as _bacc
    from concourse.bass_utils import run_bass_kernel_spmd as _run

    w = {k: np.asarray(v) for k, v in inputs.items()}
    tokens = np.concatenate([w["meta_tokens"], w["x"][0]], 0)
    arrays = {
        "x_by_feature": np.ascontiguousarray(tokens.T.reshape(KT, P, T).transpose(1, 0, 2)),
        "weights": pack(w),
        "params": pack_params(w),
        "tables": shape_tables(),
        "lam": np.ascontiguousarray(np.broadcast_to(w["diff_lambda"].reshape(1, 256), (P, 256))),
        "w_uk": np.ascontiguousarray(w["w_uk_2"][0].reshape(8, P, P).transpose(1, 0, 2)),
        "w_uv": np.ascontiguousarray(w["w_uv_2"][0].transpose(2, 0, 1).reshape(P, 1024)),
        "rel": np.ascontiguousarray(w["rel_bias_2"]),
    }
    nc = _bacc.Bacc("TRN2", target_bir_lowering=False, num_devices=1)
    args = [nc.dram_tensor(f"in_{k}", a.shape, F32, kind="ExternalInput").ap() for k, a in arrays.items()]
    line = nc.dram_tensor("bias_line", (ATT_HEADS, 640), F32, kind="Internal").ap()
    skewed = nc.dram_tensor("bias_skewed", (ATT_HEADS, SKEW), F32, kind="Internal").ap()
    acum = nc.dram_tensor("acum_rows", (32, SEQ), F32, kind="Internal").ap()
    out = nc.dram_tensor("out", (P, KT, SEQ), F32, kind="ExternalOutput").ap()
    merged = nc.dram_tensor("merged_kept", (P, KT * SEQ), F32, kind="Internal").ap()
    cum = nc.dram_tensor("cum_rows", (FOX_HEADS, T), F32, kind="Internal").ap()
    kept = nc.dram_tensor("streamed_kept", (len(KEPT), P, SEQ), F32, kind="Internal").ap()
    gate = nc.dram_tensor("gate_kept", (P, KT * SEQ), F32, kind="Internal").ap()
    program(nc, *args, line, skewed, cum, acum, merged, kept, gate, out)
    r = _run(nc, [{f"in_{k}": a for k, a in arrays.items()}], core_ids=[0])
    return np.ascontiguousarray(r.results[0]["out"].transpose(2, 1, 0).reshape(1, SEQ, D))
```
